# Optimizing a Trainium2 kernel written in Bass

```python
import jax, jax.numpy as jnp
from jax import lax
import numpy as np

D_MODEL = 1024
BATCH = 1
SEQ = 2048
DEPTH = 1

POOL_WIDTH = D_MODEL // 2
POOL_WINDOWS = (2, 4, 8, 16)
N_POOL_GROUPS = len(POOL_WINDOWS)
POOL_GROUP = POOL_WIDTH // N_POOL_GROUPS
N_HEADS = 8
HEAD_DIM = 64
ATTN_WIDTH = N_HEADS * HEAD_DIM
Q_BLOCK = 128
IN_WIDTH = 2 * POOL_WIDTH + 4 * ATTN_WIDTH + 2 * D_MODEL
RMS_EPS = 1e-6

kernel_name = "hybrid_pool_stickbreak_gated"

def rms_norm(x, g):
    xf = x.astype(jnp.float32)
    y = xf * lax.rsqrt(jnp.mean(xf * xf, axis=-1, keepdims=True) + RMS_EPS)
    return (y * g.astype(jnp.float32)).astype(x.dtype)

def multiscale_pool(u, w_group, scale):
    B, S, _ = u.shape
    grp = u.astype(jnp.float32).reshape(B, S, N_POOL_GROUPS, POOL_GROUP)
    cs = jnp.cumsum(grp, axis=1)
    pos = jnp.arange(S)
    means = []
    for g, w in enumerate(POOL_WINDOWS):
        c = cs[:, :, g]
        prev = jnp.pad(c, ((0, 0), (w, 0), (0, 0)))[:, :S]
        cnt = jnp.minimum(pos + 1, w).astype(jnp.float32)[None, :, None]
        means.append((c - prev) / cnt)
    pooled = jnp.stack(means, axis=2) - grp
    mixed = jnp.einsum('bsgc,gcd->bsgd', pooled, w_group.astype(jnp.float32))
    return (mixed.reshape(B, S, POOL_WIDTH) * scale.astype(jnp.float32)).astype(u.dtype)

def stick_breaking_attention(q, k, v):
    B, S, H, Dh = q.shape
    n_blocks = S // Q_BLOCK
    qb = q.reshape(B, n_blocks, Q_BLOCK, H, Dh).transpose(1, 0, 2, 3, 4)
    kf = k.astype(jnp.float32)
    vf = v.astype(jnp.float32)
    key_pos = jnp.arange(S)
    inv_sqrt_d = 1.0 / float(np.sqrt(Dh))

    def one_block(args):
        q_blk, blk = args
        logits = jnp.einsum('bqhd,bkhd->bhqk', q_blk.astype(jnp.float32), kf) * inv_sqrt_d
        q_pos = blk * Q_BLOCK + jnp.arange(Q_BLOCK)
        mask = (key_pos[None, :] < q_pos[:, None])[None, None]
        log_beta = jax.nn.log_sigmoid(logits)
        log_1m_beta = jnp.where(mask, jax.nn.log_sigmoid(-logits), 0.0)
        later = lax.cumsum(log_1m_beta, axis=3, reverse=True) - log_1m_beta
        wts = jnp.where(mask, jnp.exp(log_beta + later), 0.0)
        return jnp.einsum('bhqk,bkhd->bqhd', wts, vf)

    out = lax.map(one_block, (qb, jnp.arange(n_blocks)))
    return out.transpose(1, 0, 2, 3, 4).reshape(B, S, H, Dh).astype(q.dtype)

def setup_inputs(seed: int = 0) -> dict:
    key = jax.random.key(seed)
    ks = jax.random.split(key, 11)
    f32 = jnp.float32
    x = jax.random.normal(ks[0], (BATCH, SEQ, D_MODEL), f32)
    norm_g = 1.0 + 0.05 * jax.random.normal(ks[1], (DEPTH, D_MODEL), f32)
    w_in = jax.random.normal(ks[2], (DEPTH, D_MODEL, IN_WIDTH), f32) * D_MODEL ** -0.5
    b_gate = 0.01 * jax.random.normal(ks[3], (DEPTH, 2 * D_MODEL), f32)
    pool_w = jax.random.normal(ks[4], (DEPTH, N_POOL_GROUPS, POOL_GROUP, POOL_GROUP), f32) * POOL_GROUP ** -0.5
    pool_scale = 1.0 + 0.1 * jax.random.normal(ks[5], (DEPTH, POOL_WIDTH), f32)
    w_pool_up = jax.random.normal(ks[6], (DEPTH, POOL_WIDTH, D_MODEL), f32) * POOL_WIDTH ** -0.5
    w_attn_up = jax.random.normal(ks[7], (DEPTH, ATTN_WIDTH, D_MODEL), f32) * ATTN_WIDTH ** -0.5
    w_out = jax.random.normal(ks[8], (DEPTH, D_MODEL, D_MODEL), f32) * D_MODEL ** -0.5
    final_g = 1.0 + 0.05 * jax.random.normal(ks[9], (D_MODEL,), f32)
    return {"x": x, "norm_g": norm_g, "w_in": w_in, "b_gate": b_gate, "pool_w": pool_w,
            "pool_scale": pool_scale, "w_pool_up": w_pool_up, "w_attn_up": w_attn_up,
            "w_out": w_out, "final_g": final_g}

def reference(x, norm_g, w_in, b_gate, pool_w, pool_scale, w_pool_up, w_attn_up, w_out, final_g):
    B, S, D = x.shape
    splits = np.cumsum([POOL_WIDTH, POOL_WIDTH, ATTN_WIDTH, ATTN_WIDTH, ATTN_WIDTH, ATTN_WIDTH]).tolist()
    for l in range(DEPTH):
        h = rms_norm(x, norm_g[l])
        proj = jnp.einsum('bsd,de->bse', h, w_in[l])
        u_pool, z_pool, q, k, v, z_attn, gate_logits = jnp.split(proj, splits, axis=-1)
        y_pool = multiscale_pool(u_pool, pool_w[l], pool_scale[l]) * jax.nn.silu(z_pool)
        attn = stick_breaking_attention(q.reshape(B, S, N_HEADS, HEAD_DIM),
                                        k.reshape(B, S, N_HEADS, HEAD_DIM),
                                        v.reshape(B, S, N_HEADS, HEAD_DIM))
        y_attn = attn.reshape(B, S, ATTN_WIDTH) * jax.nn.silu(z_attn)
        gates = jax.nn.sigmoid(gate_logits + b_gate[l]).reshape(B, S, 2, D)
        merged = (gates[:, :, 0] * jnp.einsum('bsp,pd->bsd', y_pool, w_pool_up[l])
                  + gates[:, :, 1] * jnp.einsum('bsa,ad->bsd', y_attn, w_attn_up[l]))
        x = x + jnp.einsum('bsd,de->bse', merged, w_out[l])
    return rms_norm(x, final_g)


_drawn_inputs = setup_inputs


def setup_inputs(seed=0):
    import zlib

    import numpy as np

    out = dict(_drawn_inputs(seed))
    spreads = {}
    factors = {'b_gate': 45.241}
    for name, (base, spread) in spreads.items():
        noise = np.random.default_rng([zlib.crc32(name.encode()), seed]).standard_normal(out[name].shape)
        drawn = base * np.exp(spread * noise) if base else spread * noise
        out[name] = __import__('jax').numpy.asarray(drawn.astype(out[name].dtype))
    for name, factor in factors.items():
        out[name] = (out[name] * factor).astype(out[name].dtype)
    return out
```

```python
from contextlib import ExitStack

import concourse.bass as bass
from concourse import mybir

F32 = mybir.dt.float32
F32R = mybir.dt.float32r
ALU = mybir.AluOpType
ACT = mybir.ActivationFunctionType

P = 128
SEQ = 2048
D = 1024
KT = D // P
TT = SEQ // P
CH = 512
NC = SEQ // CH
HD = 64
HEADS = 8
PAIRS = HEADS // 2
AW = HEADS * HD
WINDOWS = (2, 4, 8, 16)
PAD = max(WINDOWS)
EPS = 1e-6
SCALE = HD ** -0.5
MASK = -1.0e30
DMA = 16
S_U, S_ZP, S_Q, S_K, S_ZA, S_G = 0, 4, 8, 12, 20, 24


class Arena:

    def __init__(self, nc, at, end):
        self.nc, self.at, self.end = nc, at, end

    def __call__(self, name, shape, dtype=F32):
        t = self.nc.alloc_sbuf_tensor_at(name, shape, dtype, offset=self.at)
        size = 4
        for n in shape[1:]:
            size *= n
        self.at += -(-size // 32) * 32
        assert self.at <= self.end, (name, self.at, self.end)
        return t


def split3(pe, out, w_hi, w_lo, m_hi, m_lo, start, stop):
    pe.matmul(out, w_hi, m_hi, start=start, stop=False)
    pe.matmul(out, w_hi, m_lo, start=False, stop=False)
    return pe.matmul(out, w_lo, m_hi, start=False, stop=stop)


def build(nc, x, norm_gT, w_strips, w_v, b_gateT, pool_w, pool_scaleT, w_pool_up, w_attn_up, w_out,
          final_g, pool_fix, out):
    def scratch(name, shape):
        return nc.dram_tensor(name, shape, F32, kind="Internal").ap()

    qk_d = scratch("qk_scratch", [2 * PAIRS, P, SEQ])
    v_d = scratch("v_scratch", [SEQ, AW])
    mix_d = scratch("mix_scratch", [PAIRS, P, SEQ])
    yp_d = scratch("y_pool_scratch", [PAIRS, P, SEQ])
    za_d = scratch("z_attn_scratch", [PAIRS, P, SEQ])
    at_d = scratch("attn_scratch", [PAIRS, P, SEQ])
    gate_d = scratch("gate_scratch", [4 * PAIRS, P, SEQ])

    with ExitStack() as ctx:
        def sem(name):
            return ctx.enter_context(nc.semaphore(name))

        psum = ctx.enter_context(nc.psum_tensor("psum", [P, 8, 512], F32))
        base = -(-nc.sbuf_base // 32) * 32
        end = nc.sbuf_usable_end
        fixed = Arena(nc, base, end)
        ident = fixed("ident", [P, P])
        ident_r = fixed("ident_r", [P, P], F32R)
        mask_f = fixed("mask_f", [P, P])
        mask_r = fixed("mask_r", [P, P], F32R)
        gcol = fixed("gcol", [P, KT])
        bcol = fixed("bcol", [P, 2 * KT])
        pscol = fixed("pscol", [P, PAIRS])
        hT_at = fixed.at
        hT_hi = fixed("hT_hi", [P, KT, SEQ], F32R)
        hT_lo = fixed("hT_lo", [P, KT, SEQ], F32R)
        w_raw = fixed("w_raw", [P, KT, P])
        w_hi = fixed("w_hi", [P, 2, KT, P], F32R)
        w_lo = fixed("w_lo", [P, 2, KT, P], F32R)
        free_at = fixed.at

        stage1(nc, sem, psum, Arena(nc, free_at, end), ident, ident_r, mask_f, mask_r, gcol, bcol, pscol,
               hT_hi, hT_lo, w_raw, x, norm_gT, w_v, b_gateT, pool_scaleT, v_d)
        stage2(nc, sem, psum, Arena(nc, free_at, end), pscol, hT_hi, hT_lo, w_raw, w_hi, w_lo,
               w_strips, pool_w, pool_fix, qk_d, mix_d)
        stage3(nc, sem, psum, Arena(nc, free_at, end), ident, ident_r, mask_r, bcol, hT_hi, hT_lo,
               w_raw, w_hi, w_lo, w_strips, qk_d, v_d, mix_d, yp_d, za_d, at_d, gate_d)
        stage4(nc, sem, psum, Arena(nc, hT_at, end), x, yp_d, za_d, at_d, gate_d, w_pool_up,
               w_attn_up, w_out, final_g, out)


def stage1(nc, sem, psum, sb, ident, ident_r, mask_f, mask_r, gcol, bcol, pscol, hT_hi, hT_lo, w_raw,
           x, norm_gT, w_v, b_gateT, pool_scaleT, v_d):
    wv_hi = sb("wv_hi", [P, KT, AW], F32R)
    wv_lo = sb("wv_lo", [P, KT, AW], F32R)
    xt = sb("xt", [P, 2, D])
    xn = sb("xn", [P, 2, D])
    scaled = sb("scaled", [P, 2, CH])
    v_out = sb("v_out", [P, 2, AW])
    stat = sb("stat", [P, TT, 8])
    wv_piece = w_raw[:, :, :].rearrange("p (a b) n -> p a (b n)", a=2)
    WV = KT // 2

    const_in, ident_done = sem("s1_const_in"), sem("s1_ident_done")
    mask_done, consts_r = sem("s1_mask_done"), sem("s1_consts_r")
    x_in = [sem(f"s1_x_in{i}") for i in range(2)]
    wv_in, wv_hi_done, wv_lo_done = sem("s1_wv_in"), sem("s1_wv_hi"), sem("s1_wv_lo")
    squared, rooted, normed = sem("s1_squared"), sem("s1_rooted"), sem("s1_normed")
    mean_done = sem("s1_mean")
    transposed, scaled_done = sem("s1_transposed"), sem("s1_scaled")
    hi_done, lo_done = sem("s1_hi"), sem("s1_lo")
    v_done, v_copied = sem("s1_v_done"), sem("s1_v_copied")
    v_stored = [sem(f"s1_v_stored{i}") for i in range(2)]

    with nc.Block() as block:
        @block.sync
        def _(sp):
            def load_x(t):
                if t >= 2:
                    sp.wait_ge(normed, t - 1)
                sp.dma_start(xt[:, t % 2, :], x[t * P:(t + 1) * P, :]).then_inc(x_in[t % 2], DMA)

            load_x(0)
            sp.dma_start(gcol[:, :], norm_gT).then_inc(const_in, DMA)
            sp.dma_start(bcol[:, :], b_gateT).then_inc(const_in, DMA)
            sp.dma_start(pscol[:, :], pool_scaleT).then_inc(const_in, DMA)
            for i in range(WV):
                if i >= 1:
                    sp.wait_ge(wv_lo_done, i)
                sp.dma_start(wv_piece, w_v[:, 2 * i:2 * i + 2, :]).then_inc(wv_in, DMA)
                load_x(i + 1)
            for t in range(WV + 1, TT):
                load_x(t)
                if t >= 5:
                    i = t - 5
                    sp.wait_ge(v_copied, i + 1)
                    sp.dma_start(v_d[i * P:(i + 1) * P, :], v_out[:, i % 2, :]).then_inc(v_stored[i % 2], DMA)
            for i in range(TT - 5, TT):
                sp.wait_ge(v_copied, i + 1)
                sp.dma_start(v_d[i * P:(i + 1) * P, :], v_out[:, i % 2, :]).then_inc(v_stored[i % 2], DMA)
            for s in v_stored:
                sp.wait_ge(s, DMA * TT // 2)
            sp.wait_ge(const_in, 3 * DMA)

        @block.gpsimd
        def _(pool):
            pool.memset(ident[:, :], 0.0).then_inc(ident_done, 1)
            pool.memset(mask_f[:, :], 0.0).then_inc(mask_done, 1)
            pool.wait_ge(ident_done, 1)
            pool.affine_select(out=ident[:, :], in_=ident[:, :], compare_op=ALU.not_equal, fill=1.0,
                               base=0, pattern=[[-1, P]], channel_multiplier=1).then_inc(ident_done, 1)
            pool.wait_ge(mask_done, 1)
            pool.affine_select(out=mask_f[:, :], in_=mask_f[:, :], compare_op=ALU.is_gt, fill=MASK,
                               base=0, pattern=[[-1, P]], channel_multiplier=1).then_inc(mask_done, 1)
            for t in range(TT):
                for hb in range(2):
                    n = 2 * t + hb
                    pool.wait_ge(hi_done, n + 1)
                    k = slice(4 * hb, 4 * hb + 4)
                    pool.tensor_tensor(hT_lo[:, k, t * P:(t + 1) * P],
                                       scaled[:, hb, :].rearrange("p (k n) -> p k n", k=4),
                                       hT_hi[:, k, t * P:(t + 1) * P].bitcast(F32),
                                       ALU.subtract).then_inc(lo_done, 1)

        @block.scalar
        def _(act):
            def part_hi(t):
                for hb in range(2):
                    n = 2 * t + hb
                    act.wait_ge(scaled_done, n + 1)
                    act.activation(hT_hi[:, 4 * hb:4 * hb + 4, t * P:(t + 1) * P],
                                   scaled[:, hb, :].rearrange("p (k n) -> p k n", k=4),
                                   ACT.Copy).then_inc(hi_done, 1)

            for t in range(TT):
                act.wait_ge(x_in[t % 2], DMA * (t // 2 + 1))
                if t >= 2:
                    act.wait_ge(transposed, 2 * (t - 1))
                act.activation(xn[:, t % 2, :], xt[:, t % 2, :], ACT.Square,
                               accum_out=stat[:, t, 0:1]).then_inc(squared, 1)
                if t >= 1:
                    part_hi(t - 1)
                act.wait_ge(mean_done, 2 * t + 2)
                act.activation(stat[:, t, 3:4], stat[:, t, 2:3], ACT.Sqrt).then_inc(rooted, 1)
                if t < WV:
                    act.wait_ge(wv_in, DMA * (t + 1))
                    act.activation(wv_hi[:, 2 * t:2 * t + 2, :], wv_piece, ACT.Copy).then_inc(wv_hi_done, 1)
            part_hi(TT - 1)

        @block.vector
        def _(dve):
            dve.wait_ge(ident_done, 2)
            dve.tensor_copy(ident_r[:, :], ident[:, :]).then_inc(consts_r, 1)
            dve.wait_ge(mask_done, 2)
            dve.tensor_copy(mask_r[:, :], mask_f[:, :]).then_inc(consts_r, 1)
            newton = sem("s1_newton")

            def copy_v(i):
                dve.wait_ge(v_done, i + 1)
                if i >= 2:
                    dve.wait_ge(v_stored[i % 2], DMA * (i // 2))
                dve.tensor_copy(v_out[:, i % 2, :], psum[:, 4 + i % 2, :]).then_inc(v_copied, 1)

            def scale_rows(t):
                for hb in range(2):
                    n = 2 * t + hb
                    dve.wait_ge(transposed, n + 1)
                    if t >= 1:
                        dve.wait_ge(lo_done, n - 1)
                    k = slice(4 * hb, 4 * hb + 4)
                    dve.tensor_tensor(scaled[:, hb, :].rearrange("p (k n) -> p k n", k=4),
                                      psum[:, 2 * (t % 2) + hb, :].rearrange("p (k n) -> p k n", k=4),
                                      gcol[:, k].unsqueeze(2).broadcast_to([P, 4, P]),
                                      ALU.mult).then_inc(scaled_done, 1)

            dve.wait_ge(const_in, 3 * DMA)
            for t in range(TT):
                dve.wait_ge(squared, t + 1)
                dve.tensor_scalar(stat[:, t, 1:2], stat[:, t, 0:1], 1.0 / D, EPS, ALU.mult,
                                  ALU.add).then_inc(mean_done, 1)
                dve.wait_ge(mean_done, 2 * t + 1)
                dve.reciprocal(stat[:, t, 2:3], stat[:, t, 1:2]).then_inc(mean_done, 1)
                if t >= 1:
                    scale_rows(t - 1)
                if t < WV:
                    dve.wait_ge(wv_hi_done, t + 1)
                    dve.tensor_tensor(wv_lo[:, 2 * t:2 * t + 2, :], wv_piece,
                                      wv_hi[:, 2 * t:2 * t + 2, :].bitcast(F32),
                                      ALU.subtract).then_inc(wv_lo_done, 1)
                dve.wait_ge(rooted, t + 1)
                dve.tensor_scalar(stat[:, t, 4:5], stat[:, t, 3:4], stat[:, t, 3:4], stat[:, t, 1:2],
                                  ALU.mult, ALU.mult).then_inc(newton, 1)
                dve.wait_ge(newton, 2 * t + 1)
                dve.tensor_scalar(stat[:, t, 5:6], stat[:, t, 4:5], -0.5, 1.5, ALU.mult,
                                  ALU.add).then_inc(newton, 1)
                dve.wait_ge(newton, 2 * t + 2)
                dve.tensor_scalar(xn[:, t % 2, :], xt[:, t % 2, :], stat[:, t, 3:4], stat[:, t, 5:6],
                                  ALU.mult, ALU.mult).then_inc(normed, 1)
                if t >= 4:
                    copy_v(t - 4)
            scale_rows(TT - 1)
            for i in range(TT - 4, TT):
                copy_v(i)

        @block.tensor
        def _(pe):
            def transpose_tile(t):
                pe.wait_ge(normed, t + 1)
                for hb in range(2):
                    if t >= 2:
                        pe.wait_ge(scaled_done, 2 * (t - 2) + hb + 1)
                    for k in range(4):
                        last = pe.transpose(psum[:, 2 * (t % 2) + hb, k * P:(k + 1) * P],
                                            xn[:, t % 2, (4 * hb + k) * P:(4 * hb + k + 1) * P], ident[:, :])
                    last.then_inc(transposed, 1)

            def project_v(t):
                pe.wait_ge(lo_done, 2 * t + 2)
                if t == 0:
                    pe.wait_ge(wv_lo_done, WV)
                if t >= 2:
                    pe.wait_ge(v_copied, t - 1)
                tok = slice(t * P, (t + 1) * P)
                for k in range(KT):
                    last = split3(pe, psum[:, 4 + t % 2, :], hT_hi[:, k, tok], hT_lo[:, k, tok],
                                  wv_hi[:, k, :], wv_lo[:, k, :], k == 0, k == KT - 1)
                last.then_inc(v_done, 1)

            pe.wait_ge(ident_done, 2)
            pe.wait_ge(consts_r, 2)
            for t in range(2):
                transpose_tile(t)
            for t in range(TT):
                if t + 2 < TT:
                    transpose_tile(t + 2)
                project_v(t)


def stage2(nc, sem, psum, sb, pscol, hT_hi, hT_lo, w_raw, w_hi, w_lo, w_strips, pool_w, pool_fix,
           qk_d, mix_d):
    G = len(WINDOWS)
    W = PAD + SEQ
    u = sb("u", [P, W])
    sums = [sb(f"sums{i}", [P, W]) for i in range(2)]
    pooled = sb("pooled", [P, SEQ])
    pl_hi = sb("pl_hi", [P, SEQ], F32R)
    pl_lo = sb("pl_lo", [P, SEQ], F32R)
    pw = sb("pw", [P, G, P])
    pw_hi = sb("pw_hi", [P, G, P], F32R)
    pw_lo = sb("pw_lo", [P, G, P], F32R)
    fix = sb("fix", [P, G, PAD])
    store = sb("store", [P, 2, CH])
    order = [3, 2, 1, 0]
    UM, QM = G, 2 * PAIRS

    raw_in, hi_done, lo_done = sem("s2_w_in"), sem("s2_w_hi"), sem("s2_w_lo")
    proj_done, copied = sem("s2_proj_done"), sem("s2_copied")
    mixed = sem("s2_mixed")
    staged = sem("s2_staged")
    stored = [sem(f"s2_stored{i}") for i in range(2)]
    pw_in, pw_hi_done, pw_lo_done = sem("s2_pw_in"), sem("s2_pw_hi"), sem("s2_pw_lo")
    zeroed, level, pool_hi, pool_lo = sem("s2_zeroed"), sem("s2_level"), sem("s2_pool_hi"), sem("s2_pool_lo")
    levels = {g: WINDOWS[g].bit_length() - 1 for g in range(G)}
    first_level = {}
    at = 0
    for g in order:
        first_level[g] = at
        at += levels[g] + 2

    def use_of_mix(m, c):
        return 4 * m + c if m < G - 1 else 4 * (G - 1) + 4 + c

    def use_of_strip(j, c):
        return 4 * (G - 1) + c if isinstance(j, int) and j == 0 else j * 4 + 4 * G + c

    with nc.Block() as block:
        @block.sync
        def _(sp):
            def load(strip, n):
                sp.wait_ge(lo_done, n) if not isinstance(n, int) or n > 0 else None
                sp.dma_start(w_raw[:, :, :], w_strips[strip]).then_inc(raw_in, DMA)

            def put(dst, use, slot):
                sp.wait_ge(staged, use + 1)
                sp.dma_start(dst, store[:, slot, :]).then_inc(stored[slot], DMA)

            load(S_U + order[0], 0)
            sp.dma_start(pw[:, :, :], pool_w.rearrange("g c d -> c g d")).then_inc(pw_in, DMA)
            sp.dma_start(fix[:, :, :], pool_fix).then_inc(pw_in, DMA)
            for j in range(1, UM):
                load(S_U + order[j], j)
                if j >= 2:
                    for c in range(NC):
                        put(mix_d[order[j - 2], :, c * CH:(c + 1) * CH], use_of_mix(j - 2, c), c % 2)
            load(S_Q, UM)
            load(S_Q + 1, UM + 1)
            for c in range(NC):
                put(mix_d[order[2], :, c * CH:(c + 1) * CH], use_of_mix(2, c), c % 2)
            load(S_Q + 2, UM + 2)
            for c in range(NC):
                put(qk_d[0, :, c * CH:(c + 1) * CH], use_of_strip(0, c), c % 2)
            for c in range(NC):
                put(mix_d[order[3], :, c * CH:(c + 1) * CH], use_of_mix(3, c), c % 2)
            load(S_Q + 3, UM + 3)
            for c in range(NC):
                put(qk_d[1, :, c * CH:(c + 1) * CH], use_of_strip(1, c), c % 2)
            with sp.Fori(1, QM // 2 - 1) as p:
                for r in range(2):
                    load(p * 2 + (S_Q + 2 + r), p * 2 + (UM + 2 + r))
                    for c in range(NC):
                        put(qk_d[p * 2 + r, :, c * CH:(c + 1) * CH], use_of_strip(p * 2 + r, c), c % 2)
            for j in (QM - 2, QM - 1):
                for c in range(NC):
                    put(qk_d[j, :, c * CH:(c + 1) * CH], use_of_strip(j, c), c % 2)
            for s in stored:
                sp.wait_ge(s, DMA * (4 * (UM + QM)) // 2)

        def scalar_weights(act, n, slot):
            act.wait_ge(raw_in, n * DMA + DMA)
            if not isinstance(n, int) or n >= 2:
                act.wait_ge(proj_done, n * 4 - 4)
            act.activation(w_hi[:, slot, :, :], w_raw[:, :, :], ACT.Copy).then_inc(hi_done, 1)

        @block.scalar
        def _(act):
            def take_staging(use, slot):
                if not isinstance(use, int) or use >= 2:
                    act.wait_ge(stored[slot], (use - slot) * (DMA // 2))

            def copy_u(j):
                for c in range(NC):
                    act.wait_ge(proj_done, 4 * j + c + 1)
                    if j >= 1 and c == 0:
                        act.wait_ge(level, first_level[order[j - 1]] + levels[order[j - 1]] + 2)
                    act.activation(u[:, PAD + c * CH:PAD + (c + 1) * CH], psum[:, c % 2, :],
                                   ACT.Copy).then_inc(copied, 1)

            def split_pooled(j):
                act.wait_ge(level, first_level[order[j]] + levels[order[j]] + 2)
                if j >= 1:
                    act.wait_ge(mixed, 4 * j)
                act.activation(pl_hi[:, :], pooled[:, :], ACT.Copy).then_inc(pool_hi, 1)

            def scale_mix(j):
                for c in range(NC):
                    use = use_of_mix(j, c)
                    act.wait_ge(mixed, 4 * j + c + 1)
                    take_staging(use, c % 2)
                    act.activation(store[:, c % 2, :], psum[:, 2 + c % 2, :], ACT.Copy,
                                   scale=pscol[:, order[j]:order[j] + 1]).then_inc(staged, 1)

            def copy_strip(j, c):
                act.wait_ge(proj_done, j * 4 + (4 * UM + c + 1))
                take_staging(use_of_strip(j, c), c % 2)
                act.activation(store[:, c % 2, :], psum[:, c % 2, :], ACT.Copy).then_inc(staged, 1)

            scalar_weights(act, 0, 0)
            act.wait_ge(pw_in, 2 * DMA)
            act.activation(pw_hi[:, :, :], pw[:, :, :], ACT.Copy).then_inc(pw_hi_done, 1)
            scalar_weights(act, 1, 1)
            for j in range(UM):
                copy_u(j)
                if j >= 1:
                    scale_mix(j - 1)
                scalar_weights(act, j + 2, j % 2)
                split_pooled(j)
            for c in range(NC):
                copy_strip(0, c)
            scale_mix(UM - 1)
            scalar_weights(act, UM + 2, 0)
            for c in range(NC):
                copy_strip(1, c)
            scalar_weights(act, UM + 3, 1)
            with act.Fori(1, QM // 2 - 1) as p:
                for r in range(2):
                    for c in range(NC):
                        copy_strip(p * 2 + r, c)
                    scalar_weights(act, p * 2 + (UM + 2 + r), r)
            for j in (QM - 2, QM - 1):
                for c in range(NC):
                    copy_strip(j, c)

        @block.gpsimd
        def _(pool):
            def weights_lo(n, slot):
                pool.wait_ge(hi_done, n + 1)
                pool.tensor_tensor(w_lo[:, slot, :, :], w_raw[:, :, :], w_hi[:, slot, :, :].bitcast(F32),
                                   ALU.subtract).then_inc(lo_done, 1)

            for t in (u, *sums):
                pool.memset(t[:, 0:PAD], 0.0).then_inc(zeroed, 1)
            weights_lo(0, 0)
            pool.wait_ge(pw_hi_done, 1)
            pool.tensor_tensor(pw_lo[:, :, :], pw[:, :, :], pw_hi[:, :, :].bitcast(F32),
                               ALU.subtract).then_inc(pw_lo_done, 1)
            weights_lo(1, 1)
            for n in range(2, 4):
                weights_lo(n, n % 2)
            with pool.Fori(2, (UM + QM) // 2) as p:
                for r in range(2):
                    weights_lo(p * 2 + r, r)

        @block.vector
        def _(dve):
            dve.wait_ge(zeroed, 3)
            dve.wait_ge(pw_in, 2 * DMA)
            for j in range(UM):
                g = order[j]
                n = first_level[g]
                dve.wait_ge(copied, 4 * (j + 1))
                src = u
                for i in range(levels[g]):
                    if i >= 1:
                        dve.wait_ge(level, n)
                    dst = sums[i % 2]
                    dve.tensor_tensor(dst[:, PAD:W], src[:, PAD:W], src[:, PAD - (1 << i):W - (1 << i)],
                                      ALU.add).then_inc(level, 1)
                    n += 1
                    src = dst
                dve.wait_ge(level, n)
                dve.tensor_tensor(src[:, PAD:2 * PAD], src[:, PAD:2 * PAD], fix[:, g, :],
                                  ALU.mult).then_inc(level, 1)
                dve.wait_ge(level, n + 1)
                if j >= 1:
                    dve.wait_ge(pool_lo, j)
                dve.scalar_tensor_tensor(pooled[:, :], src[:, PAD:W], 1.0 / WINDOWS[g], u[:, PAD:W],
                                         ALU.mult, ALU.subtract).then_inc(level, 1)
                dve.wait_ge(pool_hi, j + 1)
                dve.tensor_tensor(pl_lo[:, :], pooled[:, :], pl_hi[:, :].bitcast(F32),
                                  ALU.subtract).then_inc(pool_lo, 1)

        @block.tensor
        def _(pe):
            def strip(n, slot, free):
                pe.wait_ge(lo_done, n + 1)
                for c in range(NC):
                    free(c)
                    tok = slice(c * CH, (c + 1) * CH)
                    for k in range(KT):
                        last = split3(pe, psum[:, c % 2, :], w_hi[:, slot, k, :], w_lo[:, slot, k, :],
                                      hT_hi[:, k, tok], hT_lo[:, k, tok], k == 0, k == KT - 1)
                    last.then_inc(proj_done, 1)

            def mix(j):
                pe.wait_ge(pool_lo, j + 1)
                for c in range(NC):
                    tok = slice(c * CH, (c + 1) * CH)
                    use = use_of_mix(j, c)
                    if 4 * j + c >= 2:
                        back = use - 2 if c >= 2 else use_of_mix(j - 1, c + 2)
                        pe.wait_ge(staged, back + 1)
                    g = order[j]
                    last = split3(pe, psum[:, 2 + c % 2, :], pw_hi[:, g, :], pw_lo[:, g, :],
                                  pl_hi[:, tok], pl_lo[:, tok], True, True)
                    last.then_inc(mixed, 1)

            def free_u(j):
                def wait(c):
                    if 4 * j + c >= 2:
                        pe.wait_ge(copied, 4 * j + c - 1)
                return wait

            def free_strip(j):
                def wait(c):
                    if isinstance(j, int) and j == 0 and c < 2:
                        pe.wait_ge(copied, 4 * UM - 1 + c)
                    elif isinstance(j, int) and j == 1 and c < 2:
                        pe.wait_ge(staged, use_of_strip(0, c + 2) + 1)
                    elif c < 2:
                        pe.wait_ge(staged, j * 4 + (4 * G + c - 1))
                    else:
                        pe.wait_ge(staged, use_of_strip(j, c - 2) + 1)
                return wait

            pe.wait_ge(pw_lo_done, 1)
            for j in range(UM):
                strip(j, j % 2, free_u(j))
                if j >= 1:
                    mix(j - 1)
            strip(UM, 0, free_strip(0))
            mix(UM - 1)
            strip(UM + 1, 1, free_strip(1))
            with pe.Fori(1, QM // 2) as p:
                for r in range(2):
                    strip(p * 2 + (UM + r), r, free_strip(p * 2 + r))


def attention_items():
    return [(e, i, c, (i % 4 + 1) * P if c == i // 4 else CH, c == i // 4, c == 0)
            for e in range(2) for i in reversed(range(TT)) for c in reversed(range(i // 4 + 1))]


def stage3(nc, sem, psum, sb, ident, ident_r, mask_r, bcol, hT_hi, hT_lo, w_raw, w_hi, w_lo, w_strips,
           qk_d, v_d, mix_d, yp_d, za_d, at_d, gate_d):
    ITEMS = attention_items()
    NI = len(ITEMS)
    T_LAG, AV_LAG = 2, 3
    STEPS = NI + 6
    STRIPS = 6
    GROUPS = STRIPS * NC
    MM = 3 * KT
    ROWS = 2 * TT
    last_of_row = [n for n, it in enumerate(ITEMS) if it[5]]
    row_of = {n: r for r, n in enumerate(last_of_row)}
    row_at = []
    for n, it in enumerate(ITEMS):
        row_at.append(sum(1 for m in last_of_row if m < n))

    cost = [450.0 + 3.1 * ITEMS[s][3] if s < NI else 500.0 for s in range(STEPS - 2)]
    due, total = [], 0.0
    for cst in cost:
        total += cst
        due.append(total)
    due = [min(GROUPS * MM, round(d / total * GROUPS * MM)) for d in due] + [GROUPS * MM] * 2
    fin = [next(s for s in range(STEPS) if due[s] >= (k + 1) * MM) for k in range(GROUPS)]

    def first_step(test):
        return next(n for n, it in enumerate(ITEMS) if test(it))

    def last_step(test):
        return max(n for n, it in enumerate(ITEMS) if test(it))

    kv_units = []
    for e in range(2):
        for c in reversed(range(NC)):
            need = first_step(lambda it: it[0] == e and it[2] == c)
            before = last_step(lambda it: it[0] == 1 - e and it[2] == c) - (NI if e == 0 else 0)
            kv_units.append((e, c, max(0, need - 3), max(0, need), before))
    q_units = []
    for e in range(2):
        for r in reversed(range(TT // 2)):
            need = first_step(lambda it: it[0] == e and it[1] // 2 == r)
            u = len(q_units)
            if u >= 2:
                e2, r2 = q_units[u - 2][0], q_units[u - 2][1]
                before = last_step(lambda it: it[0] == e2 and it[1] // 2 == r2)
            else:
                before = last_step(lambda it: it[0] == 1 and it[1] // 2 == 1 - u) - NI
            q_units.append((e, r, max(0, need - 2), before))
    w_step = [0, 1] + [fin[4 * (j - 2) + 3] + 1 for j in range(2, STRIPS)]

    km = sb("km", [P, SEQ], F32R)
    vm = sb("vm", [P, TT, 2 * HD], F32R)
    qm_hi = sb("qm_hi", [P, 2, 2 * P], F32R)
    qm_lo = sb("qm_lo", [P, 2, 2 * P], F32R)
    k_raw = sb("k_raw", [P, CH])
    v_raw = sb("v_raw", [P, 4, HD])
    q_raw = sb("q_raw", [P, 2 * P])
    keep = sb("keep", [P, 2, CH + 1])
    beta = sb("beta", [P, 3, CH])
    left = sb("left", [P, 2, CH + 1])
    wt = sb("wt", [P, 2, 4, 2, P], F32R)
    half_sum = sb("half_sum", [P, 2 * P])
    row_sum = sb("row_sum", [P, 2 * P])
    y_out = sb("y_out", [P, 2, CH])
    mix_in_t = sb("mix_in", [P, CH])
    res = sb("res", [P, 2, CH])
    bias = sb("bias", [P, 4])

    w_in, w_hi_done, w_lo_done = sem("s3_w_in"), sem("s3_w_hi"), sem("s3_w_lo")
    k_in, v_in, q_in = sem("s3_k_in"), sem("s3_v_in"), sem("s3_q_in")
    k_hi, v_hi, q_hi = sem("s3_k_hi"), sem("s3_v_hi"), sem("s3_q_hi")
    k_lo, v_lo, q_lo = sem("s3_k_lo"), sem("s3_v_lo"), sem("s3_q_lo")
    scored, turned, weighed = sem("s3_scored"), sem("s3_turned"), sem("s3_weighed")
    keep_done, beta_done = sem("s3_keep"), sem("s3_beta")
    scanned, weights = sem("s3_scanned"), sem("s3_weights")
    wt_hi_done, wt_lo_done = sem("s3_wt_hi"), sem("s3_wt_lo")
    half_done, row_done, y_done = sem("s3_half"), sem("s3_row"), sem("s3_y")
    proj_done, act_out, silu_done, yp_done = sem("s3_proj"), sem("s3_act_out"), sem("s3_silu"), sem("s3_yp")
    mix_in = sem("s3_mix_in")
    res_stored = [sem(f"s3_res_stored{i}") for i in range(2)]
    y_stored = [sem(f"s3_y_stored{i}") for i in range(2)]
    ones, sp_tick, bias_done = sem("s3_ones"), sem("s3_sp_tick"), sem("s3_bias")

    def event(p, per, n):
        assert n >= -per
        return p * per + (per + n + 1)

    def bank_s(n):
        return psum[:, 2 + n % 2, :]

    def bank_t(n):
        return psum[:, 4 + n % 2, :]

    def bank_o(row):
        return psum[:, 6 + row % 2, 0:2 * P]

    def kind(k):
        return k // NC

    with nc.Block() as block:
        @block.sync
        def _(sp):
            def hold(s, value):
                sp.wait_ge(s, value)
                sp.sem_inc(sp_tick, 1)

            sp.sem_inc(w_in, STRIPS * DMA)
            sp.sem_inc(k_in, 2 * len(kv_units) * DMA)
            sp.sem_inc(v_in, len(kv_units) * DMA)
            sp.sem_inc(q_in, 2 * len(q_units) * DMA)
            sp.sem_inc(mix_in, NC * DMA)
            for i in range(2):
                sp.sem_inc(res_stored[i], GROUPS // 2 * DMA)
                sp.sem_inc(y_stored[i], 8 // 2 * DMA)
            with sp.Fori(0, PAIRS) as p:
                for s in range(-3, STEPS + 2):
                    def at(step):
                        return max(-3, step) == s
                    for u, (e, c, k_step, v_step, _b) in enumerate(kv_units):
                        cols = slice(c * CH, (c + 1) * CH)
                        if at(k_step - 3):
                            hold(k_lo, event(p, 8, u - 1))
                            for h in range(2):
                                sp.dma_start(k_raw[h * HD:(h + 1) * HD, :],
                                             qk_d[p + PAIRS, e * HD:(e + 1) * HD, cols]).then_inc(k_in, DMA)
                        if at(v_step - 3):
                            hold(v_lo, event(p, 8, u - 1))
                            sp.dma_start(v_raw[:, :, :],
                                         v_d[cols, bass.ds(p * P + e * HD, HD)].rearrange("(a q) d -> q a d", q=P)
                                         ).then_inc(v_in, DMA)
                    for u, (e, r, q_step, _b) in enumerate(q_units):
                        if at(q_step - 3):
                            hold(q_lo, event(p, 16, u - 1))
                            for h in range(2):
                                sp.dma_start(q_raw[h * HD:(h + 1) * HD, :],
                                             qk_d[p, e * HD:(e + 1) * HD, r * 2 * P:(r + 1) * 2 * P]
                                             ).then_inc(q_in, DMA)
                    for j in range(STRIPS):
                        if at(w_step[j] - 3):
                            hold(w_lo_done, event(p, STRIPS, j - 1))
                            strip = (p + S_ZP, p + S_ZA)[j] if j < 2 else p * 4 + (S_G + j - 2)
                            sp.dma_start(w_raw[:, :, :], w_strips[strip]).then_inc(w_in, DMA)
                    for k in range(NC):
                        if at(fin[k] - 2):
                            hold(yp_done, event(p, NC, k - 1))
                            sp.dma_start(mix_in_t[:, :], mix_d[p, :, k * CH:(k + 1) * CH]).then_inc(mix_in, DMA)
                    for k in range(GROUPS):
                        if fin[k] + 2 == s:
                            cols = slice(k % NC * CH, (k % NC + 1) * CH)
                            if kind(k) == 0:
                                sp.wait_ge(yp_done, event(p, NC, k))
                                dst = yp_d[p, :, cols]
                            elif kind(k) == 1:
                                sp.wait_ge(silu_done, event(p, 2 * NC, k))
                                dst = za_d[p, :, cols]
                            else:
                                sp.wait_ge(act_out, event(p, GROUPS, k))
                                dst = gate_d[p * 4 + (kind(k) - 2), :, cols]
                            sp.dma_start(dst, res[:, k % 2, :]).then_inc(res_stored[k % 2], DMA)
                    for n in last_of_row:
                        e, i = ITEMS[n][0:2]
                        if n + AV_LAG + 2 == s or (s == STEPS + 1 and n + AV_LAG + 2 > s):
                            if i % 4 == 0:
                                u = 4 * e + 3 - i // 4
                                sp.wait_ge(y_done, event(p, ROWS, row_of[n]))
                                sp.dma_start(at_d[p, e * HD:(e + 1) * HD, i * P:i * P + CH],
                                             y_out[e * HD:(e + 1) * HD, u % 2, :]).then_inc(y_stored[u % 2], DMA)
            for i in range(2):
                sp.wait_ge(res_stored[i], (PAIRS + 1) * GROUPS // 2 * DMA)
                sp.wait_ge(y_stored[i], (PAIRS + 1) * 4 * DMA)

        @block.tensor
        def _(pe):
            pe.sem_inc(scored, NI)
            pe.sem_inc(turned, NI)
            pe.sem_inc(weighed, NI)
            pe.sem_inc(proj_done, GROUPS)

            def projections(p):
                for j in range(STRIPS):
                    pe.wait_ge(w_lo_done, event(p, STRIPS, j))
                    for c in range(NC):
                        k = j * NC + c
                        m = k - 2 if k >= 2 else k - 2 + GROUPS
                        if kind(m) < 2:
                            pe.wait_ge(silu_done, event(p, 2 * NC, m))
                        else:
                            pe.wait_ge(act_out, event(p, GROUPS, k - 2))
                        tok = slice(c * CH, (c + 1) * CH)
                        for kt in range(KT):
                            hi, lo = w_hi[:, j % 2, kt, :], w_lo[:, j % 2, kt, :]
                            o = psum[:, k % 2, :]
                            pe.matmul(o, hi, hT_hi[:, kt, tok], start=kt == 0, stop=False)
                            yield
                            pe.matmul(o, hi, hT_lo[:, kt, tok], start=False, stop=False)
                            yield
                            last = pe.matmul(o, lo, hT_hi[:, kt, tok], start=False, stop=kt == KT - 1)
                            if kt == KT - 1:
                                last.then_inc(proj_done, 1)
                            yield

            def score(p, n):
                e, i, c, w, first, _l = ITEMS[n]
                pe.wait_ge(beta_done, event(p, NI, n - 2))
                u = 4 * e + 3 - c
                pe.wait_ge(k_lo, event(p, 8, u))
                uq = 8 * e + 7 - i // 2
                pe.wait_ge(q_lo, event(p, 16, uq))
                cols = slice(i % 2 * P, i % 2 * P + P)
                o = bank_s(n)
                keys = slice(c * CH, c * CH + w)
                pe.matmul(o[:, 0:w], qm_hi[:, uq % 2, cols], km[:, keys], start=True, stop=False)
                last = pe.matmul(o[:, 0:w], qm_lo[:, uq % 2, cols], km[:, keys], start=False, stop=not first)
                if first:
                    last = pe.matmul(o[:, w - P:w], ident_r[:, :], mask_r[:, :], start=False, stop=True)
                last.then_inc(scored, 1)

            def turn(p, n):
                w = ITEMS[n][3]
                pe.wait_ge(weights, event(p, NI, n))
                pe.wait_ge(wt_lo_done, event(p, NI, n - 2))
                for j in range(w // P):
                    a = CH - w + j * P
                    last = pe.transpose(bank_t(n)[:, j * P:(j + 1) * P], beta[:, n % 3, a:a + P], ident[:, :])
                last.then_inc(turned, 1)

            def weigh(p, n):
                e, i, c, w, first, final = ITEMS[n]
                row = row_at[n]
                pe.wait_ge(wt_lo_done, event(p, NI, n))
                pe.wait_ge(v_lo, event(p, 8, 4 * e + 3 - c))
                if first:
                    pe.wait_ge(row_done, event(p, ROWS, row - 2))
                for j in range(w // P):
                    last = pe.matmul(bank_o(row), vm[:, 4 * c + j, :],
                                     wt[:, n % 2, j, :, :].rearrange("p a q -> p (a q)"),
                                     start=first and j == 0, stop=final and j == w // P - 1)
                last.then_inc(weighed, 1)

            with pe.Fori(0, PAIRS) as p:
                proj, done = projections(p), 0
                for s in range(STEPS):
                    if s < NI:
                        score(p, s)
                    mid = done + (due[s] - done) // 2
                    while done < mid:
                        next(proj)
                        done += 1
                    if 0 <= s - T_LAG < NI:
                        turn(p, s - T_LAG)
                    while done < due[s]:
                        next(proj)
                        done += 1
                    if 0 <= s - AV_LAG < NI:
                        weigh(p, s - AV_LAG)

        @block.scalar
        def _(act):
            act.sem_inc(w_hi_done, STRIPS)
            for s, n in ((k_hi, 8), (v_hi, 8), (q_hi, 16), (keep_done, NI), (beta_done, NI), (wt_hi_done, NI),
                         (half_done, ROWS), (act_out, GROUPS)):
                act.sem_inc(s, n)

            def splits(p, s):
                for u, (e, c, k_step, v_step, before) in enumerate(kv_units):
                    if k_step == s:
                        act.wait_ge(k_in, p * (16 * DMA) + (16 + 2 * u + 2) * DMA)
                        act.wait_ge(scored, event(p, NI, before))
                        act.activation(km[:, c * CH:(c + 1) * CH], k_raw[:, :], ACT.Copy).then_inc(k_hi, 1)
                    if v_step == s:
                        act.wait_ge(v_in, p * (8 * DMA) + (8 + u + 1) * DMA)
                        act.wait_ge(weighed, event(p, NI, before))
                        act.activation(vm[:, 4 * c:4 * c + 4, 0:HD], v_raw[:, :, :], ACT.Copy).then_inc(v_hi, 1)
                for u, (e, r, q_step, before) in enumerate(q_units):
                    if q_step == s:
                        act.wait_ge(q_in, p * (32 * DMA) + (32 + 2 * u + 2) * DMA)
                        act.wait_ge(scored, event(p, NI, before))
                        act.activation(qm_hi[:, u % 2, :], q_raw[:, :], ACT.Copy).then_inc(q_hi, 1)
                for j in range(STRIPS):
                    if w_step[j] == s:
                        act.wait_ge(w_in, p * (STRIPS * DMA) + (STRIPS + j + 1) * DMA)
                        act.wait_ge(proj_done, event(p, GROUPS, NC * (j - 2) + NC - 1))
                        act.activation(w_hi[:, j % 2, :, :], w_raw[:, :, :], ACT.Copy).then_inc(w_hi_done, 1)

            def result(p, k):
                act.wait_ge(proj_done, event(p, GROUPS, k))
                act.wait_ge(res_stored[k % 2], p * (GROUPS // 2 * DMA) + (GROUPS // 2 + k // 2) * DMA)
                if kind(k) < 2:
                    act.activation(res[:, k % 2, :], psum[:, k % 2, :], ACT.Sigmoid).then_inc(act_out, 1)
                else:
                    act.activation(res[:, k % 2, :], psum[:, k % 2, :], ACT.Sigmoid,
                                   bias=bias[:, kind(k) - 2:kind(k) - 1]).then_inc(act_out, 1)

            with act.Fori(0, PAIRS) as p:
                act.activation(bias[:, :], bcol[:, bass.ds(p * 4, 4)], ACT.Copy).then_inc(bias_done, 1)
                act.wait_ge(bias_done, p + 1)
                for s in range(STEPS + 2):
                    splits(p, s)
                    if s < NI:
                        w = ITEMS[s][3]
                        act.wait_ge(scored, event(p, NI, s))
                        act.wait_ge(scanned, event(p, NI, s - 2))
                        act.activation(keep[:, s % 2, CH - w:CH], bank_s(s)[:, 0:w], ACT.Sigmoid,
                                       scale=-SCALE).then_inc(keep_done, 1)
                        act.wait_ge(turned, event(p, NI, s - 3 if s >= 3 else (NI - 1 - (NI - 1 - s) % 3) - NI))
                        act.activation(beta[:, s % 3, CH - w:CH], bank_s(s)[:, 0:w], ACT.Sigmoid,
                                       scale=SCALE).then_inc(beta_done, 1)
                    n = s - T_LAG
                    if 0 <= n < NI:
                        w = ITEMS[n][3]
                        act.wait_ge(turned, event(p, NI, n))
                        act.wait_ge(weighed, event(p, NI, n - 2))
                        act.activation(wt[:, n % 2, 0:w // P, 0, :],
                                       bank_t(n)[:, 0:w].rearrange("p (j q) -> p j q", q=P),
                                       ACT.Copy).then_inc(wt_hi_done, 1)
                    n = s - AV_LAG - 1
                    if n in row_of:
                        e, row = ITEMS[n][0], row_of[n]
                        mine, other = slice(e * HD, e * HD + HD), slice(HD - e * HD, 2 * HD - e * HD)
                        act.wait_ge(weighed, event(p, NI, n))
                        act.wait_ge(row_done, event(p, ROWS, row - 1))
                        act.activation(half_sum[mine, :], bank_o(row)[other, :], ACT.Copy).then_inc(half_done, 1)
                    for k in range(GROUPS):
                        if fin[k] + 1 == s:
                            result(p, k)
                act.wait_ge(act_out, event(p, GROUPS, GROUPS - 1))

        @block.vector
        def _(dve):
            for s, n in ((scanned, NI), (weights, NI), (wt_lo_done, NI), (row_done, ROWS), (silu_done, 2 * NC)):
                dve.sem_inc(s, n)
            dve.wait_ge(ones, 2)

            def low_part(p, n):
                w = ITEMS[n][3]
                dve.wait_ge(wt_hi_done, event(p, NI, n))
                dve.tensor_tensor(wt[:, n % 2, 0:w // P, 1, :],
                                  bank_t(n)[:, 0:w].rearrange("p (j q) -> p j q", q=P),
                                  wt[:, n % 2, 0:w // P, 0, :].bitcast(F32), ALU.subtract).then_inc(wt_lo_done, 1)

            with dve.Fori(0, PAIRS) as p:
                for s in range(STEPS + 2):
                    if s < NI:
                        _e, _i, _c, w, first, _l = ITEMS[s]
                        span = slice(CH - w, CH + 1)
                        if first:
                            carry = 1.0
                        else:
                            dve.wait_ge(scanned, event(p, NI, s - 1))
                            a = CH - ITEMS[s - 1][3]
                            carry = left[:, (s - 1) % 2, a:a + 1]
                        dve.wait_ge(keep_done, event(p, NI, s))
                        k = keep[:, s % 2, span][:, ::-1]
                        dve.tensor_tensor_scan(left[:, s % 2, span][:, ::-1], k, k, carry,
                                               ALU.mult, ALU.bypass).then_inc(scanned, 1)
                    if 0 <= s - T_LAG - 1 < NI:
                        low_part(p, s - T_LAG - 1)
                    if s < NI:
                        w = ITEMS[s][3]
                        dve.wait_ge(beta_done, event(p, NI, s))
                        dve.wait_ge(scanned, event(p, NI, s))
                        dve.tensor_tensor(beta[:, s % 3, CH - w:CH], beta[:, s % 3, CH - w:CH],
                                          left[:, s % 2, CH - w + 1:CH + 1], ALU.mult).then_inc(weights, 1)
                    n = s - AV_LAG - 1
                    if n in row_of:
                        e, row = ITEMS[n][0], row_of[n]
                        mine = slice(e * HD, e * HD + HD)
                        dve.wait_ge(half_done, event(p, ROWS, row))
                        dve.wait_ge(y_done, event(p, ROWS, row - 1))
                        dve.tensor_tensor(row_sum[mine, :], bank_o(row)[mine, :], half_sum[mine, :],
                                          ALU.add).then_inc(row_done, 1)
                    for k in range(2 * NC):
                        if fin[k] + 1 == s:
                            dve.wait_ge(act_out, event(p, GROUPS, k))
                            dve.tensor_tensor(res[:, k % 2, :], psum[:, k % 2, :], res[:, k % 2, :],
                                              ALU.mult).then_inc(silu_done, 1)

        @block.gpsimd
        def _(pool):
            for s, n in ((w_lo_done, STRIPS), (k_lo, 8), (v_lo, 8), (q_lo, 16), (y_done, ROWS), (yp_done, NC)):
                pool.sem_inc(s, n)
            for i in range(2):
                pool.memset(keep[:, i, CH:CH + 1], 1.0).then_inc(ones, 1)
            pool.wait_ge(ones, 2)
            before = [ones, 2]

            def step(out_, a, b, op, s, value):
                pool.wait_ge(*before)
                pool.tensor_tensor(out_, a, b, op).then_inc(s, 1)
                before[:] = [s, value]

            with pool.Fori(0, PAIRS) as p:
                before[:] = [ones, 2]
                for s in range(STEPS + 2):
                    for u, (e, c, k_step, v_step, _b) in enumerate(kv_units):
                        if k_step == s:
                            pool.wait_ge(k_hi, event(p, 8, u))
                            low = km[HD:P, c * CH:(c + 1) * CH]
                            step(low, k_raw[HD:P, :], low.bitcast(F32), ALU.subtract, k_lo, event(p, 8, u))
                        if v_step == s:
                            pool.wait_ge(v_hi, event(p, 8, u))
                            step(vm[:, 4 * c:4 * c + 4, HD:2 * HD], v_raw[:, :, :],
                                 vm[:, 4 * c:4 * c + 4, 0:HD].bitcast(F32), ALU.subtract, v_lo, event(p, 8, u))
                    for u, (e, r, q_step, _b) in enumerate(q_units):
                        if q_step == s:
                            pool.wait_ge(q_hi, event(p, 16, u))
                            step(qm_lo[:, u % 2, :], q_raw[:, :], qm_hi[:, u % 2, :].bitcast(F32),
                                 ALU.subtract, q_lo, event(p, 16, u))
                    for j in range(STRIPS):
                        if w_step[j] == s:
                            pool.wait_ge(w_hi_done, event(p, STRIPS, j))
                            step(w_lo[:, j % 2, :, :], w_raw[:, :, :], w_hi[:, j % 2, :, :].bitcast(F32),
                                 ALU.subtract, w_lo_done, event(p, STRIPS, j))
                    n = s - AV_LAG - 1
                    if n in row_of:
                        e, i, row = ITEMS[n][0], ITEMS[n][1], row_of[n]
                        mine = slice(e * HD, e * HD + HD)
                        u = row // 4
                        pool.wait_ge(row_done, event(p, ROWS, row))
                        if i % 4 == 3:
                            pool.wait_ge(y_stored[u % 2], p * (4 * DMA) + (4 + u // 2) * DMA)
                        step(y_out[mine, u % 2, i % 4 * P:i % 4 * P + P], row_sum[mine, 0:P],
                             row_sum[mine, P:2 * P], ALU.add, y_done, event(p, ROWS, row))
                    for k in range(NC):
                        if fin[k] + 1 == s:
                            pool.wait_ge(silu_done, event(p, 2 * NC, k))
                            pool.wait_ge(mix_in, p * (NC * DMA) + (NC + k + 1) * DMA)
                            step(res[:, k % 2, :], res[:, k % 2, :], mix_in_t[:, :], ALU.mult,
                                 yp_done, event(p, NC, k))
                pool.wait_ge(*before)


def stage4(nc, sem, psum, sb, x, yp_d, za_d, at_d, gate_d, w_pool_up, w_attn_up, w_out, final_g, out):
    UK = AW // P
    up_hi = [sb(f"up_hi{b}", [P, UK, D], F32R) for b in range(2)]
    up_lo = [sb(f"up_lo{b}", [P, UK, D], F32R) for b in range(2)]
    wo_hi = sb("wo_hi", [P, KT, D], F32R)
    wo_lo = sb("wo_lo", [P, KT, D], F32R)
    y_hi = [sb(f"y_hi{b}", [P, UK, CH], F32R) for b in range(2)]
    y_lo = [sb(f"y_lo{b}", [P, UK, CH], F32R) for b in range(2)]
    y_raw = sb("y_raw", [P, 2, CH])
    z_raw = sb("z_raw", [P, CH])
    gate = sb("gate", [P, 4, CH])
    m_hi = sb("m_hi", [P, KT, CH], F32R)
    m_lo = sb("m_lo", [P, KT, CH], F32R)
    row = sb("row", [P, 2, D])
    raw = row[:, :, 0:CH]
    fg = sb("fg", [P, D])
    st = sb("st4", [P, 2, 8])

    n_raw = 2 * (2 * UK + KT)
    up_n = 4 * UK
    fg_in = sem("s4_fg_in")
    raw_in = [sem(f"s4_raw_in{i}") for i in range(2)]
    raw_hi, raw_lo = sem("s4_raw_hi"), sem("s4_raw_lo")
    y_in = [sem(f"s4_y_in{i}") for i in range(2)]
    z_in, z_done = sem("s4_z_in"), sem("s4_z_done")
    y_hi_done, y_lo_done = sem("s4_y_hi"), sem("s4_y_lo")
    g_in = [sem(f"s4_g_in{i}") for i in range(2)]
    up_done, gated, summed = sem("s4_up_done"), sem("s4_gated"), sem("s4_summed")
    m_hi_done, m_lo_done = sem("s4_m_hi"), sem("s4_m_lo")
    out_done, added = sem("s4_out_done"), sem("s4_added")
    x_in = [sem(f"s4_x_in{i}") for i in range(2)]
    squared, mean, rooted, newton, scaled = (sem(f"s4_{n}") for n in ("squared", "mean", "rooted", "newton", "scaled"))
    finished = sem("s4_finished")
    stored = [sem(f"s4_stored{i}") for i in range(2)]
    NY, NM, NT = 2 * UK, KT, CH // P

    def event(c, per, n):
        assert n >= -per
        return c * per + (per + n + 1)

    def piece(i):
        half = slice(i % 2 * CH, (i % 2 + 1) * CH)
        k = i // 2
        if k < 2 * UK:
            b, k = divmod(k, UK)
            return (w_pool_up, w_attn_up)[b][:, k, half], up_hi[b][:, k, half], up_lo[b][:, k, half]
        k -= 2 * UK
        return w_out[:, k, half], wo_hi[:, k, half], wo_lo[:, k, half]

    with nc.Block() as block:
        @block.sync
        def _(sp):
            def load_weights(a, b):
                for i in range(a, b):
                    if i >= 2:
                        sp.wait_ge(raw_lo, i - 1)
                    sp.dma_start(raw[:, i % 2, :], piece(i)[0]).then_inc(raw_in[i % 2], DMA)

            def load_y(c, i):
                b, k = divmod(i, UK)
                tok = bass.ds(c * CH, CH)
                sp.wait_ge(y_lo_done, event(c, NY, i - 2))
                sp.dma_start(y_raw[:, i % 2, :], (yp_d, at_d)[b][k, :, tok]).then_inc(y_in[i % 2], DMA)
                if b == 1:
                    sp.wait_ge(z_done, event(c, UK, k - 1))
                    sp.dma_start(z_raw[:, :], za_d[k, :, tok]).then_inc(z_in, DMA)

            def load_gates(c, m):
                tok = bass.ds(c * CH, CH)
                sp.wait_ge(m_lo_done, event(c, NM, m - 2))
                for b in range(2):
                    sp.dma_start(gate[:, m % 2 * 2 + b, :], gate_d[b * KT + m, :, tok]).then_inc(g_in[m % 2], DMA)

            def load_x(c, t):
                sp.wait_ge(stored[t % 2], c * (2 * DMA) + (2 + t // 2) * DMA)
                sp.dma_start(row[:, t % 2, :], x[bass.ds(c * CH + t * P, P), :]).then_inc(x_in[t % 2], DMA)

            def store(c, t):
                sp.wait_ge(finished, event(c, NT, t))
                sp.dma_start(out[bass.ds(c * CH + t * P, P), :], row[:, t % 2, :]).then_inc(stored[t % 2], DMA)

            def tail(c):
                for m in range(NM):
                    load_gates(c, m)
                load_x(c, 0)
                load_x(c, 1)
                store(c, 0)
                load_x(c, 2)
                store(c, 1)
                load_x(c, 3)
                store(c, 2)
                store(c, 3)

            for s, n in ((y_in[0], NY // 2), (y_in[1], NY // 2), (z_in, UK), (g_in[0], NM), (g_in[1], NM),
                         (x_in[0], 2), (x_in[1], 2), (stored[0], 2), (stored[1], 2)):
                sp.sem_inc(s, n * DMA)
            load_weights(0, up_n // 2)
            for i in range(UK):
                load_y(0, i)
            load_weights(up_n // 2, up_n)
            for i in range(UK, NY):
                load_y(0, i)
            sp.dma_start(fg[:, :], final_g.partition_broadcast(P)).then_inc(fg_in, DMA)
            load_gates(0, 0)
            load_gates(0, 1)
            per = (n_raw - up_n) // NM
            load_weights(up_n, up_n + 2 * per)
            for m in range(2, NM):
                load_gates(0, m)
                load_weights(up_n + per * m, up_n + per * (m + 1))
            sp.wait_ge(raw_lo, n_raw)
            load_x(0, 0)
            load_x(0, 1)
            for i in range(2):
                load_y(1, i)
            store(0, 0)
            load_x(0, 2)
            store(0, 1)
            load_x(0, 3)
            for i in range(2, NY):
                load_y(1, i)
            store(0, 2)
            store(0, 3)
            with sp.Fori(1, NC - 1) as c:
                for m in range(NM):
                    load_gates(c, m)
                load_x(c, 0)
                load_x(c, 1)
                for i in range(2):
                    load_y(c + 1, i)
                store(c, 0)
                load_x(c, 2)
                store(c, 1)
                load_x(c, 3)
                for i in range(2, NY):
                    load_y(c + 1, i)
                store(c, 2)
                store(c, 3)
            tail(NC - 1)
            for s in stored:
                sp.wait_ge(s, (NC + 1) * 2 * DMA)

        @block.tensor
        def _(pe):
            for s, n in ((up_done, 2 * NM), (out_done, 2 * NT)):
                pe.sem_inc(s, n)
            pe.wait_ge(raw_lo, up_n)

            def up(c, m):
                for b in range(2):
                    if m == 0:
                        pe.wait_ge(y_lo_done, event(c, NY, UK * (b + 1) - 1))
                    pe.wait_ge(gated, event(c, 2 * NM, 2 * m + b - 4))
                    for k in range(UK):
                        cols = slice(m * P, (m + 1) * P)
                        last = split3(pe, psum[:, m % 2 * 2 + b, :], up_hi[b][:, k, cols], up_lo[b][:, k, cols],
                                      y_hi[b][:, k, :], y_lo[b][:, k, :], k == 0, k == UK - 1)
                    last.then_inc(up_done, 1)

            def project(c, t, h, ks):
                n = 2 * t + h
                cols, tok = slice(h * CH, (h + 1) * CH), slice(t * P, (t + 1) * P)
                for k in ks:
                    pe.wait_ge(m_lo_done, event(c, NM, k)) if t == 0 else None
                    if k == 0:
                        pe.wait_ge(squared, event(c, NT, t - 2))
                    last = split3(pe, psum[:, 4 + n % 4, :], m_hi[:, k, tok], m_lo[:, k, tok],
                                  wo_hi[:, k, cols], wo_lo[:, k, cols], k == 0, k == KT - 1)
                if KT - 1 in ks:
                    last.then_inc(out_done, 1)

            with pe.Fori(0, NC) as c:
                for m in range(NM):
                    up(c, m)
                pe.wait_ge(raw_lo, n_raw)
                for h in range(2):
                    project(c, 0, h, range(KT - 1))
                for h in range(2):
                    project(c, 0, h, range(KT - 1, KT))
                for t in range(1, NT):
                    for h in range(2):
                        project(c, t, h, range(KT))

        @block.scalar
        def _(act):
            for s, n in ((y_hi_done, NY), (m_hi_done, NM), (squared, NT), (rooted, NT)):
                act.sem_inc(s, n)

            def split_weights(a, b):
                for i in range(a, b):
                    act.wait_ge(raw_in[i % 2], DMA * (i // 2 + 1))
                    act.activation(piece(i)[1], raw[:, i % 2, :], ACT.Copy).then_inc(raw_hi, 1)

            def split_y(c, i):
                b, k = divmod(i, UK)
                if b == 0:
                    act.wait_ge(y_in[i % 2], c * (NY // 2 * DMA) + (NY // 2 + i // 2 + 1) * DMA)
                else:
                    act.wait_ge(z_done, event(c, UK, k))
                act.wait_ge(up_done, event(c, 2 * NM, b - 2))
                act.activation(y_hi[b][:, k, :], y_raw[:, i % 2, :], ACT.Copy).then_inc(y_hi_done, 1)

            def merge(c, m):
                act.wait_ge(summed, event(c, NM, m))
                act.wait_ge(out_done, event(c, 2 * NT, -1))
                act.activation(m_hi[:, m, :], gate[:, m % 2 * 2, :], ACT.Copy).then_inc(m_hi_done, 1)

            def square(c, t):
                act.wait_ge(added, event(c, 2 * NT, 2 * t + 1))
                act.activation(psum[:, 4 + 2 * t % 4:6 + 2 * t % 4, :],
                               row[:, t % 2, :].rearrange("p (a b) -> p a b", a=2), ACT.Square,
                               accum_out=st[:, t % 2, 0:1]).then_inc(squared, 1)

            def root(c, t):
                act.wait_ge(mean, event(c, 2 * NT, 2 * t + 1))
                act.activation(st[:, t % 2, 3:4], st[:, t % 2, 2:3], ACT.Sqrt).then_inc(rooted, 1)

            split_weights(0, up_n // 2)
            for i in range(UK):
                split_y(0, i)
            split_weights(up_n // 2, up_n)
            for i in range(UK, NY):
                split_y(0, i)
            per = (n_raw - up_n) // NM
            for m in range(NM):
                split_weights(up_n + per * m, up_n + per * (m + 1))
                merge(0, m)
            for t in range(NT):
                square(0, t)
                root(0, t)
                for i in (2 * t, 2 * t + 1):
                    split_y(1, i)
            with act.Fori(1, NC - 1) as c:
                for m in range(NM):
                    merge(c, m)
                for t in range(NT):
                    square(c, t)
                    root(c, t)
                    for i in (2 * t, 2 * t + 1):
                        split_y(c + 1, i)
            for m in range(NM):
                merge(NC - 1, m)
            for t in range(NT):
                square(NC - 1, t)
                root(NC - 1, t)

        @block.vector
        def _(dve):
            for s, n in ((y_lo_done, NY), (gated, 2 * NM), (added, 2 * NT), (mean, 2 * NT), (newton, 2 * NT),
                         (scaled, NT), (finished, NT)):
                dve.sem_inc(s, n)

            def weights_lo(a, b):
                for i in range(a, b):
                    dve.wait_ge(raw_hi, i + 1)
                    _src, hi, lo = piece(i)
                    dve.tensor_tensor(lo, raw[:, i % 2, :], hi.bitcast(F32), ALU.subtract).then_inc(raw_lo, 1)

            def y_low(c, i):
                b, k = divmod(i, UK)
                dve.wait_ge(y_hi_done, event(c, NY, i))
                dve.tensor_tensor(y_lo[b][:, k, :], y_raw[:, i % 2, :], y_hi[b][:, k, :].bitcast(F32),
                                  ALU.subtract).then_inc(y_lo_done, 1)

            def apply_gates(c, m):
                for b in range(2):
                    g = gate[:, m % 2 * 2 + b, :]
                    dve.wait_ge(g_in[m % 2], c * (NM * DMA) + (NM + m // 2 * 2 + 2) * DMA)
                    dve.wait_ge(up_done, event(c, 2 * NM, 2 * m + b))
                    dve.tensor_tensor(g, psum[:, m % 2 * 2 + b, :], g, ALU.mult).then_inc(gated, 1)

            def finish(c, t):
                s = st[:, t % 2, :]
                for h in range(2):
                    r = row[:, t % 2, h * CH:(h + 1) * CH]
                    n = 2 * t + h
                    dve.wait_ge(out_done, event(c, 2 * NT, n))
                    if h == 0:
                        dve.wait_ge(x_in[t % 2], c * (2 * DMA) + (2 + t // 2 + 1) * DMA)
                    dve.tensor_tensor(r, psum[:, 4 + n % 4, :], r, ALU.add).then_inc(added, 1)
                dve.wait_ge(squared, event(c, NT, t))
                dve.tensor_scalar(s[:, 1:2], s[:, 0:1], 1.0 / D, EPS, ALU.mult, ALU.add).then_inc(mean, 1)
                dve.wait_ge(mean, event(c, 2 * NT, 2 * t))
                dve.reciprocal(s[:, 2:3], s[:, 1:2]).then_inc(mean, 1)
                dve.wait_ge(rooted, event(c, NT, t))
                dve.tensor_scalar(s[:, 4:5], s[:, 3:4], s[:, 3:4], s[:, 1:2], ALU.mult,
                                  ALU.mult).then_inc(newton, 1)
                dve.wait_ge(newton, event(c, 2 * NT, 2 * t))
                dve.tensor_scalar(s[:, 5:6], s[:, 4:5], -0.5, 1.5, ALU.mult, ALU.add).then_inc(newton, 1)
                dve.wait_ge(newton, event(c, 2 * NT, 2 * t + 1))
                r = row[:, t % 2, :]
                dve.tensor_scalar(r, r, s[:, 3:4], s[:, 5:6], ALU.mult, ALU.mult).then_inc(scaled, 1)
                dve.wait_ge(scaled, event(c, NT, t))
                dve.tensor_tensor(r, r, fg[:, :], ALU.mult).then_inc(finished, 1)

            weights_lo(0, up_n // 2)
            for i in range(UK):
                y_low(0, i)
            weights_lo(up_n // 2, up_n)
            for i in range(UK, NY):
                y_low(0, i)
            dve.wait_ge(fg_in, DMA)
            per = (n_raw - up_n) // NM
            for m in range(NM):
                weights_lo(up_n + per * m, up_n + per * (m + 1))
                apply_gates(0, m)
            for t in range(NT):
                finish(0, t)
                for i in (2 * t, 2 * t + 1):
                    y_low(1, i)
            with dve.Fori(1, NC - 1) as c:
                for m in range(NM):
                    apply_gates(c, m)
                for t in range(NT):
                    finish(c, t)
                    for i in (2 * t, 2 * t + 1):
                        y_low(c + 1, i)
            for m in range(NM):
                apply_gates(NC - 1, m)
            for t in range(NT):
                finish(NC - 1, t)

        @block.gpsimd
        def _(pool):
            for s, n in ((z_done, UK), (summed, NM), (m_lo_done, NM)):
                pool.sem_inc(s, n)

            def gate_attention(c, k):
                i = UK + k
                pool.wait_ge(y_in[i % 2], c * (NY // 2 * DMA) + (NY // 2 + i // 2 + 1) * DMA)
                pool.wait_ge(z_in, c * (UK * DMA) + (UK + k + 1) * DMA)
                pool.tensor_tensor(y_raw[:, i % 2, :], y_raw[:, i % 2, :], z_raw[:, :], ALU.mult).then_inc(z_done, 1)

            def merge(c, m):
                g = m % 2 * 2
                pool.wait_ge(gated, event(c, 2 * NM, 2 * m + 1))
                pool.tensor_tensor(gate[:, g, :], gate[:, g, :], gate[:, g + 1, :], ALU.add).then_inc(summed, 1)
                pool.wait_ge(m_hi_done, event(c, NM, m))
                pool.tensor_tensor(m_lo[:, m, :], gate[:, g, :], m_hi[:, m, :].bitcast(F32),
                                   ALU.subtract).then_inc(m_lo_done, 1)

            with pool.Fori(0, NC) as c:
                for k in range(UK):
                    gate_attention(c, k)
                for m in range(NM):
                    merge(c, m)


def kernel(x, norm_g, w_in, b_gate, pool_w, pool_scale, w_pool_up, w_attn_up, w_out, final_g):
    import numpy as np
    import concourse.bacc as bacc
    from concourse.bass_utils import run_bass_kernel_spmd

    def columns(a):
        return np.ascontiguousarray(np.asarray(a).reshape(-1, P).T)

    def by_k(a):
        a = np.asarray(a)
        return np.ascontiguousarray(a.reshape(-1, P, a.shape[-1]).transpose(1, 0, 2))

    w = np.asarray(w_in)[0]
    v_cols = slice(S_ZA * P - AW, S_ZA * P)
    counts = np.minimum(np.arange(PAD)[None, :] + 1, np.array(WINDOWS)[:, None])
    fix = np.broadcast_to((np.array(WINDOWS)[:, None] / counts).astype(np.float32), (P, len(WINDOWS), PAD))
    arrays = {
        "x": np.ascontiguousarray(np.asarray(x)[0]),
        "norm_gT": columns(np.asarray(norm_g)[0]),
        "w_strips": np.ascontiguousarray(w.reshape(KT, P, -1, P).transpose(2, 1, 0, 3)),
        "w_v": by_k(w[:, v_cols]),
        "b_gateT": columns(np.asarray(b_gate)[0]),
        "pool_w": np.ascontiguousarray(np.asarray(pool_w)[0]),
        "pool_scaleT": columns(np.asarray(pool_scale)[0]),
        "w_pool_up": by_k(np.asarray(w_pool_up)[0]),
        "w_attn_up": by_k(np.asarray(w_attn_up)[0]),
        "w_out": by_k(np.asarray(w_out)[0]),
        "final_g": np.ascontiguousarray(np.asarray(final_g)),
        "pool_fix": np.ascontiguousarray(fix),
    }
    nc = bacc.Bacc("TRN2", target_bir_lowering=False, num_devices=1, dynamic_dma_scratch_size=2048)
    args = {n: nc.dram_tensor("in_" + n, a.shape, mybir.dt.from_np(a.dtype), kind="ExternalInput").ap()
            for n, a in arrays.items()}
    out = nc.dram_tensor("out_0", (SEQ, D), F32, kind="ExternalOutput").ap()
    build(nc, **args, out=out)
    r = run_bass_kernel_spmd(nc, [{"in_" + n: a for n, a in arrays.items()}], core_ids=[0])
    return r.results[0]["out_0"].reshape(1, SEQ, D)
```

```python
from contextlib import ExitStack

import concourse.bass as bass
from concourse import mybir

F32 = mybir.dt.float32
F32R = mybir.dt.float32r
ALU = mybir.AluOpType
ACT = mybir.ActivationFunctionType

P = 128
SEQ = 2048
D = 1024
KT = D // P
TT = SEQ // P
CH = 512
NC = SEQ // CH
HD = 64
HEADS = 8
PAIRS = HEADS // 2
AW = HEADS * HD
WINDOWS = (2, 4, 8, 16)
PAD = max(WINDOWS)
EPS = 1e-6
SCALE = HD ** -0.5
MASK = -1.0e30
DMA = 16
POOL_ORDER = (3, 2, 1, 0)
S_U, S_ZP, S_Q, S_K, S_ZA, S_G = 0, 4, 8, 12, 20, 24


class Arena:

    def __init__(self, nc, at, end):
        self.nc, self.at, self.end = nc, at, end

    def __call__(self, name, shape, dtype=F32):
        t = self.nc.alloc_sbuf_tensor_at(name, shape, dtype, offset=self.at)
        size = 4
        for n in shape[1:]:
            size *= n
        self.at += -(-size // 32) * 32
        assert self.at <= self.end, (name, self.at, self.end)
        return t


def split3(pe, out, w_hi, w_lo, m_hi, m_lo, start, stop):
    pe.matmul(out, w_hi, m_hi, start=start, stop=False)
    pe.matmul(out, w_hi, m_lo, start=False, stop=False)
    return pe.matmul(out, w_lo, m_hi, start=False, stop=stop)


def build(nc, x, norm_gT, w_strips, w_v, b_gateT, pool_w, pool_scaleT, w_pool_up, w_attn_up, w_out,
          final_g, pool_fix, out):
    def scratch(name, shape):
        return nc.dram_tensor(name, shape, F32, kind="Internal").ap()

    qk_d = scratch("qk_scratch", [2 * PAIRS, P, SEQ])
    v_d = scratch("v_scratch", [SEQ, AW])
    mix_d = scratch("mix_scratch", [PAIRS, P, SEQ])
    yp_d = scratch("y_pool_scratch", [PAIRS, P, SEQ])
    za_d = scratch("z_attn_scratch", [PAIRS, P, SEQ])
    at_d = scratch("attn_scratch", [PAIRS, P, SEQ])
    gate_d = scratch("gate_scratch", [4 * PAIRS, P, SEQ])

    with ExitStack() as ctx:
        def sem(name):
            return ctx.enter_context(nc.semaphore(name))

        psum = ctx.enter_context(nc.psum_tensor("psum", [P, 8, 512], F32))
        base = -(-nc.sbuf_base // 32) * 32
        end = nc.sbuf_usable_end
        fixed = Arena(nc, base, end)
        ident = fixed("ident", [P, P])
        ident_r = fixed("ident_r", [P, P], F32R)
        mask_f = fixed("mask_f", [P, P])
        mask_r = fixed("mask_r", [P, P], F32R)
        gcol = fixed("gcol", [P, KT])
        bcol = fixed("bcol", [P, 2 * KT])
        pscol = fixed("pscol", [P, PAIRS])
        hT_at = fixed.at
        hT_hi = fixed("hT_hi", [P, KT, SEQ], F32R)
        hT_lo = fixed("hT_lo", [P, KT, SEQ], F32R)
        w_raw = fixed("w_raw", [P, KT, P])
        w_hi = fixed("w_hi", [P, 2, KT, P], F32R)
        w_lo = fixed("w_lo", [P, 2, KT, P], F32R)
        free_at = fixed.at

        stage1(nc, sem, psum, Arena(nc, free_at, end), ident, ident_r, mask_f, mask_r, gcol, bcol, pscol,
               hT_hi, hT_lo, w_raw, w_hi, w_lo, x, norm_gT, w_v, b_gateT, pool_scaleT,
               w_strips[S_U + POOL_ORDER[0]], v_d)
        stage2(nc, sem, psum, Arena(nc, free_at, end), pscol, hT_hi, hT_lo, w_raw, w_hi, w_lo,
               w_strips, pool_w, pool_fix, qk_d, mix_d)
        stage3(nc, sem, psum, Arena(nc, free_at, end), ident, ident_r, mask_r, bcol, hT_hi, hT_lo,
               w_raw, w_hi, w_lo, w_strips, qk_d, v_d, mix_d, yp_d, za_d, at_d, gate_d)
        stage4(nc, sem, psum, Arena(nc, hT_at, end), x, yp_d, za_d, at_d, gate_d, w_pool_up,
               w_attn_up, w_out, final_g, out)


def stage1(nc, sem, psum, sb, ident, ident_r, mask_f, mask_r, gcol, bcol, pscol, hT_hi, hT_lo, w_raw, w_hi,
           w_lo, x, norm_gT, w_v, b_gateT, pool_scaleT, first_strip, v_d):
    wv_hi = sb("wv_hi", [P, KT, AW], F32R)
    wv_lo = sb("wv_lo", [P, KT, AW], F32R)
    xt = sb("xt", [P, 2, D])
    xn = sb("xn", [P, 2, D])
    scaled = sb("scaled", [P, 2, CH])
    v_out = sb("v_out", [P, 2, AW])
    stat = sb("stat", [P, TT, 8])
    WV = KT // 2
    wv_raw = sb("wv_raw", [P, KT, AW])
    strip_in, strip_hi, strip_lo = sem("s1_strip_in"), sem("s1_strip_hi"), sem("s1_strip_lo")

    bias_in = sem("s1_bias_in")
    const_in, ident_done = sem("s1_const_in"), sem("s1_ident_done")
    mask_done, consts_r = sem("s1_mask_done"), sem("s1_consts_r")
    x_in = [sem(f"s1_x_in{i}") for i in range(2)]
    wv_in = [sem(f"s1_wv_in{i}") for i in range(WV)]
    wv_hi_done, wv_lo_done = sem("s1_wv_hi"), sem("s1_wv_lo")
    squared, rooted, normed = sem("s1_squared"), sem("s1_rooted"), sem("s1_normed")
    mean_done = sem("s1_mean")
    transposed, scaled_done = sem("s1_transposed"), sem("s1_scaled")
    hi_done, lo_done = sem("s1_hi"), sem("s1_lo")
    v_done, v_copied = sem("s1_v_done"), sem("s1_v_copied")
    v_stored = [sem(f"s1_v_stored{i}") for i in range(2)]

    with nc.Block() as block:
        @block.sync
        def _(sp):
            def load_x(t):
                if t >= 2:
                    sp.wait_ge(normed, t - 1)
                sp.dma_start(xt[:, t % 2, :], x[t * P:(t + 1) * P, :]).then_inc(x_in[t % 2], DMA)

            load_x(0)
            sp.dma_start(gcol[:, :], norm_gT).then_inc(const_in, DMA)
            for i in range(WV):
                sp.dma_start(wv_raw[:, 2 * i:2 * i + 2, :], w_v[:, 2 * i:2 * i + 2, :]).then_inc(wv_in[i], DMA)
                if i == 1:
                    load_x(1)
            sp.dma_start(bcol[:, :], b_gateT).then_inc(bias_in, DMA)
            sp.dma_start(pscol[:, :], pool_scaleT).then_inc(bias_in, DMA)
            for t in range(2, WV + 1):
                load_x(t)
            sp.dma_start(w_raw[:, :, :], first_strip).then_inc(strip_in, DMA)
            for t in range(WV + 1, TT):
                load_x(t)
                if t >= 5:
                    i = t - 5
                    sp.wait_ge(v_copied, i + 1)
                    sp.dma_start(v_d[i * P:(i + 1) * P, :], v_out[:, i % 2, :]).then_inc(v_stored[i % 2], DMA)
            for i in range(TT - 5, TT):
                sp.wait_ge(v_copied, i + 1)
                sp.dma_start(v_d[i * P:(i + 1) * P, :], v_out[:, i % 2, :]).then_inc(v_stored[i % 2], DMA)
            for s in v_stored:
                sp.wait_ge(s, DMA * TT // 2)
            sp.wait_ge(bias_in, 2 * DMA)

        @block.gpsimd
        def _(pool):
            pool.memset(ident[:, :], 0.0).then_inc(ident_done, 1)
            pool.memset(mask_f[:, :], 0.0).then_inc(mask_done, 1)
            pool.wait_ge(ident_done, 1)
            pool.affine_select(out=ident[:, :], in_=ident[:, :], compare_op=ALU.not_equal, fill=1.0,
                               base=0, pattern=[[-1, P]], channel_multiplier=1).then_inc(ident_done, 1)
            pool.wait_ge(mask_done, 1)
            pool.affine_select(out=mask_f[:, :], in_=mask_f[:, :], compare_op=ALU.is_gt, fill=MASK,
                               base=0, pattern=[[-1, P]], channel_multiplier=1).then_inc(mask_done, 1)
            for t in range(TT):
                for hb in range(2):
                    n = 2 * t + hb
                    pool.wait_ge(hi_done, n + 1)
                    k = slice(4 * hb, 4 * hb + 4)
                    pool.tensor_tensor(hT_lo[:, k, t * P:(t + 1) * P],
                                       scaled[:, hb, :].rearrange("p (k n) -> p k n", k=4),
                                       hT_hi[:, k, t * P:(t + 1) * P].bitcast(F32),
                                       ALU.subtract).then_inc(lo_done, 1)
                if t == TT // 2:
                    pool.wait_ge(strip_hi, 1)
                    pool.tensor_tensor(w_lo[:, 0, :, :], w_raw[:, :, :], w_hi[:, 0, :, :].bitcast(F32),
                                       ALU.subtract).then_inc(strip_lo, 1)

        @block.scalar
        def _(act):
            def part_hi(t):
                for hb in range(2):
                    n = 2 * t + hb
                    act.wait_ge(scaled_done, n + 1)
                    act.activation(hT_hi[:, 4 * hb:4 * hb + 4, t * P:(t + 1) * P],
                                   scaled[:, hb, :].rearrange("p (k n) -> p k n", k=4),
                                   ACT.Copy).then_inc(hi_done, 1)

            for t in range(TT):
                act.wait_ge(x_in[t % 2], DMA * (t // 2 + 1))
                if t >= 2:
                    act.wait_ge(transposed, 2 * (t - 1))
                act.activation(xn[:, t % 2, :], xt[:, t % 2, :], ACT.Square,
                               accum_out=stat[:, t, 0:1]).then_inc(squared, 1)
                if t >= 1:
                    part_hi(t - 1)
                act.wait_ge(mean_done, 2 * t + 2)
                act.activation(stat[:, t, 3:4], stat[:, t, 2:3], ACT.Sqrt).then_inc(rooted, 1)
                if t == 0:
                    for i in range(WV):
                        part = slice(2 * i, 2 * i + 2)
                        act.wait_ge(wv_in[i], DMA)
                        act.activation(wv_hi[:, part, :], wv_raw[:, part, :], ACT.Copy).then_inc(wv_hi_done, 1)
                if t == TT // 2 - 1:
                    act.wait_ge(strip_in, DMA)
                    act.activation(w_hi[:, 0, :, :], w_raw[:, :, :], ACT.Copy).then_inc(strip_hi, 1)
            part_hi(TT - 1)

        @block.vector
        def _(dve):
            dve.wait_ge(ident_done, 2)
            dve.tensor_copy(ident_r[:, :], ident[:, :]).then_inc(consts_r, 1)
            dve.wait_ge(mask_done, 2)
            dve.tensor_copy(mask_r[:, :], mask_f[:, :]).then_inc(consts_r, 1)
            newton = sem("s1_newton")

            def copy_v(i):
                dve.wait_ge(v_done, i + 1)
                if i >= 2:
                    dve.wait_ge(v_stored[i % 2], DMA * (i // 2))
                dve.tensor_copy(v_out[:, i % 2, :], psum[:, 4 + i % 2, :]).then_inc(v_copied, 1)

            def scale_rows(t):
                for hb in range(2):
                    n = 2 * t + hb
                    dve.wait_ge(transposed, n + 1)
                    if t >= 1:
                        dve.wait_ge(lo_done, n - 1)
                    k = slice(4 * hb, 4 * hb + 4)
                    dve.tensor_tensor(scaled[:, hb, :].rearrange("p (k n) -> p k n", k=4),
                                      psum[:, 2 * (t % 2) + hb, :].rearrange("p (k n) -> p k n", k=4),
                                      gcol[:, k].unsqueeze(2).broadcast_to([P, 4, P]),
                                      ALU.mult).then_inc(scaled_done, 1)

            dve.wait_ge(const_in, DMA)
            for t in range(TT):
                dve.wait_ge(squared, t + 1)
                dve.tensor_scalar(stat[:, t, 1:2], stat[:, t, 0:1], 1.0 / D, EPS, ALU.mult,
                                  ALU.add).then_inc(mean_done, 1)
                dve.wait_ge(mean_done, 2 * t + 1)
                dve.reciprocal(stat[:, t, 2:3], stat[:, t, 1:2]).then_inc(mean_done, 1)
                if t >= 1:
                    scale_rows(t - 1)
                dve.wait_ge(rooted, t + 1)
                dve.tensor_scalar(stat[:, t, 4:5], stat[:, t, 3:4], stat[:, t, 3:4], stat[:, t, 1:2],
                                  ALU.mult, ALU.mult).then_inc(newton, 1)
                dve.wait_ge(newton, 2 * t + 1)
                dve.tensor_scalar(stat[:, t, 5:6], stat[:, t, 4:5], -0.5, 1.5, ALU.mult,
                                  ALU.add).then_inc(newton, 1)
                dve.wait_ge(newton, 2 * t + 2)
                dve.tensor_scalar(xn[:, t % 2, :], xt[:, t % 2, :], stat[:, t, 3:4], stat[:, t, 5:6],
                                  ALU.mult, ALU.mult).then_inc(normed, 1)
                if t == 0:
                    for i in range(WV):
                        part = slice(2 * i, 2 * i + 2)
                        dve.wait_ge(wv_hi_done, i + 1)
                        dve.tensor_tensor(wv_lo[:, part, :], wv_raw[:, part, :], wv_hi[:, part, :].bitcast(F32),
                                          ALU.subtract).then_inc(wv_lo_done, 1)
                if t >= 4:
                    copy_v(t - 4)
            scale_rows(TT - 1)
            for i in range(TT - 4, TT):
                copy_v(i)

        @block.tensor
        def _(pe):
            def transpose_tile(t):
                pe.wait_ge(normed, t + 1)
                for hb in range(2):
                    if t >= 2:
                        pe.wait_ge(scaled_done, 2 * (t - 2) + hb + 1)
                    for k in range(4):
                        last = pe.transpose(psum[:, 2 * (t % 2) + hb, k * P:(k + 1) * P],
                                            xn[:, t % 2, (4 * hb + k) * P:(4 * hb + k + 1) * P], ident[:, :])
                    last.then_inc(transposed, 1)

            def project_v(t):
                pe.wait_ge(lo_done, 2 * t + 2)
                if t == 0:
                    pe.wait_ge(wv_lo_done, WV)
                if t >= 2:
                    pe.wait_ge(v_copied, t - 1)
                tok = slice(t * P, (t + 1) * P)
                for k in range(KT):
                    last = split3(pe, psum[:, 4 + t % 2, :], hT_hi[:, k, tok], hT_lo[:, k, tok],
                                  wv_hi[:, k, :], wv_lo[:, k, :], k == 0, k == KT - 1)
                last.then_inc(v_done, 1)

            pe.wait_ge(ident_done, 2)
            pe.wait_ge(consts_r, 2)
            for t in range(2):
                transpose_tile(t)
            for t in range(TT):
                if t + 2 < TT:
                    transpose_tile(t + 2)
                project_v(t)


def stage2(nc, sem, psum, sb, pscol, hT_hi, hT_lo, w_raw, w_hi, w_lo, w_strips, pool_w, pool_fix,
           qk_d, mix_d):
    G = len(WINDOWS)
    W = PAD + SEQ
    us = [sb(f"u{i}", [P, W]) for i in range(2)]
    sums = [sb(f"sums{i}", [P, W]) for i in range(2)]
    pooled = sb("pooled", [P, SEQ])
    pl_hi = sb("pl_hi", [P, SEQ], F32R)
    pl_lo = sb("pl_lo", [P, SEQ], F32R)
    pw = sb("pw", [P, G, P])
    pw_hi = sb("pw_hi", [P, G, P], F32R)
    pw_lo = sb("pw_lo", [P, G, P], F32R)
    fix = sb("fix", [P, G, PAD])
    store = sb("store", [P, 2, CH])
    order = POOL_ORDER
    UM, QM = G, 2 * PAIRS

    raw_in, hi_done, lo_done = sem("s2_w_in"), sem("s2_w_hi"), sem("s2_w_lo")
    proj_done, copied = sem("s2_proj_done"), sem("s2_copied")
    mixed = sem("s2_mixed")
    staged = sem("s2_staged")
    stored = [sem(f"s2_stored{i}") for i in range(2)]
    pw_in, pw_hi_done, pw_lo_done = sem("s2_pw_in"), sem("s2_pw_hi"), sem("s2_pw_lo")
    zeroed, level, pool_hi, pool_lo = sem("s2_zeroed"), sem("s2_level"), sem("s2_pool_hi"), sem("s2_pool_lo")
    levels = {g: WINDOWS[g].bit_length() - 1 for g in range(G)}
    first_level = {}
    at = 0
    for g in order:
        first_level[g] = at
        at += levels[g] + 2

    def use_of_mix(m, c):
        return 4 * m + c if m < G - 1 else 4 * (G - 1) + 4 + c

    def use_of_strip(j, c):
        return 4 * (G - 1) + c if isinstance(j, int) and j == 0 else j * 4 + 4 * G + c

    with nc.Block() as block:
        @block.sync
        def _(sp):
            def load(strip, n):
                sp.wait_ge(lo_done, n) if not isinstance(n, int) or n > 0 else None
                sp.dma_start(w_raw[:, :, :], w_strips[strip]).then_inc(raw_in, DMA)

            def put(dst, use, slot):
                sp.wait_ge(staged, use + 1)
                sp.dma_start(dst, store[:, slot, :]).then_inc(stored[slot], DMA)

            sp.sem_inc(raw_in, DMA)
            sp.dma_start(pw[:, :, :], pool_w.rearrange("g c d -> c g d")).then_inc(pw_in, DMA)
            sp.dma_start(fix[:, :, :], pool_fix).then_inc(pw_in, DMA)
            for j in range(1, UM):
                load(S_U + order[j], j)
                if j >= 2:
                    for c in range(NC):
                        put(mix_d[order[j - 2], :, c * CH:(c + 1) * CH], use_of_mix(j - 2, c), c % 2)
            load(S_Q, UM)
            load(S_Q + 1, UM + 1)
            for c in range(NC):
                put(mix_d[order[2], :, c * CH:(c + 1) * CH], use_of_mix(2, c), c % 2)
            load(S_Q + 2, UM + 2)
            for c in range(NC):
                put(qk_d[0, :, c * CH:(c + 1) * CH], use_of_strip(0, c), c % 2)
            for c in range(NC):
                put(mix_d[order[3], :, c * CH:(c + 1) * CH], use_of_mix(3, c), c % 2)
            load(S_Q + 3, UM + 3)
            for c in range(NC):
                put(qk_d[1, :, c * CH:(c + 1) * CH], use_of_strip(1, c), c % 2)
            with sp.Fori(1, QM // 2 - 1) as p:
                for r in range(2):
                    load(p * 2 + (S_Q + 2 + r), p * 2 + (UM + 2 + r))
                    for c in range(NC):
                        put(qk_d[p * 2 + r, :, c * CH:(c + 1) * CH], use_of_strip(p * 2 + r, c), c % 2)
            load(S_ZP, UM + QM)
            for j in (QM - 2, QM - 1):
                for c in range(NC):
                    put(qk_d[j, :, c * CH:(c + 1) * CH], use_of_strip(j, c), c % 2)
            for s in stored:
                sp.wait_ge(s, DMA * (4 * (UM + QM)) // 2)

        def scalar_weights(act, n, slot):
            act.wait_ge(raw_in, n * DMA + DMA)
            if not isinstance(n, int) or n >= 2:
                act.wait_ge(proj_done, n * 4 - 4)
            act.activation(w_hi[:, slot, :, :], w_raw[:, :, :], ACT.Copy).then_inc(hi_done, 1)

        @block.scalar
        def _(act):
            def take_staging(use, slot):
                if not isinstance(use, int) or use >= 2:
                    act.wait_ge(stored[slot], (use - slot) * (DMA // 2))

            def copy_u(j):
                for c in range(NC):
                    act.wait_ge(proj_done, 4 * j + c + 1)
                    if j >= 2 and c == 0:
                        act.wait_ge(level, first_level[order[j - 2]] + levels[order[j - 2]] + 2)
                    act.activation(us[j % 2][:, PAD + c * CH:PAD + (c + 1) * CH], psum[:, c % 2, :],
                                   ACT.Copy).then_inc(copied, 1)

            def split_pooled(j):
                act.wait_ge(level, first_level[order[j]] + levels[order[j]] + 2)
                if j >= 1:
                    act.wait_ge(mixed, 4 * j)
                act.activation(pl_hi[:, :], pooled[:, :], ACT.Copy).then_inc(pool_hi, 1)

            def scale_mix(j):
                for c in range(NC):
                    use = use_of_mix(j, c)
                    act.wait_ge(mixed, 4 * j + c + 1)
                    take_staging(use, c % 2)
                    act.activation(store[:, c % 2, :], psum[:, 2 + c % 2, :], ACT.Copy,
                                   scale=pscol[:, order[j]:order[j] + 1]).then_inc(staged, 1)

            def copy_strip(j, c):
                act.wait_ge(proj_done, j * 4 + (4 * UM + c + 1))
                take_staging(use_of_strip(j, c), c % 2)
                act.activation(store[:, c % 2, :], psum[:, c % 2, :], ACT.Copy).then_inc(staged, 1)

            act.sem_inc(hi_done, 1)
            act.wait_ge(pw_in, 2 * DMA)
            act.activation(pw_hi[:, :, :], pw[:, :, :], ACT.Copy).then_inc(pw_hi_done, 1)
            scalar_weights(act, 1, 1)
            for j in range(UM):
                copy_u(j)
                if j >= 1:
                    scale_mix(j - 1)
                scalar_weights(act, j + 2, j % 2)
                split_pooled(j)
            for c in range(NC):
                copy_strip(0, c)
            scale_mix(UM - 1)
            scalar_weights(act, UM + 2, 0)
            for c in range(NC):
                copy_strip(1, c)
            scalar_weights(act, UM + 3, 1)
            with act.Fori(1, QM // 2 - 1) as p:
                for r in range(2):
                    for c in range(NC):
                        copy_strip(p * 2 + r, c)
                    scalar_weights(act, p * 2 + (UM + 2 + r), r)
            for c in range(NC):
                copy_strip(QM - 2, c)
            scalar_weights(act, UM + QM, 0)
            for c in range(NC):
                copy_strip(QM - 1, c)

        @block.gpsimd
        def _(pool):
            def weights_lo(n, slot):
                pool.wait_ge(hi_done, n + 1)
                pool.tensor_tensor(w_lo[:, slot, :, :], w_raw[:, :, :], w_hi[:, slot, :, :].bitcast(F32),
                                   ALU.subtract).then_inc(lo_done, 1)

            for t in (*us, *sums):
                pool.memset(t[:, 0:PAD], 0.0).then_inc(zeroed, 1)
            pool.sem_inc(lo_done, 1)
            pool.wait_ge(pw_hi_done, 1)
            pool.tensor_tensor(pw_lo[:, :, :], pw[:, :, :], pw_hi[:, :, :].bitcast(F32),
                               ALU.subtract).then_inc(pw_lo_done, 1)
            weights_lo(1, 1)
            for n in range(2, 4):
                weights_lo(n, n % 2)
            with pool.Fori(2, (UM + QM) // 2) as p:
                for r in range(2):
                    weights_lo(p * 2 + r, r)
            weights_lo(UM + QM, 0)

        @block.vector
        def _(dve):
            dve.wait_ge(zeroed, 4)
            dve.wait_ge(pw_in, 2 * DMA)
            for j in range(UM):
                g = order[j]
                n = first_level[g]
                dve.wait_ge(copied, 4 * (j + 1))
                u = us[j % 2]
                src = u
                for i in range(levels[g]):
                    if i >= 1:
                        dve.wait_ge(level, n)
                    dst = sums[i % 2]
                    dve.tensor_tensor(dst[:, PAD:W], src[:, PAD:W], src[:, PAD - (1 << i):W - (1 << i)],
                                      ALU.add).then_inc(level, 1)
                    n += 1
                    src = dst
                dve.wait_ge(level, n)
                dve.tensor_tensor(src[:, PAD:2 * PAD], src[:, PAD:2 * PAD], fix[:, g, :],
                                  ALU.mult).then_inc(level, 1)
                dve.wait_ge(level, n + 1)
                if j >= 1:
                    dve.wait_ge(pool_lo, j)
                dve.scalar_tensor_tensor(pooled[:, :], src[:, PAD:W], 1.0 / WINDOWS[g], u[:, PAD:W],
                                         ALU.mult, ALU.subtract).then_inc(level, 1)
                dve.wait_ge(pool_hi, j + 1)
                dve.tensor_tensor(pl_lo[:, :], pooled[:, :], pl_hi[:, :].bitcast(F32),
                                  ALU.subtract).then_inc(pool_lo, 1)

        @block.tensor
        def _(pe):
            def strip(n, slot, free):
                pe.wait_ge(lo_done, n + 1)
                for c in range(NC):
                    free(c)
                    tok = slice(c * CH, (c + 1) * CH)
                    for k in range(KT):
                        last = split3(pe, psum[:, c % 2, :], w_hi[:, slot, k, :], w_lo[:, slot, k, :],
                                      hT_hi[:, k, tok], hT_lo[:, k, tok], k == 0, k == KT - 1)
                    last.then_inc(proj_done, 1)

            def mix(j):
                pe.wait_ge(pool_lo, j + 1)
                for c in range(NC):
                    tok = slice(c * CH, (c + 1) * CH)
                    use = use_of_mix(j, c)
                    if 4 * j + c >= 2:
                        back = use - 2 if c >= 2 else use_of_mix(j - 1, c + 2)
                        pe.wait_ge(staged, back + 1)
                    g = order[j]
                    last = split3(pe, psum[:, 2 + c % 2, :], pw_hi[:, g, :], pw_lo[:, g, :],
                                  pl_hi[:, tok], pl_lo[:, tok], True, True)
                    last.then_inc(mixed, 1)

            def free_u(j):
                def wait(c):
                    if 4 * j + c >= 2:
                        pe.wait_ge(copied, 4 * j + c - 1)
                return wait

            def free_strip(j):
                def wait(c):
                    if isinstance(j, int) and j == 0 and c < 2:
                        pe.wait_ge(copied, 4 * UM - 1 + c)
                    elif isinstance(j, int) and j == 1 and c < 2:
                        pe.wait_ge(staged, use_of_strip(0, c + 2) + 1)
                    elif c < 2:
                        pe.wait_ge(staged, j * 4 + (4 * G + c - 1))
                    else:
                        pe.wait_ge(staged, use_of_strip(j, c - 2) + 1)
                return wait

            for j in range(UM):
                if j == 1:
                    pe.wait_ge(pw_lo_done, 1)
                strip(j, j % 2, free_u(j))
                if j >= 1:
                    mix(j - 1)
            strip(UM, 0, free_strip(0))
            mix(UM - 1)
            strip(UM + 1, 1, free_strip(1))
            with pe.Fori(1, QM // 2) as p:
                for r in range(2):
                    strip(p * 2 + (UM + r), r, free_strip(p * 2 + r))


def attention_items():
    return [(e, i, c, (i % 4 + 1) * P if c == i // 4 else CH, c == i // 4, c == 0)
            for e in range(2) for i in reversed(range(TT)) for c in reversed(range(i // 4 + 1))]


def stage3(nc, sem, psum, sb, ident, ident_r, mask_r, bcol, hT_hi, hT_lo, w_raw, w_hi, w_lo, w_strips,
           qk_d, v_d, mix_d, yp_d, za_d, at_d, gate_d):
    ITEMS = attention_items()
    NI = len(ITEMS)
    T_LAG, AV_LAG = 2, 3
    LOAD = 4
    STRIPS = 6
    GROUPS = STRIPS * NC
    MM = 3 * KT
    ROWS = 2 * TT
    AHEAD = 2
    ROW_OF = {}
    for n, it in enumerate(ITEMS):
        if it[5]:
            ROW_OF[n] = len(ROW_OF)
    row_at = [sum(1 for m in ROW_OF if m < n) for n in range(NI)]

    cost = [450.0 + 3.1 * it[3] for it in ITEMS]
    due = [round(sum(cost[:s + 1]) / sum(cost) * GROUPS * MM) for s in range(NI)]
    fin = [next(s for s in range(NI) if due[s] >= (k + 1) * MM) for k in range(GROUPS)]

    def first_item(test):
        return next(n for n, it in enumerate(ITEMS) if test(it))

    def last_item(test):
        return max(n for n, it in enumerate(ITEMS) if test(it))

    kv_units = [(e, c, last_item(lambda it: it[0] == 1 - e and it[2] == c) - (NI if e == 0 else 0))
                for e in range(2) for c in reversed(range(NC))]
    k_step = [before + 1 for _e, _c, before in kv_units]
    v_step = [before + AV_LAG + 1 for _e, _c, before in kv_units]
    QN = 4
    q_units = [(e, r) for e in range(2) for r in reversed(range(TT // 2))]

    def q_last(u):
        e, r = q_units[u % len(q_units)]
        return last_item(lambda it: it[0] == e and it[1] // 2 == r) - (0 if u >= 0 else NI)

    q_before = [q_last(u - QN) for u in range(len(q_units))]
    q_step = [max(q_before[u] + 1, first_item(lambda it: it[0] == e and it[1] // 2 == r) - 4)
              for u, (e, r) in enumerate(q_units)]
    w_step = [fin[(NC * (j - 2) + NC - 1) % GROUPS] + 1 - (NI if j < 2 else 0) for j in range(STRIPS)]
    BIAS_STEP = 6

    km = sb("km", [P, SEQ], F32R)
    vm = sb("vm", [P, TT, 2 * HD], F32R)
    qm_hi = sb("qm_hi", [P, QN, 2 * P], F32R)
    qm_lo = sb("qm_lo", [P, QN, 2 * P], F32R)
    k_raw = sb("k_raw", [P, 2, CH])
    v_raw = sb("v_raw", [P, 2, 4, HD])
    q_raw = sb("q_raw", [P, 2, 2 * P])
    keep = sb("keep", [P, 2, CH + 1])
    beta = sb("beta", [P, 4, CH])
    left = sb("left", [P, 2, CH + 1])
    wt = sb("wt", [P, 2, 4, 2, P], F32R)
    half_sum = sb("half_sum", [P, 2 * P])
    row_sum = sb("row_sum", [P, 2 * P])
    y_out = sb("y_out", [P, 2, CH])
    mix_t = sb("mix_t", [P, CH])
    res = sb("res", [P, 2, CH])
    bias = sb("bias", [P, 4])

    w_in, w_hi_done, w_lo_done = sem("s3_w_in"), sem("s3_w_hi"), sem("s3_w_lo")
    k_in = [sem(f"s3_k_in{i}") for i in range(2)]
    v_in = [sem(f"s3_v_in{i}") for i in range(2)]
    q_in = [sem(f"s3_q_in{i}") for i in range(2)]
    k_hi, v_hi, q_hi = sem("s3_k_hi"), sem("s3_v_hi"), sem("s3_q_hi")
    k_lo, v_lo, q_lo = sem("s3_k_lo"), sem("s3_v_lo"), sem("s3_q_lo")
    scored, turned, weighed = sem("s3_scored"), sem("s3_turned"), sem("s3_weighed")
    keep_done, beta_done = sem("s3_keep"), sem("s3_beta")
    scanned, weights = sem("s3_scanned"), sem("s3_weights")
    wt_hi_done, wt_lo_done = sem("s3_wt_hi"), sem("s3_wt_lo")
    half_done, row_done, y_done = sem("s3_half"), sem("s3_row"), sem("s3_y")
    proj_done, act_out, silu_done, yp_done = sem("s3_proj"), sem("s3_act_out"), sem("s3_silu"), sem("s3_yp")
    mix_in = sem("s3_mix_in")
    res_stored = [sem(f"s3_res_stored{i}") for i in range(2)]
    y_stored = [sem(f"s3_y_stored{i}") for i in range(2)]
    ones, sp_tick, bias_done = sem("s3_ones"), sem("s3_sp_tick"), sem("s3_bias")
    NK, NQ = len(kv_units), len(q_units)

    def event(pair, per, n):
        p, o = pair
        return p * per + (o * per + n + 1)

    def wait(eng, s, value, unit=1):
        if not isinstance(value, int) or value > 0:
            eng.wait_ge(s, value * unit)

    def turns(eng, walk):
        walk(0, range(-NI, 0), False, False, True)
        walk(0, range(NI), False, True, True)
        with eng.Fori(1, PAIRS - 1) as p:
            walk(p, range(NI), True, True, True)
        walk(PAIRS - 1, range(NI), True, True, False)
        walk(PAIRS, range(10), True, False, False)

    def placed(p, s, prev, own, nxt):
        def here(step):
            if s < 0:
                return (p, 0) if step == s else None
            for there, offset in ((own, 0), (prev, -1), (nxt, 1)):
                if there and step == s - offset * NI:
                    return (p, offset)
            return None
        return here

    def bank_s(n):
        return psum[:, 2 + n % 2, :]

    def bank_t(n):
        return psum[:, 4 + n % 2, :]

    def bank_o(row):
        return psum[:, 6 + row % 2, 0:2 * P]

    with nc.Block() as block:
        @block.sync
        def _(sp):
            def hold(s, value):
                if not isinstance(value, int) or value > 0:
                    sp.wait_ge(s, value)
                    sp.sem_inc(sp_tick, 1)

            def load_k(pair, u):
                e, c, _before = kv_units[u]
                hold(k_lo, event(pair, NK, u - 2))
                for h in range(2):
                    sp.dma_start(k_raw[h * HD:(h + 1) * HD, u % 2, :],
                                 qk_d[pair[0] + (pair[1] + PAIRS), e * HD:(e + 1) * HD, c * CH:(c + 1) * CH]
                                 ).then_inc(k_in[u % 2], DMA)

            def load_v(pair, u):
                e, c, _before = kv_units[u]
                hold(v_lo, event(pair, NK, u - 2))
                cols = bass.ds(pair[0] * P + (pair[1] * P + e * HD), HD)
                sp.dma_start(v_raw[:, u % 2, :, :], v_d[c * CH:(c + 1) * CH, cols].rearrange("(a q) d -> q a d", q=P)
                             ).then_inc(v_in[u % 2], DMA)

            def load_q(pair, u):
                e, r = q_units[u]
                hold(q_lo, event(pair, NQ, u - 2))
                for h in range(2):
                    sp.dma_start(q_raw[h * HD:(h + 1) * HD, u % 2, :],
                                 qk_d[pair[0] + pair[1], e * HD:(e + 1) * HD, r * 2 * P:(r + 1) * 2 * P]
                                 ).then_inc(q_in[u % 2], DMA)

            def load_w(pair, j):
                hold(w_lo_done, event(pair, STRIPS, j - 1))
                p, o = pair
                strip = p + (o + (S_ZP, S_ZA)[j]) if j < 2 else p * 4 + (o * 4 + S_G + j - 2)
                sp.dma_start(w_raw[:, :, :], w_strips[strip]).then_inc(w_in, DMA)

            def load_mix(pair, c):
                hold(yp_done, event(pair, NC, c - 1))
                sp.dma_start(mix_t[:, :], mix_d[pair[0] + pair[1], :, c * CH:(c + 1) * CH]).then_inc(mix_in, DMA)

            def store_result(pair, k):
                p, o = pair
                j, c = divmod(k, NC)
                cols = slice(c * CH, (c + 1) * CH)
                if j == 0:
                    hold(yp_done, event(pair, NC, k))
                    dst = yp_d[p + o, :, cols]
                elif j == 1:
                    hold(silu_done, event(pair, 2 * NC, k))
                    dst = za_d[p + o, :, cols]
                else:
                    hold(act_out, event(pair, GROUPS, k))
                    dst = gate_d[p * 4 + (o * 4 + j - 2), :, cols]
                sp.dma_start(dst, res[:, k % 2, :]).then_inc(res_stored[k % 2], DMA)

            def store_y(pair, n):
                e, i = ITEMS[n][0:2]
                u = ROW_OF[n] // 4
                hold(y_done, event(pair, ROWS, ROW_OF[n]))
                sp.dma_start(at_d[pair[0] + pair[1], e * HD:(e + 1) * HD, i * P:i * P + CH],
                             y_out[e * HD:(e + 1) * HD, u % 2, :]).then_inc(y_stored[u % 2], DMA)

            def walk(p, steps, prev, own, nxt):
                for s in steps:
                    here = placed(p, s, prev, own, nxt)
                    for u in range(NK):
                        if pair := here(k_step[u] - LOAD):
                            load_k(pair, u)
                        if pair := here(v_step[u] - LOAD):
                            load_v(pair, u)
                    for u in range(NQ):
                        if pair := here(q_step[u] - LOAD):
                            load_q(pair, u)
                    for j in range(STRIPS):
                        if pair := here(w_step[j] - LOAD):
                            if not (s < 0 and j == 0):
                                load_w(pair, j)
                    for c in range(NC):
                        if pair := here(fin[c] + 1 - LOAD):
                            load_mix(pair, c)
                    for k in range(GROUPS):
                        if pair := here(fin[k] + 2):
                            store_result(pair, k)
                    for n in ROW_OF:
                        if ITEMS[n][1] % 4 == 0:
                            if pair := here(n + AV_LAG + 2):
                                store_y(pair, n)

            sp.sem_inc(w_in, DMA)
            turns(sp, walk)
            for i in range(2):
                sp.wait_ge(res_stored[i], PAIRS * GROUPS // 2 * DMA)
                sp.wait_ge(y_stored[i], PAIRS * 4 * DMA)

        @block.tensor
        def _(pe):
            def projections(p):
                for j in range(STRIPS):
                    pe.wait_ge(w_lo_done, event((p, 0), STRIPS, j))
                    for c in range(NC):
                        k = j * NC + c
                        if 2 <= k < 2 * NC + 2:
                            pe.wait_ge(silu_done, event((p, 0), 2 * NC, k - 2))
                        else:
                            wait(pe, act_out, event((p, 0), GROUPS, k - 2))
                        tok = slice(c * CH, (c + 1) * CH)
                        for kt in range(KT):
                            hi, lo = w_hi[:, j % 2, kt, :], w_lo[:, j % 2, kt, :]
                            o = psum[:, k % 2, :]
                            pe.matmul(o, hi, hT_hi[:, kt, tok], start=kt == 0, stop=False)
                            yield
                            pe.matmul(o, hi, hT_lo[:, kt, tok], start=False, stop=False)
                            yield
                            last = pe.matmul(o, lo, hT_hi[:, kt, tok], start=False, stop=kt == KT - 1)
                            if kt == KT - 1:
                                last.then_inc(proj_done, 1)
                            yield

            def score(pair, n):
                e, i, c, w, first, _l = ITEMS[n]
                wait(pe, beta_done, event(pair, NI, n - 2))
                pe.wait_ge(k_lo, event(pair, NK, NC * e + NC - 1 - c))
                u = TT // 2 * (e + 1) - 1 - i // 2
                pe.wait_ge(q_lo, event(pair, NQ, u))
                cols = slice(i % 2 * P, i % 2 * P + P)
                o = bank_s(n)
                keys = slice(c * CH, c * CH + w)
                pe.matmul(o[:, 0:w], qm_hi[:, u % QN, cols], km[:, keys], start=True, stop=False)
                last = pe.matmul(o[:, 0:w], qm_lo[:, u % QN, cols], km[:, keys], start=False, stop=not first)
                if first:
                    last = pe.matmul(o[:, w - P:w], ident_r[:, :], mask_r[:, :], start=False, stop=True)
                last.then_inc(scored, 1)

            def turn(pair, n):
                w = ITEMS[n][3]
                pe.wait_ge(weights, event(pair, NI, n))
                wait(pe, wt_lo_done, event(pair, NI, n - 2))
                for j in range(w // P):
                    a = CH - w + j * P
                    last = pe.transpose(bank_t(n)[:, j * P:(j + 1) * P], beta[:, n % 4, a:a + P], ident[:, :])
                last.then_inc(turned, 1)

            def weigh(pair, n):
                e, i, c, w, first, final = ITEMS[n]
                row = row_at[n]
                pe.wait_ge(wt_lo_done, event(pair, NI, n))
                pe.wait_ge(v_lo, event(pair, NK, NC * e + NC - 1 - c))
                if first:
                    wait(pe, row_done, event(pair, ROWS, row - 2))
                for j in range(w // P):
                    last = pe.matmul(bank_o(row), vm[:, NC * c + j, :],
                                     wt[:, n % 2, j, :, :].rearrange("p a q -> p (a q)"),
                                     start=first and j == 0, stop=final and j == w // P - 1)
                last.then_inc(weighed, 1)

            def walk(p, steps, prev, own, nxt):
                proj, done = projections(p), 0
                if own and not prev:
                    for done in range(1, AHEAD * MM + 1):
                        next(proj)
                for s in steps:
                    here = placed(p, s, prev, own, nxt)
                    half = (due[s - 1] if s > 0 else 0) + due[s] if own else 0
                    for n in range(NI):
                        if pair := here(n):
                            score(pair, n)
                    while own and 2 * done < half:
                        next(proj)
                        done += 1
                    for n in range(NI):
                        if pair := here(n + T_LAG):
                            turn(pair, n)
                    while own and done < due[s]:
                        next(proj)
                        done += 1
                    for n in range(NI):
                        if pair := here(n + AV_LAG):
                            weigh(pair, n)

            turns(pe, walk)

        @block.scalar
        def _(act):
            def split_k(pair, u):
                _e, c, before = kv_units[u]
                act.wait_ge(k_in[u % 2], event(pair, NK // 2, u // 2) * (2 * DMA))
                wait(act, scored, event(pair, NI, before))
                act.activation(km[:, c * CH:(c + 1) * CH], k_raw[:, u % 2, :], ACT.Copy).then_inc(k_hi, 1)

            def split_v(pair, u):
                _e, c, before = kv_units[u]
                act.wait_ge(v_in[u % 2], event(pair, NK // 2, u // 2) * DMA)
                wait(act, weighed, event(pair, NI, before))
                act.activation(vm[:, 4 * c:4 * c + 4, 0:HD], v_raw[:, u % 2, :, :], ACT.Copy).then_inc(v_hi, 1)

            def split_q(pair, u):
                act.wait_ge(q_in[u % 2], event(pair, NQ // 2, u // 2) * (2 * DMA))
                wait(act, scored, event(pair, NI, q_before[u]))
                act.activation(qm_hi[:, u % QN, :], q_raw[:, u % 2, :], ACT.Copy).then_inc(q_hi, 1)

            def split_w(pair, j):
                act.wait_ge(w_in, event(pair, STRIPS, j) * DMA)
                wait(act, proj_done, event(pair, GROUPS, NC * (j - 2) + NC - 1))
                act.activation(w_hi[:, j % 2, :, :], w_raw[:, :, :], ACT.Copy).then_inc(w_hi_done, 1)

            def sigmoids(pair, n):
                w = ITEMS[n][3]
                act.wait_ge(scored, event(pair, NI, n))
                wait(act, scanned, event(pair, NI, n - 2))
                act.activation(keep[:, n % 2, CH - w:CH], bank_s(n)[:, 0:w], ACT.Sigmoid,
                               scale=-SCALE).then_inc(keep_done, 1)
                wait(act, turned, event(pair, NI, n - 4))
                act.activation(beta[:, n % 4, CH - w:CH], bank_s(n)[:, 0:w], ACT.Sigmoid,
                               scale=SCALE).then_inc(beta_done, 1)

            def high_part(pair, n):
                w = ITEMS[n][3]
                act.wait_ge(turned, event(pair, NI, n))
                wait(act, weighed, event(pair, NI, n - 2))
                act.activation(wt[:, n % 2, 0:w // P, 0, :], bank_t(n)[:, 0:w].rearrange("p (j q) -> p j q", q=P),
                               ACT.Copy).then_inc(wt_hi_done, 1)

            def other_half(pair, n):
                e, row = ITEMS[n][0], ROW_OF[n]
                mine, other = slice(e * HD, e * HD + HD), slice(HD - e * HD, 2 * HD - e * HD)
                act.wait_ge(weighed, event(pair, NI, n))
                wait(act, row_done, event(pair, ROWS, row - 1))
                act.activation(half_sum[mine, :], bank_o(row)[other, :], ACT.Copy).then_inc(half_done, 1)

            def result(pair, k):
                act.wait_ge(proj_done, event(pair, GROUPS, k))
                wait(act, res_stored[k % 2], event(pair, GROUPS // 2, k // 2 - 1), DMA)
                if k < 2 * NC:
                    act.activation(res[:, k % 2, :], psum[:, k % 2, :], ACT.Sigmoid).then_inc(act_out, 1)
                else:
                    b = k // NC - 2
                    act.wait_ge(bias_done, event(pair, 1, 0))
                    act.activation(res[:, k % 2, :], psum[:, k % 2, :], ACT.Sigmoid,
                                   bias=bias[:, b:b + 1]).then_inc(act_out, 1)

            def fetch_bias(pair):
                wait(act, act_out, event(pair, GROUPS, -1))
                act.sem_inc(bias_tick, 1)
                act.activation(bias[:, :], bcol[:, bass.ds(pair[0] * 4 + pair[1] * 4, 4)],
                               ACT.Copy).then_inc(bias_done, 1)

            def walk(p, steps, prev, own, nxt):
                for s in steps:
                    here = placed(p, s, prev, own, nxt)
                    for u in range(NK):
                        if pair := here(k_step[u]):
                            split_k(pair, u)
                        if pair := here(v_step[u]):
                            split_v(pair, u)
                    for u in range(NQ):
                        if pair := here(q_step[u]):
                            split_q(pair, u)
                    for j in range(STRIPS):
                        if pair := here(w_step[j]):
                            if not (s < 0 and j == 0):
                                split_w(pair, j)
                    if pair := here(BIAS_STEP):
                        fetch_bias(pair)
                    for n in range(NI):
                        if pair := here(n):
                            sigmoids(pair, n)
                    for n in range(NI):
                        if pair := here(n + T_LAG):
                            high_part(pair, n)
                    for n in ROW_OF:
                        if pair := here(n + AV_LAG + 1):
                            other_half(pair, n)
                    for k in range(GROUPS):
                        if pair := here(fin[k] + 1):
                            result(pair, k)

            bias_tick = sem("s3_bias_tick")
            act.sem_inc(w_hi_done, 1)
            turns(act, walk)

        @block.vector
        def _(dve):
            def scan(pair, n):
                w, first = ITEMS[n][3:5]
                span = slice(CH - w, CH + 1)
                if first:
                    carry = 1.0
                else:
                    dve.wait_ge(scanned, event(pair, NI, n - 1))
                    a = CH - ITEMS[n - 1][3]
                    carry = left[:, (n - 1) % 2, a:a + 1]
                dve.wait_ge(keep_done, event(pair, NI, n))
                k = keep[:, n % 2, span][:, ::-1]
                dve.tensor_tensor_scan(left[:, n % 2, span][:, ::-1], k, k, carry,
                                       ALU.mult, ALU.bypass).then_inc(scanned, 1)

            def weight(pair, n):
                w = ITEMS[n][3]
                dve.wait_ge(beta_done, event(pair, NI, n))
                dve.wait_ge(scanned, event(pair, NI, n))
                dve.tensor_tensor(beta[:, n % 4, CH - w:CH], beta[:, n % 4, CH - w:CH],
                                  left[:, n % 2, CH - w + 1:CH + 1], ALU.mult).then_inc(weights, 1)

            def low_part(pair, n):
                w = ITEMS[n][3]
                dve.wait_ge(wt_hi_done, event(pair, NI, n))
                dve.tensor_tensor(wt[:, n % 2, 0:w // P, 1, :],
                                  bank_t(n)[:, 0:w].rearrange("p (j q) -> p j q", q=P),
                                  wt[:, n % 2, 0:w // P, 0, :].bitcast(F32), ALU.subtract).then_inc(wt_lo_done, 1)

            def add_halves(pair, n):
                e, row = ITEMS[n][0], ROW_OF[n]
                mine = slice(e * HD, e * HD + HD)
                dve.wait_ge(half_done, event(pair, ROWS, row))
                wait(dve, y_done, event(pair, ROWS, row - 1))
                dve.tensor_tensor(row_sum[mine, :], bank_o(row)[mine, :], half_sum[mine, :],
                                  ALU.add).then_inc(row_done, 1)

            def silu(pair, k):
                dve.wait_ge(act_out, event(pair, GROUPS, k))
                dve.tensor_tensor(res[:, k % 2, :], psum[:, k % 2, :], res[:, k % 2, :],
                                  ALU.mult).then_inc(silu_done, 1)

            def walk(p, steps, prev, own, nxt):
                for s in steps:
                    here = placed(p, s, prev, own, nxt)
                    for n in range(NI):
                        if pair := here(n + T_LAG + 1):
                            low_part(pair, n)
                    for n in range(NI):
                        if pair := here(n):
                            scan(pair, n)
                    for n in range(NI):
                        if pair := here(n):
                            weight(pair, n)
                    for n in ROW_OF:
                        if pair := here(n + AV_LAG + 1):
                            add_halves(pair, n)
                    for k in range(2 * NC):
                        if pair := here(fin[k] + 1):
                            silu(pair, k)

            dve.wait_ge(ones, 2)
            turns(dve, walk)

        @block.gpsimd
        def _(pool):
            before = []

            def step(out_, a, b, op, s, value):
                if before:
                    pool.wait_ge(*before)
                pool.tensor_tensor(out_, a, b, op).then_inc(s, 1)
                before[:] = [s, value]

            def low_k(pair, u):
                c = kv_units[u][1]
                pool.wait_ge(k_hi, event(pair, NK, u))
                low = km[HD:P, c * CH:(c + 1) * CH]
                step(low, k_raw[HD:P, u % 2, :], low.bitcast(F32), ALU.subtract, k_lo, event(pair, NK, u))

            def low_v(pair, u):
                c = kv_units[u][1]
                pool.wait_ge(v_hi, event(pair, NK, u))
                step(vm[:, 4 * c:4 * c + 4, HD:2 * HD], v_raw[:, u % 2, :, :],
                     vm[:, 4 * c:4 * c + 4, 0:HD].bitcast(F32), ALU.subtract, v_lo, event(pair, NK, u))

            def low_q(pair, u):
                pool.wait_ge(q_hi, event(pair, NQ, u))
                step(qm_lo[:, u % QN, :], q_raw[:, u % 2, :], qm_hi[:, u % QN, :].bitcast(F32),
                     ALU.subtract, q_lo, event(pair, NQ, u))

            def low_w(pair, j):
                pool.wait_ge(w_hi_done, event(pair, STRIPS, j))
                step(w_lo[:, j % 2, :, :], w_raw[:, :, :], w_hi[:, j % 2, :, :].bitcast(F32),
                     ALU.subtract, w_lo_done, event(pair, STRIPS, j))

            def finish_row(pair, n):
                e, i, row = ITEMS[n][0], ITEMS[n][1], ROW_OF[n]
                mine = slice(e * HD, e * HD + HD)
                u = row // 4
                pool.wait_ge(row_done, event(pair, ROWS, row))
                if i % 4 == 3:
                    wait(pool, y_stored[u % 2], event(pair, 4, u // 2 - 1), DMA)
                step(y_out[mine, u % 2, i % 4 * P:i % 4 * P + P], row_sum[mine, 0:P],
                     row_sum[mine, P:2 * P], ALU.add, y_done, event(pair, ROWS, row))

            def times_mix(pair, c):
                pool.wait_ge(silu_done, event(pair, 2 * NC, c))
                pool.wait_ge(mix_in, event(pair, NC, c) * DMA)
                step(res[:, c % 2, :], res[:, c % 2, :], mix_t[:, :], ALU.mult, yp_done, event(pair, NC, c))

            def walk(p, steps, prev, own, nxt):
                before.clear()
                for s in steps:
                    here = placed(p, s, prev, own, nxt)
                    for u in range(NK):
                        if pair := here(k_step[u]):
                            low_k(pair, u)
                        if pair := here(v_step[u]):
                            low_v(pair, u)
                    for u in range(NQ):
                        if pair := here(q_step[u]):
                            low_q(pair, u)
                    for n in ROW_OF:
                        if pair := here(n + AV_LAG + 1):
                            finish_row(pair, n)
                    for c in range(NC):
                        if pair := here(fin[c] + 1):
                            times_mix(pair, c)
                    for j in range(STRIPS):
                        if pair := here(w_step[j]):
                            if not (s < 0 and j == 0):
                                low_w(pair, j)
                if before:
                    pool.wait_ge(*before)

            for i in range(2):
                pool.memset(keep[:, i, CH:CH + 1], 1.0).then_inc(ones, 1)
            pool.wait_ge(ones, 2)
            pool.sem_inc(w_lo_done, 1)
            turns(pool, walk)


def stage4(nc, sem, psum, sb, x, yp_d, za_d, at_d, gate_d, w_pool_up, w_attn_up, w_out, final_g, out):
    UK = AW // P
    up_hi = [sb(f"up_hi{b}", [P, UK, D], F32R) for b in range(2)]
    up_lo = [sb(f"up_lo{b}", [P, UK, D], F32R) for b in range(2)]
    wo_hi = sb("wo_hi", [P, KT, D], F32R)
    wo_lo = sb("wo_lo", [P, KT, D], F32R)
    y_hi = [sb(f"y_hi{b}", [P, UK, CH], F32R) for b in range(2)]
    y_lo = [sb(f"y_lo{b}", [P, UK, CH], F32R) for b in range(2)]
    y_raw = sb("y_raw", [P, 2, CH])
    z_raw = sb("z_raw", [P, CH])
    gate = sb("gate", [P, 4, CH])
    m_hi = sb("m_hi", [P, KT, CH], F32R)
    m_lo = sb("m_lo", [P, KT, CH], F32R)
    row = sb("row", [P, 2, D])
    raw = row[:, :, :].rearrange("p a (b n) -> p (a b) n", n=CH)
    fg = sb("fg", [P, D])
    st = sb("st4", [P, 2, 8])

    UP, SLOTS = 2 * KT, 4
    arrival = [0, 1, 2, 3]
    for m in range(KT):
        arrival += [2 * m + 4, 2 * m + 5] if m + 2 < KT else []
        arrival += [UP + 2 * m, UP + 2 * m + 1]
    n_raw = len(arrival)
    up_ready = [arrival.index(2 * m + 1) + 1 for m in range(KT)]
    by = [up_ready[min(m + 1, KT - 1)] for m in range(KT)]
    fg_in = sem("s4_fg_in")
    raw_in = [sem(f"s4_raw_in{i}") for i in range(SLOTS)]
    raw_hi, raw_lo = sem("s4_raw_hi"), sem("s4_raw_lo")
    y_in = [sem(f"s4_y_in{i}") for i in range(2)]
    z_in, z_done = sem("s4_z_in"), sem("s4_z_done")
    y_hi_done, y_lo_done = sem("s4_y_hi"), sem("s4_y_lo")
    g_in = [sem(f"s4_g_in{i}") for i in range(2)]
    up_done, gated, summed = sem("s4_up_done"), sem("s4_gated"), sem("s4_summed")
    m_hi_done, m_lo_done = sem("s4_m_hi"), sem("s4_m_lo")
    out_done, added = sem("s4_out_done"), sem("s4_added")
    x_in = [sem(f"s4_x_in{i}") for i in range(2)]
    squared, mean, rooted, newton, scaled = (sem(f"s4_{n}") for n in ("squared", "mean", "rooted", "newton", "scaled"))
    finished = sem("s4_finished")
    stored = [sem(f"s4_stored{i}") for i in range(2)]
    NY, NM, NT = 2 * UK, KT, CH // P

    def event(c, per, n):
        assert n >= -per
        return c * per + (per + n + 1)

    def piece(i):
        n = arrival[i]
        if n < UP:
            m, b = divmod(n, 2)
            cols = slice(m * P, (m + 1) * P)
            slot = raw[:, i % SLOTS, :].rearrange("p (k n) -> p k n", n=P)
            return (w_pool_up, w_attn_up)[b][:, :, cols], up_hi[b][:, :, cols], up_lo[b][:, :, cols], slot
        k, h = divmod(n - UP, 2)
        half = slice(h * CH, (h + 1) * CH)
        return w_out[:, k, half], wo_hi[:, k, half], wo_lo[:, k, half], raw[:, i % SLOTS, :]

    with nc.Block() as block:
        @block.sync
        def _(sp):
            def load_weights(a, b):
                for i in range(a, b):
                    if i >= SLOTS:
                        sp.wait_ge(raw_lo, i - SLOTS + 1)
                    src, _hi, _lo, slot = piece(i)
                    sp.dma_start(slot, src).then_inc(raw_in[i % SLOTS], DMA)

            def load_y(c, i):
                b, k = divmod(i, UK)
                tok = bass.ds(c * CH, CH)
                sp.wait_ge(y_lo_done, event(c, NY, i - 2))
                sp.dma_start(y_raw[:, i % 2, :], (yp_d, at_d)[b][k, :, tok]).then_inc(y_in[i % 2], DMA)
                if b == 1:
                    sp.wait_ge(z_done, event(c, UK, k - 1))
                    sp.dma_start(z_raw[:, :], za_d[k, :, tok]).then_inc(z_in, DMA)

            def load_gates(c, m):
                tok = bass.ds(c * CH, CH)
                sp.wait_ge(m_lo_done, event(c, NM, m - 2))
                for b in range(2):
                    sp.dma_start(gate[:, m % 2 * 2 + b, :], gate_d[b * KT + m, :, tok]).then_inc(g_in[m % 2], DMA)

            def load_x(c, t):
                sp.wait_ge(stored[t % 2], c * (2 * DMA) + (2 + t // 2) * DMA)
                sp.dma_start(row[:, t % 2, :], x[bass.ds(c * CH + t * P, P), :]).then_inc(x_in[t % 2], DMA)

            def store(c, t):
                sp.wait_ge(finished, event(c, NT, t))
                sp.dma_start(out[bass.ds(c * CH + t * P, P), :], row[:, t % 2, :]).then_inc(stored[t % 2], DMA)

            def finish(c, following):
                def y(*tiles):
                    for i in tiles:
                        if following:
                            load_y(c + 1, i)

                y(0, 1)
                load_x(c, 0)
                load_x(c, 1)
                y(2, 3, 4)
                store(c, 0)
                load_x(c, 2)
                y(5, 6)
                store(c, 1)
                load_x(c, 3)
                y(7)
                if following:
                    load_gates(c + 1, 0)
                    load_gates(c + 1, 1)
                store(c, 2)
                store(c, 3)

            for s, n in ((y_in[0], NY // 2), (y_in[1], NY // 2), (z_in, UK), (g_in[0], NM), (g_in[1], NM),
                         (x_in[0], 2), (x_in[1], 2), (stored[0], 2), (stored[1], 2)):
                sp.sem_inc(s, n * DMA)
            load_weights(0, 1)
            load_y(0, 0)
            load_y(0, 1)
            load_weights(1, 2)
            for i in range(2, UK):
                load_y(0, i)
            load_gates(0, 0)
            for i in range(UK, NY):
                load_y(0, i)
            load_gates(0, 1)
            load_weights(2, by[1])
            sp.dma_start(fg[:, :], final_g.partition_broadcast(P)).then_inc(fg_in, DMA)
            for m in range(2, NM):
                load_weights(by[m - 1], by[m])
                load_gates(0, m)
            load_weights(by[NM - 1], n_raw)
            sp.wait_ge(raw_lo, n_raw)
            finish(0, True)
            with sp.Fori(1, NC - 1) as c:
                for m in range(2, NM):
                    load_gates(c, m)
                finish(c, True)
            for m in range(2, NM):
                load_gates(NC - 1, m)
            finish(NC - 1, False)
            for s in stored:
                sp.wait_ge(s, (NC + 1) * 2 * DMA)

        @block.tensor
        def _(pe):
            for s, n in ((up_done, 2 * NM), (out_done, 2 * NT)):
                pe.sem_inc(s, n)
            def up(c, m):
                pe.wait_ge(raw_lo, up_ready[m])
                for b in range(2):
                    if m == 0:
                        pe.wait_ge(y_lo_done, event(c, NY, UK * (b + 1) - 1))
                    pe.wait_ge(gated, event(c, 2 * NM, 2 * m + b - 4))
                    for k in range(UK):
                        cols = slice(m * P, (m + 1) * P)
                        last = split3(pe, psum[:, m % 2 * 2 + b, :], up_hi[b][:, k, cols], up_lo[b][:, k, cols],
                                      y_hi[b][:, k, :], y_lo[b][:, k, :], k == 0, k == UK - 1)
                    last.then_inc(up_done, 1)

            def project(c, t, h, ks):
                n = 2 * t + h
                cols, tok = slice(h * CH, (h + 1) * CH), slice(t * P, (t + 1) * P)
                for k in ks:
                    pe.wait_ge(m_lo_done, event(c, NM, k)) if t == 0 else None
                    if k == 0:
                        pe.wait_ge(squared, event(c, NT, t - 2))
                    last = split3(pe, psum[:, 4 + n % 4, :], m_hi[:, k, tok], m_lo[:, k, tok],
                                  wo_hi[:, k, cols], wo_lo[:, k, cols], k == 0, k == KT - 1)
                if KT - 1 in ks:
                    last.then_inc(out_done, 1)

            with pe.Fori(0, NC) as c:
                for m in range(NM):
                    up(c, m)
                pe.wait_ge(raw_lo, n_raw)
                for h in range(2):
                    project(c, 0, h, range(KT - 1))
                for h in range(2):
                    project(c, 0, h, range(KT - 1, KT))
                for t in range(1, NT):
                    for h in range(2):
                        project(c, t, h, range(KT))

        @block.scalar
        def _(act):
            for s, n in ((y_hi_done, NY), (m_hi_done, NM), (squared, NT), (rooted, NT)):
                act.sem_inc(s, n)

            def split_weights(a, b):
                for i in range(a, b):
                    act.wait_ge(raw_in[i % SLOTS], DMA * (i // SLOTS + 1))
                    _src, hi, _lo, slot = piece(i)
                    act.activation(hi, slot, ACT.Copy).then_inc(raw_hi, 1)

            def split_y(c, i):
                b, k = divmod(i, UK)
                if b == 0:
                    act.wait_ge(y_in[i % 2], c * (NY // 2 * DMA) + (NY // 2 + i // 2 + 1) * DMA)
                else:
                    act.wait_ge(z_done, event(c, UK, k))
                act.wait_ge(up_done, event(c, 2 * NM, b - 2))
                act.activation(y_hi[b][:, k, :], y_raw[:, i % 2, :], ACT.Copy).then_inc(y_hi_done, 1)

            def merge(c, m):
                act.wait_ge(summed, event(c, NM, m))
                act.wait_ge(out_done, event(c, 2 * NT, -1))
                act.activation(m_hi[:, m, :], gate[:, m % 2 * 2, :], ACT.Copy).then_inc(m_hi_done, 1)

            def square(c, t):
                act.wait_ge(added, event(c, 2 * NT, 2 * t + 1))
                act.activation(psum[:, 4 + 2 * t % 4:6 + 2 * t % 4, :],
                               row[:, t % 2, :].rearrange("p (a b) -> p a b", a=2), ACT.Square,
                               accum_out=st[:, t % 2, 0:1]).then_inc(squared, 1)

            def root(c, t):
                act.wait_ge(mean, event(c, 2 * NT, 2 * t + 1))
                act.activation(st[:, t % 2, 3:4], st[:, t % 2, 2:3], ACT.Sqrt).then_inc(rooted, 1)

            def finish(c, following):
                for t, tiles in enumerate(((0, 1, 2), (3, 4, 5), (6, 7), ())):
                    for i in tiles:
                        if following:
                            split_y(c + 1, i)
                    square(c, t)
                    root(c, t)

            split_weights(0, 1)
            split_y(0, 0)
            split_y(0, 1)
            split_weights(1, 2)
            for i in range(2, NY):
                split_y(0, i)
            split_weights(2, by[1])
            for m in range(NM):
                if m >= 2:
                    split_weights(by[m - 1], by[m])
                merge(0, m)
            split_weights(by[NM - 1], n_raw)
            finish(0, True)
            with act.Fori(1, NC - 1) as c:
                for m in range(NM):
                    merge(c, m)
                finish(c, True)
            for m in range(NM):
                merge(NC - 1, m)
            finish(NC - 1, False)

        @block.vector
        def _(dve):
            for s, n in ((y_lo_done, NY), (gated, 2 * NM), (added, 2 * NT), (mean, 2 * NT), (newton, 2 * NT),
                         (scaled, NT), (finished, NT)):
                dve.sem_inc(s, n)

            def weights_lo(a, b):
                for i in range(a, b):
                    dve.wait_ge(raw_hi, i + 1)
                    _src, hi, lo, slot = piece(i)
                    dve.tensor_tensor(lo, slot, hi.bitcast(F32), ALU.subtract).then_inc(raw_lo, 1)

            def y_low(c, i):
                b, k = divmod(i, UK)
                dve.wait_ge(y_hi_done, event(c, NY, i))
                dve.tensor_tensor(y_lo[b][:, k, :], y_raw[:, i % 2, :], y_hi[b][:, k, :].bitcast(F32),
                                  ALU.subtract).then_inc(y_lo_done, 1)

            def apply_gates(c, m):
                for b in range(2):
                    g = gate[:, m % 2 * 2 + b, :]
                    dve.wait_ge(g_in[m % 2], c * (NM * DMA) + (NM + m // 2 * 2 + 2) * DMA)
                    dve.wait_ge(up_done, event(c, 2 * NM, 2 * m + b))
                    dve.tensor_tensor(g, psum[:, m % 2 * 2 + b, :], g, ALU.mult).then_inc(gated, 1)

            def finish_rows(c, t):
                s = st[:, t % 2, :]
                for h in range(2):
                    r = row[:, t % 2, h * CH:(h + 1) * CH]
                    n = 2 * t + h
                    dve.wait_ge(out_done, event(c, 2 * NT, n))
                    if h == 0:
                        dve.wait_ge(x_in[t % 2], c * (2 * DMA) + (2 + t // 2 + 1) * DMA)
                    dve.tensor_tensor(r, psum[:, 4 + n % 4, :], r, ALU.add).then_inc(added, 1)
                dve.wait_ge(squared, event(c, NT, t))
                dve.tensor_scalar(s[:, 1:2], s[:, 0:1], 1.0 / D, EPS, ALU.mult, ALU.add).then_inc(mean, 1)
                dve.wait_ge(mean, event(c, 2 * NT, 2 * t))
                dve.reciprocal(s[:, 2:3], s[:, 1:2]).then_inc(mean, 1)
                dve.wait_ge(rooted, event(c, NT, t))
                dve.tensor_scalar(s[:, 4:5], s[:, 3:4], s[:, 3:4], s[:, 1:2], ALU.mult,
                                  ALU.mult).then_inc(newton, 1)
                dve.wait_ge(newton, event(c, 2 * NT, 2 * t))
                dve.tensor_scalar(s[:, 5:6], s[:, 4:5], -0.5, 1.5, ALU.mult, ALU.add).then_inc(newton, 1)
                dve.wait_ge(newton, event(c, 2 * NT, 2 * t + 1))
                r = row[:, t % 2, :]
                dve.tensor_scalar(r, r, s[:, 3:4], s[:, 5:6], ALU.mult, ALU.mult).then_inc(scaled, 1)
                dve.wait_ge(scaled, event(c, NT, t))
                dve.tensor_tensor(r, r, fg[:, :], ALU.mult).then_inc(finished, 1)

            def finish(c, following):
                for t, tiles in enumerate(((0, 1, 2), (3, 4, 5), (6, 7), ())):
                    for i in tiles:
                        if following:
                            y_low(c + 1, i)
                    finish_rows(c, t)

            weights_lo(0, 1)
            y_low(0, 0)
            y_low(0, 1)
            weights_lo(1, 2)
            for i in range(2, NY):
                y_low(0, i)
            weights_lo(2, by[1])
            for m in range(NM):
                if m >= 2:
                    weights_lo(by[m - 1], by[m])
                apply_gates(0, m)
            dve.wait_ge(fg_in, DMA)
            weights_lo(by[NM - 1], n_raw)
            finish(0, True)
            with dve.Fori(1, NC - 1) as c:
                for m in range(NM):
                    apply_gates(c, m)
                finish(c, True)
            for m in range(NM):
                apply_gates(NC - 1, m)
            finish(NC - 1, False)

        @block.gpsimd
        def _(pool):
            for s, n in ((z_done, UK), (summed, NM), (m_lo_done, NM)):
                pool.sem_inc(s, n)

            def gate_attention(c, k):
                i = UK + k
                pool.wait_ge(y_in[i % 2], c * (NY // 2 * DMA) + (NY // 2 + i // 2 + 1) * DMA)
                pool.wait_ge(z_in, c * (UK * DMA) + (UK + k + 1) * DMA)
                pool.tensor_tensor(y_raw[:, i % 2, :], y_raw[:, i % 2, :], z_raw[:, :], ALU.mult).then_inc(z_done, 1)

            def merge(c, m):
                g = m % 2 * 2
                pool.wait_ge(gated, event(c, 2 * NM, 2 * m + 1))
                pool.tensor_tensor(gate[:, g, :], gate[:, g, :], gate[:, g + 1, :], ALU.add).then_inc(summed, 1)
                pool.wait_ge(m_hi_done, event(c, NM, m))
                pool.tensor_tensor(m_lo[:, m, :], gate[:, g, :], m_hi[:, m, :].bitcast(F32),
                                   ALU.subtract).then_inc(m_lo_done, 1)

            with pool.Fori(0, NC) as c:
                for k in range(UK):
                    gate_attention(c, k)
                for m in range(NM):
                    merge(c, m)


def kernel(x, norm_g, w_in, b_gate, pool_w, pool_scale, w_pool_up, w_attn_up, w_out, final_g):
    import numpy as np
    import concourse.bacc as bacc
    from concourse.bass_utils import run_bass_kernel_spmd

    def columns(a):
        return np.ascontiguousarray(np.asarray(a).reshape(-1, P).T)

    def by_k(a):
        a = np.asarray(a)
        return np.ascontiguousarray(a.reshape(-1, P, a.shape[-1]).transpose(1, 0, 2))

    w = np.asarray(w_in)[0]
    v_cols = slice(S_ZA * P - AW, S_ZA * P)
    counts = np.minimum(np.arange(PAD)[None, :] + 1, np.array(WINDOWS)[:, None])
    fix = np.broadcast_to((np.array(WINDOWS)[:, None] / counts).astype(np.float32), (P, len(WINDOWS), PAD))
    arrays = {
        "x": np.ascontiguousarray(np.asarray(x)[0]),
        "norm_gT": columns(np.asarray(norm_g)[0]),
        "w_strips": np.ascontiguousarray(w.reshape(KT, P, -1, P).transpose(2, 1, 0, 3)),
        "w_v": by_k(w[:, v_cols]),
        "b_gateT": columns(np.asarray(b_gate)[0]),
        "pool_w": np.ascontiguousarray(np.asarray(pool_w)[0]),
        "pool_scaleT": columns(np.asarray(pool_scale)[0]),
        "w_pool_up": by_k(np.asarray(w_pool_up)[0]),
        "w_attn_up": by_k(np.asarray(w_attn_up)[0]),
        "w_out": by_k(np.asarray(w_out)[0]),
        "final_g": np.ascontiguousarray(np.asarray(final_g)),
        "pool_fix": np.ascontiguousarray(fix),
    }
    nc = bacc.Bacc("TRN2", target_bir_lowering=False, num_devices=1, dynamic_dma_scratch_size=1024)
    args = {n: nc.dram_tensor("in_" + n, a.shape, mybir.dt.from_np(a.dtype), kind="ExternalInput").ap()
            for n, a in arrays.items()}
    out = nc.dram_tensor("out_0", (SEQ, D), F32, kind="ExternalOutput").ap()
    build(nc, **args, out=out)
    r = run_bass_kernel_spmd(nc, [{"in_" + n: a for n, a in arrays.items()}], core_ids=[0])
    return r.results[0]["out_0"].reshape(1, SEQ, D)
```

```python
from contextlib import ExitStack

import concourse.bass as bass
from concourse import mybir

F32 = mybir.dt.float32
F32R = mybir.dt.float32r
ALU = mybir.AluOpType
ACT = mybir.ActivationFunctionType

P = 128
SEQ = 2048
D = 1024
KT = D // P
TT = SEQ // P
CH = 512
NC = SEQ // CH
HD = 64
HEADS = 8
PAIRS = HEADS // 2
AW = HEADS * HD
WINDOWS = (2, 4, 8, 16)
PAD = max(WINDOWS)
EPS = 1e-6
SCALE = HD ** -0.5
MASK = -1.0e30
DMA = 16
POOL_ORDER = (3, 2, 1, 0)
S_U, S_ZP, S_Q, S_K, S_ZA, S_G = 0, 4, 8, 12, 20, 24


class Arena:

    def __init__(self, nc, at, end):
        self.nc, self.at, self.end = nc, at, end

    def __call__(self, name, shape, dtype=F32):
        t = self.nc.alloc_sbuf_tensor_at(name, shape, dtype, offset=self.at)
        size = 4
        for n in shape[1:]:
            size *= n
        self.at += -(-size // 32) * 32
        assert self.at <= self.end, (name, self.at, self.end)
        return t


def split3(pe, out, w_hi, w_lo, m_hi, m_lo, start, stop):
    pe.matmul(out, w_hi, m_hi, start=start, stop=False)
    pe.matmul(out, w_hi, m_lo, start=False, stop=False)
    return pe.matmul(out, w_lo, m_hi, start=False, stop=stop)


def strip_product(pe, out, w_hi, w_lo, hT_hi, hT_lo, tok):
    for k in range(KT):
        last = split3(pe, out, w_hi[:, k, :], w_lo[:, k, :], hT_hi[:, k, tok], hT_lo[:, k, tok], k == 0, k == KT - 1)
    return last


def keep_warm(pe, bank, ident_r, n):
    for _ in range(n):
        pe.matmul(bank, ident_r[:, :], ident_r[:, :].unsqueeze(1).broadcast_to([P, CH // P, P]), start=True, stop=True)


def weight_pieces():
    arrival = [0, 2, 1, 3]
    for m in range(KT):
        arrival += [2 * m + 4, 2 * m + 5] if m + 2 < KT else []
        arrival += [2 * KT + 2 * m, 2 * KT + 2 * m + 1]
    return arrival


K_RAW, V_RAW, KM, Q_RAW = (4 * n for n in (2 * CH, 2 * 4 * HD, SEQ, 2 * 2 * P))
Y_BYTES, Z_BYTES = 4 * AW // P * CH, 4 * 2 * CH


class HeadLoads:

    def __init__(self, nc, sem, free_at, qk_d, v_d):
        at = nc.alloc_sbuf_tensor_at
        self.k_raw = at("k_raw", [P, 2, CH], F32, offset=free_at)
        self.v_raw = at("v_raw", [P, 2, 4, HD], F32, offset=free_at + K_RAW)
        self.q_raw = at("q_raw", [P, 2, 2 * P], F32, offset=free_at + K_RAW + V_RAW + KM)
        self.w_in = sem("s3_w_in")
        self.k_in, self.v_in, self.q_in = ([sem(f"s3_{n}_in{i}") for i in range(2)] for n in "kvq")
        self.qk_d, self.v_d = qk_d, v_d

    def load_k(self, sp, pair, u, e, c):
        for h in range(2):
            sp.dma_start(self.k_raw[h * HD:(h + 1) * HD, u % 2, :],
                         self.qk_d[pair[0] + (pair[1] + PAIRS), e * HD:(e + 1) * HD, c * CH:(c + 1) * CH]
                         ).then_inc(self.k_in[u % 2], DMA)

    def load_v(self, sp, pair, u, e, c):
        cols = bass.ds(pair[0] * P + (pair[1] * P + e * HD), HD)
        sp.dma_start(self.v_raw[:, u % 2, :, :],
                     self.v_d[c * CH:(c + 1) * CH, cols].rearrange("(a q) d -> q a d", q=P)
                     ).then_inc(self.v_in[u % 2], DMA)

    def load_q(self, sp, pair, u, e, r):
        for h in range(2):
            sp.dma_start(self.q_raw[h * HD:(h + 1) * HD, u % 2, :],
                         self.qk_d[pair[0] + pair[1], e * HD:(e + 1) * HD, r * 2 * P:(r + 1) * 2 * P]
                         ).then_inc(self.q_in[u % 2], DMA)

    def load_first(self, sp):
        for u in range(2):
            self.load_k(sp, (0, 0), u, 0, NC - 1 - u)
            if u == 0:
                self.load_q(sp, (0, 0), 0, 0, TT // 2 - 1)
            self.load_v(sp, (0, 0), u, 0, NC - 1 - u)


class Opening:
    SLOTS, EARLY = 4, 3

    def __init__(self, sem, at, w_pool_up, w_attn_up, w_out, yp_d, at_d, za_d):
        self.up, self.w_out, self.y, self.za_d = (w_pool_up, w_attn_up), w_out, (yp_d, at_d), za_d
        self.y_lo = [at("y_lo0", 0, [P, AW // P, CH], F32R), at("y_lo1", 3, [P, AW // P, CH], F32R)]
        self.z_raw = at("z_raw", 1, [P, 2, CH], F32)
        self.row = at("row", 2, [P, 2, D], F32)
        self.raw = self.row[:, :, :].rearrange("p a (b n) -> p (a b) n", n=CH)
        self.raw_in = [sem(f"s4_raw_in{i}") for i in range(self.SLOTS)]
        self.y_in = [sem(f"s4_y_in{b}") for b in range(2)]
        self.z_in = [sem(f"s4_z_in{i}") for i in range(2)]
        self.arrival = weight_pieces()

    def load_piece(self, sp, i):
        n, slot = self.arrival[i], self.raw[:, i % self.SLOTS, :]
        if n < 2 * KT:
            m, b = divmod(n, 2)
            src = self.up[b][:, :, m * P:(m + 1) * P]
            slot = slot.rearrange("p (k n) -> p k n", n=P)
        else:
            k, h = divmod(n - 2 * KT, 2)
            src = self.w_out[:, k, h * CH:(h + 1) * CH]
        sp.dma_start(slot, src).then_inc(self.raw_in[i % self.SLOTS], DMA)

    def load_y(self, sp, b, tok):
        src = self.y[b][:, :, tok].rearrange("k p t -> p k t")
        sp.dma_start(self.y_lo[b][:, :, :].bitcast(F32), src).then_inc(self.y_in[b], DMA)

    def load_z(self, sp, k, tok):
        sp.dma_start(self.z_raw[:, k % 2, :], self.za_d[k, :, tok]).then_inc(self.z_in[k % 2], DMA)


def build(nc, x, x_T, norm_gT, w_strips, w_v, b_gateT, pool_w, pool_scaleT, w_pool_up, w_attn_up, w_out,
          final_g, pool_fix, out):
    def scratch(name, shape):
        return nc.dram_tensor(name, shape, F32, kind="Internal").ap()

    qk_d = scratch("qk_scratch", [2 * PAIRS, P, SEQ])
    v_d = scratch("v_scratch", [SEQ, AW])
    mix_d = scratch("mix_scratch", [PAIRS, P, SEQ])
    yp_d = scratch("y_pool_scratch", [PAIRS, P, SEQ])
    za_d = scratch("z_attn_scratch", [PAIRS, P, SEQ])
    at_d = scratch("attn_scratch", [PAIRS, P, SEQ])
    gate_d = scratch("gate_scratch", [4 * PAIRS, P, SEQ])

    with ExitStack() as ctx:
        def sem(name):
            return ctx.enter_context(nc.semaphore(name))

        psum = ctx.enter_context(nc.psum_tensor("psum", [P, 8, 512], F32))
        base = -(-nc.sbuf_base // 32) * 32
        end = nc.sbuf_usable_end
        fixed = Arena(nc, base, end)
        ident = fixed("ident", [P, P])
        ident_r = fixed("ident_r", [P, P], F32R)
        mask_f = fixed("mask_f", [P, P])
        mask_r = fixed("mask_r", [P, P], F32R)
        gcol = fixed("gcol", [P, KT])
        bcol = fixed("bcol", [P, 2 * KT])
        pscol = fixed("pscol", [P, PAIRS])
        staging = fixed("staging", [P, 2, CH])
        hT_at = fixed.at
        hT_hi = fixed("hT_hi", [P, KT, SEQ], F32R)
        hT_lo = fixed("hT_lo", [P, KT, SEQ], F32R)
        w_raw = fixed("w_raw", [P, KT, P])
        w_parts = fixed("w_parts", [P, 2, 2, KT, P], F32R)
        w_hi, w_lo = w_parts[:, :, 0, :, :], w_parts[:, :, 1, :, :]
        free_at = fixed.at
        stored1, stored2, stored3, y_stored = ([sem(f"{n}{i}") for i in range(2)] for n in (
            "s1_v_stored", "s2_stored", "s3_res_stored", "s3_y_stored"))

        spare = nc.alloc_sbuf_tensor_at("spare", [P, 3, P], F32, offset=free_at - 2 * KT * P * 4)
        stage1(nc, sem, psum, Arena(nc, free_at, end), ident, ident_r, mask_f, mask_r, gcol, bcol, pscol,
               hT_hi, hT_lo, w_raw, w_hi, w_lo, x, x_T, norm_gT, w_v, b_gateT, pool_scaleT,
               w_strips[S_U + POOL_ORDER[0]], v_d, spare, staging, stored1)
        head_loads = HeadLoads(nc, sem, free_at, qk_d, v_d)
        stage2(nc, sem, psum, Arena(nc, free_at, end), pscol, hT_hi, hT_lo, w_raw, w_hi, w_lo,
               w_strips, pool_w, pool_fix, qk_d, mix_d, staging, stored1, stored2,
               head_loads)
        w_at = free_at - 5 * KT * P * 4
        places = [w_at, w_at + Y_BYTES, free_at, free_at + K_RAW + V_RAW + KM // NC]
        opening = Opening(sem, lambda name, i, shape, dtype: nc.alloc_sbuf_tensor_at(
            name, shape, dtype, offset=places[i]), w_pool_up, w_attn_up, w_out, yp_d, at_d, za_d)
        last_stores = stage3(nc, sem, psum, Arena(nc, free_at, end), ident, ident_r, mask_r, bcol, hT_hi,
                             hT_lo, w_raw, w_hi, w_lo, w_strips, mix_d, yp_d, za_d, at_d, gate_d, staging,
                             stored2, stored3, y_stored, opening, head_loads)
        stage4(nc, sem, psum, Arena(nc, hT_at, w_at), Arena(nc, w_at + Y_BYTES + Z_BYTES, free_at),
               Arena(nc, places[3] + Y_BYTES, end), x, gate_d, final_g, out, stored3, y_stored, opening,
               ident_r, last_stores)


def stage1(nc, sem, psum, sb, ident, ident_r, mask_f, mask_r, gcol, bcol, pscol, hT_hi, hT_lo, w_raw, w_hi,
           w_lo, x, x_T, norm_gT, w_v, b_gateT, pool_scaleT, first_strip, v_d, spare, v_out, v_stored):
    wv_hi = sb("wv_hi", [P, KT, AW], F32R)
    wv_lo = sb("wv_lo", [P, KT, AW], F32R)
    xt = sb("xt", [P, 2, D])
    xT = sb("xT", [P, 2, KT, P])
    scaled = sb("scaled", [P, 2, CH])
    diag = spare[:, 0:2, :]
    ones = spare[:, 2, :]
    stat = sb("stat", [P, TT, 8])
    WV = KT // 2
    wv_raw = sb("wv_raw", [P, KT, AW])
    strip_in, strip_hi, strip_lo = sem("s1_strip_in"), sem("s1_strip_hi"), sem("s1_strip_lo")

    bias_in = sem("s1_bias_in")
    const_in, ident_done = sem("s1_const_in"), sem("s1_ident_done")
    mask_done, consts_r = sem("s1_mask_done"), sem("s1_consts_r")
    x_in = [sem(f"s1_x_in{i}") for i in range(2)]
    wv_in = [sem(f"s1_wv_in{i}") for i in range(WV)]
    wv_hi_done, wv_lo_done = sem("s1_wv_hi"), sem("s1_wv_lo")
    xT_in = [sem(f"s1_xT_in{i}") for i in range(2)]
    squared, rooted, diag_done = sem("s1_squared"), sem("s1_rooted"), sem("s1_diag")
    mean_done = sem("s1_mean")
    spread_done, scaled_done = sem("s1_spread"), sem("s1_scaled")
    hi_done, lo_done = sem("s1_hi"), sem("s1_lo")
    v_done, v_copied = sem("s1_v_done"), sem("s1_v_copied")

    with nc.Block() as block:
        @block.sync
        def _(sp):
            def load_x(t):
                if t >= 2:
                    sp.wait_ge(squared, t - 1)
                sp.dma_start(xt[:, t % 2, :], x[t * P:(t + 1) * P, :]).then_inc(x_in[t % 2], DMA)
                if t >= 2:
                    sp.wait_ge(scaled_done, 2 * (t - 1))
                load_xT(t)

            def load_xT(t):
                sp.dma_start(xT[:, t % 2, :, :], x_T[t]).then_inc(xT_in[t % 2], DMA)

            load_x(0)
            sp.dma_start(gcol[:, :], norm_gT).then_inc(const_in, DMA)
            for i in range(WV):
                sp.dma_start(wv_raw[:, 2 * i:2 * i + 2, :], w_v[:, 2 * i:2 * i + 2, :]).then_inc(wv_in[i], DMA)
                if i == 2:
                    sp.dma_start(xt[:, 1, :], x[P:2 * P, :]).then_inc(x_in[1], DMA)
            load_xT(1)
            sp.dma_start(bcol[:, :], b_gateT).then_inc(bias_in, DMA)
            sp.dma_start(pscol[:, :], pool_scaleT).then_inc(bias_in, DMA)
            for t in range(2, WV + 1):
                load_x(t)
            sp.dma_start(w_raw[:, :, :], first_strip).then_inc(strip_in, DMA)
            for t in range(WV + 1, TT):
                load_x(t)
                if t >= 5:
                    i = t - 5
                    sp.wait_ge(v_copied, i + 1)
                    sp.dma_start(v_d[i * P:(i + 1) * P, :], v_out[:, i % 2, :]).then_inc(v_stored[i % 2], DMA)
            for i in range(TT - 5, TT):
                sp.wait_ge(v_copied, i + 1)
                sp.dma_start(v_d[i * P:(i + 1) * P, :], v_out[:, i % 2, :]).then_inc(v_stored[i % 2], DMA)
            sp.wait_ge(bias_in, 2 * DMA)

        @block.gpsimd
        def _(pool):
            pool.memset(ident[:, :], 0.0).then_inc(ident_done, 1)
            pool.memset(mask_f[:, :], 0.0).then_inc(mask_done, 1)
            pool.wait_ge(ident_done, 1)
            pool.affine_select(out=ident[:, :], in_=ident[:, :], compare_op=ALU.not_equal, fill=1.0,
                               base=0, pattern=[[-1, P]], channel_multiplier=1).then_inc(ident_done, 1)
            pool.wait_ge(ident_done, 2)
            pool.memset(ones, 1.0).then_inc(ident_done, 1)
            pool.wait_ge(mask_done, 1)
            pool.affine_select(out=mask_f[:, :], in_=mask_f[:, :], compare_op=ALU.is_gt, fill=MASK,
                               base=0, pattern=[[-1, P]], channel_multiplier=1).then_inc(mask_done, 1)
            for t in range(TT):
                for hb in range(2):
                    n = 2 * t + hb
                    pool.wait_ge(hi_done, n + 1)
                    k = slice(4 * hb, 4 * hb + 4)
                    pool.tensor_tensor(hT_lo[:, k, t * P:(t + 1) * P],
                                       scaled[:, hb, :].rearrange("p (k n) -> p k n", k=4),
                                       hT_hi[:, k, t * P:(t + 1) * P].bitcast(F32),
                                       ALU.subtract).then_inc(lo_done, 1)
                if t == TT // 2:
                    pool.wait_ge(strip_hi, 1)
                    pool.tensor_tensor(w_lo[:, 0, :, :], w_raw[:, :, :], w_hi[:, 0, :, :].bitcast(F32),
                                       ALU.subtract).then_inc(strip_lo, 1)

        @block.scalar
        def _(act):
            def square(t):
                act.wait_ge(x_in[t % 2], DMA * (t // 2 + 1))
                act.activation(psum[:, 2:4, :], xt[:, t % 2, :].rearrange("p (a b) -> p a b", a=2), ACT.Square,
                               accum_out=stat[:, t, 0:1]).then_inc(squared, 1)

            def root(t):
                act.wait_ge(mean_done, 2 * t + 2)
                act.activation(stat[:, t, 3:4], stat[:, t, 2:3], ACT.Sqrt).then_inc(rooted, 1)

            def weights_hi(i):
                part = slice(2 * i, 2 * i + 2)
                act.wait_ge(wv_in[i], DMA)
                act.activation(wv_hi[:, part, :], wv_raw[:, part, :], ACT.Copy).then_inc(wv_hi_done, 1)

            def part_hi(t):
                for hb in range(2):
                    n = 2 * t + hb
                    act.wait_ge(scaled_done, n + 1)
                    act.activation(hT_hi[:, 4 * hb:4 * hb + 4, t * P:(t + 1) * P],
                                   scaled[:, hb, :].rearrange("p (k n) -> p k n", k=4),
                                   ACT.Copy).then_inc(hi_done, 1)

            act.wait_ge(ident_done, 2)
            act.activation(stat[:, 0, 7:8], ident[:, 0:1], ACT.Sqrt)
            square(0)
            root(0)
            weights_hi(0)
            part_hi(0)
            weights_hi(1)
            weights_hi(2)
            square(1)
            root(1)
            for i in range(3, WV):
                weights_hi(i)
            for t in range(2, TT):
                square(t)
                part_hi(t - 1)
                root(t)
                if t == TT // 2 - 1:
                    act.wait_ge(strip_in, DMA)
                    act.activation(w_hi[:, 0, :, :], w_raw[:, :, :], ACT.Copy).then_inc(strip_hi, 1)
            part_hi(TT - 1)

        @block.vector
        def _(dve):
            dve.wait_ge(ident_done, 2)
            dve.tensor_copy(ident_r[:, :], ident[:, :]).then_inc(consts_r, 1)
            dve.wait_ge(mask_done, 2)
            dve.tensor_copy(mask_r[:, :], mask_f[:, :]).then_inc(consts_r, 1)
            newton = sem("s1_newton")

            def copy_v(i):
                dve.wait_ge(v_done, i + 1)
                if i >= 2:
                    dve.wait_ge(v_stored[i % 2], DMA * (i // 2))
                dve.tensor_copy(v_out[:, i % 2, :], psum[:, 4 + i % 2, :]).then_inc(v_copied, 1)

            def scale(t):
                dve.wait_ge(xT_in[t % 2], DMA * (t // 2 + 1))
                dve.wait_ge(spread_done, t + 1)
                for k in range(KT):
                    hb, kk = divmod(k, 4)
                    n = 2 * t + hb
                    if t >= 1 and kk == 0:
                        dve.wait_ge(lo_done, n - 1)
                    last = dve.scalar_tensor_tensor(scaled[:, hb, kk * P:(kk + 1) * P], xT[:, t % 2, k, :],
                                                    gcol[:, k:k + 1], psum[:, t % 2, 0:P], ALU.mult, ALU.mult)
                    if kk == 3:
                        last.then_inc(scaled_done, 1)

            def mean(t):
                dve.wait_ge(squared, t + 1)
                dve.tensor_scalar(stat[:, t, 1:2], stat[:, t, 0:1], 1.0 / D, EPS, ALU.mult,
                                  ALU.add).then_inc(mean_done, 1)
                dve.wait_ge(mean_done, 2 * t + 1)
                dve.reciprocal(stat[:, t, 2:3], stat[:, t, 1:2]).then_inc(mean_done, 1)

            def factors(t):
                dve.wait_ge(rooted, t + 1)
                dve.tensor_scalar(stat[:, t, 4:5], stat[:, t, 3:4], stat[:, t, 3:4], stat[:, t, 1:2],
                                  ALU.mult, ALU.mult).then_inc(newton, 1)
                dve.wait_ge(newton, 2 * t + 1)
                dve.tensor_scalar(stat[:, t, 5:6], stat[:, t, 4:5], -0.5, 1.5, ALU.mult,
                                  ALU.add).then_inc(newton, 1)
                dve.wait_ge(newton, 2 * t + 2)
                if t >= 2:
                    dve.wait_ge(spread_done, t - 1)
                dve.tensor_scalar(diag[:, t % 2, :], ident[:, :], stat[:, t, 3:4], stat[:, t, 5:6],
                                  ALU.mult, ALU.mult).then_inc(diag_done, 1)

            def weights_lo(i):
                part = slice(2 * i, 2 * i + 2)
                dve.wait_ge(wv_hi_done, i + 1)
                dve.tensor_tensor(wv_lo[:, part, :], wv_raw[:, part, :], wv_hi[:, part, :].bitcast(F32),
                                  ALU.subtract).then_inc(wv_lo_done, 1)

            dve.wait_ge(const_in, DMA)
            mean(0)
            factors(0)
            scale(0)
            weights_lo(0)
            weights_lo(1)
            weights_lo(2)
            mean(1)
            factors(1)
            for i in range(3, WV):
                weights_lo(i)
            for t in range(2, TT):
                scale(t - 1)
                mean(t)
                factors(t)
                if t >= 3:
                    copy_v(t - 3)
            scale(TT - 1)
            for i in range(TT - 3, TT):
                copy_v(i)

        @block.tensor
        def _(pe):
            def spread(t):
                pe.wait_ge(diag_done, t + 1)
                if t >= 2:
                    pe.wait_ge(scaled_done, 2 * (t - 1))
                pe.matmul(psum[:, t % 2, 0:P], ones[:, :], diag[:, t % 2, :], start=True,
                          stop=True).then_inc(spread_done, 1)

            def project_v(t):
                pe.wait_ge(lo_done, 2 * t + 1)
                if t >= 2:
                    pe.wait_ge(v_copied, t - 1)
                tok = slice(t * P, (t + 1) * P)
                for k in range(KT):
                    if t == 0 and k % 2 == 0:
                        pe.wait_ge(wv_lo_done, k // 2 + 1)
                    if k == KT // 2:
                        pe.wait_ge(lo_done, 2 * t + 2)
                    if k == KT - 2 and t + (2 if t else 1) < TT:
                        spread(t + (2 if t else 1))
                    last = split3(pe, psum[:, 4 + t % 2, :], hT_hi[:, k, tok], hT_lo[:, k, tok],
                                  wv_hi[:, k, :], wv_lo[:, k, :], k == 0, k == KT - 1)
                last.then_inc(v_done, 1)

            pe.wait_ge(ident_done, 3)
            pe.wait_ge(consts_r, 2)
            keep_warm(pe, psum[:, 7, :], ident_r, 12)
            spread(0)
            keep_warm(pe, psum[:, 7, :], ident_r, 10)
            project_v(0)
            spread(2)
            for t in range(1, TT):
                project_v(t)
            pe.wait_ge(strip_lo, 1)
            pe.wait_ge(scaled_done, 2 * (TT - 1))
            strip_product(pe, psum[:, 0, :], w_hi[:, 0, :, :], w_lo[:, 0, :, :], hT_hi, hT_lo, slice(0, CH))


def stage2(nc, sem, psum, sb, pscol, hT_hi, hT_lo, w_raw, w_hi, w_lo, w_strips, pool_w, pool_fix,
           qk_d, mix_d, store, stored_before, stored, head_loads):
    G = len(WINDOWS)
    W = PAD + SEQ
    us = [sb(f"u{i}", [P, W]) for i in range(2)]
    sums = [sb(f"sums{i}", [P, W]) for i in range(2)]
    pooled = sb("pooled", [P, SEQ])
    pl_hi = sb("pl_hi", [P, SEQ], F32R)
    pl_lo = sb("pl_lo", [P, SEQ], F32R)
    pw = sb("pw", [P, G, P])
    pw_hi = sb("pw_hi", [P, G, P], F32R)
    pw_lo = sb("pw_lo", [P, G, P], F32R)
    fix = sb("fix", [P, G, PAD])
    order = POOL_ORDER
    UM, QM = G, 2 * PAIRS

    raw_in, hi_done, lo_done = sem("s2_w_in"), sem("s2_w_hi"), sem("s2_w_lo")
    proj_done, copied = sem("s2_proj_done"), sem("s2_copied")
    mixed = sem("s2_mixed")
    staged = sem("s2_staged")
    pw_in, pw_hi_done, pw_lo_done = sem("s2_pw_in"), sem("s2_pw_hi"), sem("s2_pw_lo")
    zeroed, level, pool_hi, pool_lo = sem("s2_zeroed"), sem("s2_level"), sem("s2_pool_hi"), sem("s2_pool_lo")
    levels = {g: WINDOWS[g].bit_length() - 1 for g in range(G)}
    first_level = {}
    at = 0
    for g in order:
        first_level[g] = at
        at += levels[g] + 2

    def use_of_mix(m, c):
        return 4 * m + c if m < G - 1 else 4 * (G - 1) + 4 + c

    def use_of_strip(j, c):
        return 4 * (G - 1) + c if isinstance(j, int) and j == 0 else j * 4 + 4 * G + c

    with nc.Block() as block:
        @block.sync
        def _(sp):
            def load(strip, n):
                sp.wait_ge(lo_done, n) if not isinstance(n, int) or n > 0 else None
                sp.dma_start(w_raw[:, :, :], w_strips[strip]).then_inc(raw_in, DMA)

            def put(dst, use, slot):
                sp.wait_ge(staged, use + 1)
                sp.dma_start(dst, store[:, slot, :]).then_inc(stored[slot], DMA)

            sp.sem_inc(raw_in, DMA)
            sp.dma_start(pw[:, :, :], pool_w.rearrange("g c d -> c g d")).then_inc(pw_in, DMA)
            sp.dma_start(fix[:, :, :], pool_fix).then_inc(pw_in, DMA)
            for j in range(1, UM):
                load(S_U + order[j], j)
                if j >= 2:
                    for c in range(NC):
                        put(mix_d[order[j - 2], :, c * CH:(c + 1) * CH], use_of_mix(j - 2, c), c % 2)
            load(S_Q, UM)
            load(S_Q + 1, UM + 1)
            for c in range(NC):
                put(mix_d[order[2], :, c * CH:(c + 1) * CH], use_of_mix(2, c), c % 2)
            load(S_Q + 2, UM + 2)
            for c in range(NC):
                put(qk_d[0, :, c * CH:(c + 1) * CH], use_of_strip(0, c), c % 2)
            for c in range(NC):
                put(mix_d[order[3], :, c * CH:(c + 1) * CH], use_of_mix(3, c), c % 2)
            load(S_Q + 3, UM + 3)
            for c in range(NC):
                put(qk_d[1, :, c * CH:(c + 1) * CH], use_of_strip(1, c), c % 2)
            with sp.Fori(1, QM // 2 - 1) as p:
                for r in range(2):
                    load(p * 2 + (S_Q + 2 + r), p * 2 + (UM + 2 + r))
                    for c in range(NC):
                        put(qk_d[p * 2 + r, :, c * CH:(c + 1) * CH], use_of_strip(p * 2 + r, c), c % 2)
            load(S_ZP, UM + QM)
            for j in (QM - 2, QM - 1):
                if j == QM - 1:
                    sp.wait_ge(level, at)
                    for i in range(2):
                        sp.wait_ge(stored[i], use_of_strip(PAIRS + 1, 0) // 2 * DMA)
                        sp.wait_ge(stored_before[i], DMA * TT // 2)
                    head_loads.load_first(sp)
                for c in range(NC):
                    put(qk_d[j, :, c * CH:(c + 1) * CH], use_of_strip(j, c), c % 2)
            sp.wait_ge(lo_done, UM + QM + 1)
            sp.dma_start(w_raw[:, :, :], w_strips[S_ZA]).then_inc(head_loads.w_in, DMA)

        def scalar_weights(act, n, slot):
            act.wait_ge(raw_in, n * DMA + DMA)
            if not isinstance(n, int) or n >= 2:
                act.wait_ge(proj_done, n * 4 - 4)
            act.activation(w_hi[:, slot, :, :], w_raw[:, :, :], ACT.Copy).then_inc(hi_done, 1)

        @block.scalar
        def _(act):
            def take_staging(use, slot):
                if not isinstance(use, int) or use >= 2:
                    act.wait_ge(stored[slot], (use - slot) * (DMA // 2))
                else:
                    act.wait_ge(stored_before[slot], DMA * TT // 2)

            def copy_u(j):
                for c in range(NC):
                    act.wait_ge(proj_done, 4 * j + c + 1)
                    if j >= 2 and c == 0:
                        act.wait_ge(level, first_level[order[j - 2]] + levels[order[j - 2]] + 2)
                    act.activation(us[j % 2][:, PAD + c * CH:PAD + (c + 1) * CH], psum[:, c % 2, :],
                                   ACT.Copy).then_inc(copied, 1)

            def scale_mix(j):
                for c in range(NC):
                    use = use_of_mix(j, c)
                    act.wait_ge(mixed, 4 * j + c + 1)
                    take_staging(use, c % 2)
                    act.activation(store[:, c % 2, :], psum[:, 2 + c % 2, :], ACT.Copy,
                                   scale=pscol[:, order[j]:order[j] + 1]).then_inc(staged, 1)

            def copy_strip(j, c):
                act.wait_ge(proj_done, j * 4 + (4 * UM + c + 1))
                take_staging(use_of_strip(j, c), c % 2)
                act.activation(store[:, c % 2, :], psum[:, c % 2, :], ACT.Copy).then_inc(staged, 1)

            act.sem_inc(hi_done, 1)
            act.wait_ge(pw_in, 2 * DMA)
            act.activation(pw_hi[:, :, :], pw[:, :, :], ACT.Copy).then_inc(pw_hi_done, 1)
            scalar_weights(act, 1, 1)
            for j in range(UM):
                copy_u(j)
                if j >= 1:
                    scale_mix(j - 1)
                scalar_weights(act, j + 2, j % 2)
            for c in range(NC):
                copy_strip(0, c)
            scale_mix(UM - 1)
            scalar_weights(act, UM + 2, 0)
            for c in range(NC):
                copy_strip(1, c)
            scalar_weights(act, UM + 3, 1)
            with act.Fori(1, QM // 2 - 1) as p:
                for r in range(2):
                    for c in range(NC):
                        copy_strip(p * 2 + r, c)
                    scalar_weights(act, p * 2 + (UM + 2 + r), r)
            for c in range(NC):
                copy_strip(QM - 2, c)
            scalar_weights(act, UM + QM, 0)
            for c in range(NC):
                copy_strip(QM - 1, c)
            act.activation(pw[:, 0, 0:1], pw[:, 0, 0:1], ACT.Sigmoid)

        @block.gpsimd
        def _(pool):
            def weights_lo(n, slot):
                pool.wait_ge(hi_done, n + 1)
                pool.tensor_tensor(w_lo[:, slot, :, :], w_raw[:, :, :], w_hi[:, slot, :, :].bitcast(F32),
                                   ALU.subtract).then_inc(lo_done, 1)

            for t in (*us, *sums):
                pool.memset(t[:, 0:PAD], 0.0).then_inc(zeroed, 1)
            pool.sem_inc(lo_done, 1)
            pool.wait_ge(pw_hi_done, 1)
            pool.tensor_tensor(pw_lo[:, :, :], pw[:, :, :], pw_hi[:, :, :].bitcast(F32),
                               ALU.subtract).then_inc(pw_lo_done, 1)
            weights_lo(1, 1)
            for n in range(2, 4):
                weights_lo(n, n % 2)
            with pool.Fori(2, (UM + QM) // 2) as p:
                for r in range(2):
                    weights_lo(p * 2 + r, r)
            weights_lo(UM + QM, 0)

        @block.vector
        def _(dve):
            dve.wait_ge(zeroed, 4)
            dve.wait_ge(pw_in, 2 * DMA)
            for j in range(UM):
                g = order[j]
                n = first_level[g]
                dve.wait_ge(copied, 4 * (j + 1))
                u = us[j % 2]
                src = u
                for i in range(levels[g]):
                    if i >= 1:
                        dve.wait_ge(level, n)
                    dst = sums[i % 2]
                    dve.tensor_tensor(dst[:, PAD:W], src[:, PAD:W], src[:, PAD - (1 << i):W - (1 << i)],
                                      ALU.add).then_inc(level, 1)
                    n += 1
                    src = dst
                dve.wait_ge(level, n)
                dve.tensor_tensor(src[:, PAD:2 * PAD], src[:, PAD:2 * PAD], fix[:, g, :],
                                  ALU.mult).then_inc(level, 1)
                dve.wait_ge(level, n + 1)
                if j >= 1:
                    dve.wait_ge(pool_lo, j)
                dve.scalar_tensor_tensor(pooled[:, :], src[:, PAD:W], 1.0 / WINDOWS[g], u[:, PAD:W],
                                         ALU.mult, ALU.subtract).then_inc(level, 1)
                dve.wait_ge(level, n + 2)
                if j >= 1:
                    dve.wait_ge(mixed, 4 * j)
                dve.tensor_copy(pl_hi[:, :], pooled[:, :]).then_inc(pool_hi, 1)
                dve.wait_ge(pool_hi, j + 1)
                dve.tensor_tensor(pl_lo[:, :], pooled[:, :], pl_hi[:, :].bitcast(F32),
                                  ALU.subtract).then_inc(pool_lo, 1)

        @block.tensor
        def _(pe):
            def strip(n, slot, free, behind_first=None):
                pe.wait_ge(lo_done, n + 1)
                for c in range(NC):
                    if isinstance(n, int) and n == 0 and c == 0:
                        pe.sem_inc(proj_done, 1)
                        continue
                    free(c)
                    strip_product(pe, psum[:, c % 2, :], w_hi[:, slot, :, :], w_lo[:, slot, :, :], hT_hi, hT_lo,
                                  slice(c * CH, (c + 1) * CH)).then_inc(proj_done, 1)
                    if c == 0 and behind_first:
                        behind_first()

            def mix(j, chunks=range(NC)):
                pe.wait_ge(pool_lo, j + 1)
                for c in chunks:
                    tok = slice(c * CH, (c + 1) * CH)
                    use = use_of_mix(j, c)
                    if 4 * j + c >= 2:
                        back = use - 2 if c >= 2 else use_of_mix(j - 1, c + 2)
                        pe.wait_ge(staged, back + 1)
                    g = order[j]
                    last = split3(pe, psum[:, 2 + c % 2, :], pw_hi[:, g, :], pw_lo[:, g, :],
                                  pl_hi[:, tok], pl_lo[:, tok], True, True)
                    last.then_inc(mixed, 1)

            def free_u(j):
                def wait(c):
                    if 4 * j + c >= 2:
                        pe.wait_ge(copied, 4 * j + c - 1)
                return wait

            def free_strip(j):
                def wait(c):
                    if isinstance(j, int) and j == 0 and c < 2:
                        pe.wait_ge(copied, 4 * UM - 1 + c)
                    elif isinstance(j, int) and j == 1 and c < 2:
                        pe.wait_ge(staged, use_of_strip(0, c + 2) + 1)
                    elif c < 2:
                        pe.wait_ge(staged, j * 4 + (4 * G + c - 1))
                    else:
                        pe.wait_ge(staged, use_of_strip(j, c - 2) + 1)
                return wait

            for j in range(UM):
                if j == 1:
                    pe.wait_ge(pw_lo_done, 1)
                strip(j, j % 2, free_u(j))
                if j >= 1:
                    mix(j - 1)
            strip(UM, 0, free_strip(0))
            mix(UM - 1, (0, 1))
            strip(UM + 1, 1, free_strip(1), lambda: mix(UM - 1, (2, 3)))
            with pe.Fori(1, QM // 2) as p:
                for r in range(2):
                    strip(p * 2 + (UM + r), r, free_strip(p * 2 + r))
            pe.wait_ge(lo_done, UM + QM + 1)
            pe.wait_ge(staged, use_of_strip(QM - 1, 2) + 1)
            strip_product(pe, psum[:, 0, :], w_hi[:, 0, :, :], w_lo[:, 0, :, :], hT_hi, hT_lo, slice(0, CH))


def attention_items():
    return [(e, i, c, (i % 4 + 1) * P if c == i // 4 else CH, c == i // 4, c == 0)
            for e in range(2) for i in reversed(range(TT)) for c in reversed(range(i // 4 + 1))]


def stage3(nc, sem, psum, sb, ident, ident_r, mask_r, bcol, hT_hi, hT_lo, w_raw, w_hi, w_lo, w_strips,
           mix_d, yp_d, za_d, at_d, gate_d, res, stored_before, res_stored, y_stored, opening,
           head_loads):
    ITEMS = attention_items()
    NI = len(ITEMS)
    T_LAG, AV_LAG = 2, 3
    LOAD = 4
    STRIPS = 6
    GROUPS = STRIPS * NC
    MM = 3 * KT
    ROWS = 2 * TT
    AHEAD = MM + MM // 2
    ROW_OF = {}
    for n, it in enumerate(ITEMS):
        if it[5]:
            ROW_OF[n] = len(ROW_OF)
    row_at = [sum(1 for m in ROW_OF if m < n) for n in range(NI)]

    cost = [450.0 + 3.1 * it[3] for it in ITEMS]
    due = [round(sum(cost[:s + 1]) / sum(cost) * GROUPS * MM) for s in range(NI)]
    fin = [next(s for s in range(NI) if due[s] >= (k + 1) * MM) for k in range(GROUPS)]
    due_first = [max(due[s], min(2 * MM, AHEAD + 4 * (s + 1)), min(3 * MM, 2 * MM + 4 * (s - 1)))
                 for s in range(NI)]
    fin_first = [-1, 2] + fin[2:]
    LATE, KEPT = fin[GROUPS - NC - 1], (GROUPS - NC) * MM
    due_last = [due[s] if s <= LATE else KEPT + round((due[s] - KEPT) * (NC - 1) / NC) for s in range(NI)]
    fin_last = [next(s for s in range(NI) if due_last[s] >= (k + 1) * MM) for k in range(GROUPS - 1)] + [NI + AV_LAG]

    def first_item(test):
        return next(n for n, it in enumerate(ITEMS) if test(it))

    def last_item(test):
        return max(n for n, it in enumerate(ITEMS) if test(it))

    kv_units = [(e, c, last_item(lambda it: it[0] == 1 - e and it[2] == c) - (NI if e == 0 else 0))
                for e in range(2) for c in reversed(range(NC))]
    k_step = [before + 1 for _e, _c, before in kv_units]
    v_step = [before + AV_LAG + 1 for _e, _c, before in kv_units]
    QN = 4
    q_units = [(e, r) for e in range(2) for r in reversed(range(TT // 2))]

    def q_last(u):
        e, r = q_units[u % len(q_units)]
        return last_item(lambda it: it[0] == e and it[1] // 2 == r) - (0 if u >= 0 else NI)

    q_before = [q_last(u - QN) for u in range(len(q_units))]
    q_step = [max(q_before[u] + 1, first_item(lambda it: it[0] == e and it[1] // 2 == r) - 4)
              for u, (e, r) in enumerate(q_units)]
    w_step = [fin[(NC * (j - 2) + NC - 1) % GROUPS] + 1 - (NI if j < 2 else 0) for j in range(STRIPS)]
    first_steps = {("k", 0): -9, ("q", 0): -8, ("v", 0): -7, ("k", 1): -6, ("v", 1): -5, ("k", 2): 0, ("k", 3): 1,
                   ("v", 2): 1, ("v", 3): 3, ("w", 1): 5}
    BIAS_STEP = 6

    k_raw, v_raw, q_raw = head_loads.k_raw, head_loads.v_raw, head_loads.q_raw
    sb.at += K_RAW + V_RAW
    km = sb("km", [P, SEQ], F32R)
    sb.at += Q_RAW
    vm = sb("vm", [P, TT, 2 * HD], F32R)
    qm_hi = sb("qm_hi", [P, QN, 2 * P], F32R)
    qm_lo = sb("qm_lo", [P, QN, 2 * P], F32R)
    keep = sb("keep", [P, 2, CH + 1])
    beta = sb("beta", [P, 4, CH])
    left = sb("left", [P, 2, CH + 1])
    wt = sb("wt", [P, 2, 4, 2, P], F32R)
    half_sum = sb("half_sum", [P, 2 * P])
    row_sum = sb("row_sum", [P, 2 * P])
    mix_t = sb("mix_t", [P, CH])
    bias = sb("bias", [P, 4])
    y_out = sb("y_out", [P, 2, CH])

    w_in, w_hi_done, w_lo_done = head_loads.w_in, sem("s3_w_hi"), sem("s3_w_lo")
    k_in, v_in, q_in = head_loads.k_in, head_loads.v_in, head_loads.q_in
    k_hi, v_hi, q_hi = sem("s3_k_hi"), sem("s3_v_hi"), sem("s3_q_hi")
    k_lo, v_lo, q_lo = sem("s3_k_lo"), sem("s3_v_lo"), sem("s3_q_lo")
    scored, turned, weighed = sem("s3_scored"), sem("s3_turned"), sem("s3_weighed")
    keep_done, beta_done = sem("s3_keep"), sem("s3_beta")
    scanned, weights = sem("s3_scanned"), sem("s3_weights")
    wt_hi_done, wt_lo_done = sem("s3_wt_hi"), sem("s3_wt_lo")
    half_done, row_done, y_done = sem("s3_half"), sem("s3_row"), sem("s3_y")
    proj_done, act_out, silu_done, yp_done = sem("s3_proj"), sem("s3_act_out"), sem("s3_silu"), sem("s3_yp")
    mix_in = sem("s3_mix_in")
    ones, sp_tick, bias_done = sem("s3_ones"), sem("s3_sp_tick"), sem("s3_bias")
    NK, NQ = len(kv_units), len(q_units)

    def event(pair, per, n):
        p, o = pair
        return p * per + (o * per + n + 1)

    def wait(eng, s, value, unit=1):
        if not isinstance(value, int) or value > 0:
            eng.wait_ge(s, value * unit)

    def turns(eng, walk):
        walk(0, range(-NI, 0), False, False, True)
        walk(0, range(NI), False, True, True)
        with eng.Fori(1, PAIRS - 1) as p:
            walk(p, range(NI), True, True, True)
        walk(PAIRS - 1, range(NI), True, True, False)
        walk(PAIRS, range(10), True, False, False)

    def placed(p, s, prev, own, nxt):
        def here(step):
            if s < 0:
                return (p, 0) if step == s else None
            for there, offset in ((own, 0), (prev, -1), (nxt, 1)):
                if there and step == s - offset * NI:
                    return (p, offset)
            return None
        return here

    def operand(here, p, s, prev, own, kind, u, step):
        if (s < 0 or (own and not prev)) and (kind, u) in first_steps:
            if s == first_steps[kind, u]:
                return (p, 0)
            if s < 0 or step >= 0:
                return None
        return here(step)

    def formed(p, s, prev, own, nxt, k, lag, first=fin):
        if own and s == (fin_last if not nxt else fin if prev else first)[k] + lag:
            return (p, 0)
        if prev and s + NI == (fin if own else fin_last)[k] + lag:
            return (p, -1)
        return None

    def bank_s(n):
        return psum[:, 2 + n % 2, :]

    def bank_t(n):
        return psum[:, 4 + n % 2, :]

    def bank_o(row):
        return psum[:, 6 + row % 2, 0:2 * P]

    def last_stores(sp):
        sp.dma_start(gate_d[4 * PAIRS - 1, :, SEQ - CH:SEQ], res[:, 1, :]).then_inc(res_stored[1], DMA)
        sp.dma_start(at_d[PAIRS - 1, HD:P, 0:CH], y_out[HD:P, 1, :]).then_inc(y_stored[1], DMA)

    before_in_all = 4 * (len(WINDOWS) + 2 * PAIRS) // 2 * DMA

    with nc.Block() as block:
        @block.sync
        def _(sp):
            def hold(s, value):
                if not isinstance(value, int) or value > 0:
                    sp.wait_ge(s, value)
                    sp.sem_inc(sp_tick, 1)

            def load_k(pair, u):
                e, c, _before = kv_units[u]
                hold(k_lo, event(pair, NK, u - 2))
                head_loads.load_k(sp, pair, u, e, c)

            def load_v(pair, u):
                e, c, _before = kv_units[u]
                hold(v_lo, event(pair, NK, u - 2))
                head_loads.load_v(sp, pair, u, e, c)

            def load_q(pair, u):
                e, r = q_units[u]
                hold(q_lo, event(pair, NQ, u - 2))
                head_loads.load_q(sp, pair, u, e, r)

            def load_w(pair, j):
                hold(w_lo_done, event(pair, STRIPS, j - 1))
                p, o = pair
                strip = p + (o + (S_ZP, S_ZA)[j]) if j < 2 else p * 4 + (o * 4 + S_G + j - 2)
                sp.dma_start(w_raw[:, :, :], w_strips[strip]).then_inc(w_in, DMA)

            def load_mix(pair, c):
                hold(yp_done, event(pair, NC, c - 1))
                sp.dma_start(mix_t[:, :], mix_d[pair[0] + pair[1], :, c * CH:(c + 1) * CH]).then_inc(mix_in, DMA)

            def store_result(pair, k):
                p, o = pair
                j, c = divmod(k, NC)
                cols = slice(c * CH, (c + 1) * CH)
                if j == 0:
                    hold(yp_done, event(pair, NC, k))
                    dst = yp_d[p + o, :, cols]
                elif j == 1:
                    hold(silu_done, event(pair, 2 * NC, k))
                    dst = za_d[p + o, :, cols]
                else:
                    hold(act_out, event(pair, GROUPS, k))
                    dst = gate_d[p * 4 + (o * 4 + j - 2), :, cols]
                sp.dma_start(dst, res[:, k % 2, :]).then_inc(res_stored[k % 2], DMA)

            def store_y(pair, n):
                e, i = ITEMS[n][0:2]
                u = ROW_OF[n] // 4
                hold(y_done, event(pair, ROWS, ROW_OF[n]))
                sp.dma_start(at_d[pair[0] + pair[1], e * HD:(e + 1) * HD, i * P:i * P + CH],
                             y_out[e * HD:(e + 1) * HD, u % 2, :]).then_inc(y_stored[u % 2], DMA)

            def open_stage4(s):
                pair, tok = (PAIRS - 1, 0), slice(SEQ - CH, SEQ)
                if s == fin[5 * NC - 1] + 2:
                    sp.wait_ge(proj_done, event(pair, GROUPS, 5 * NC - 1))
                    sp.wait_ge(w_lo_done, event(pair, STRIPS, STRIPS - 1))
                    for i in range(2):
                        sp.wait_ge(res_stored[i], event(pair, GROUPS // 2, NC - 1) * DMA)
                    opening.load_y(sp, 0, tok)
                    opening.load_z(sp, 0, tok)
                    opening.load_z(sp, 1, tok)
                    sp.wait_ge(k_lo, event(pair, NK, NK - 1))
                    sp.wait_ge(v_lo, event(pair, NK, NK - 1))
                    for i in range(opening.EARLY):
                        opening.load_piece(sp, i)
                if s == q_step[NQ - 1] + 1:
                    past_first_chunk = last_item(lambda it: it[2] > 0)
                    sp.wait_ge(scored, event(pair, NI, past_first_chunk))
                    sp.wait_ge(q_lo, event(pair, NQ, NQ - 1))
                    sp.wait_ge(y_stored[0], event(pair, 4, 2) * DMA)
                    opening.load_y(sp, 1, tok)

            def walk(p, steps, prev, own, nxt):
                for s in steps:
                    here = placed(p, s, prev, own, nxt)
                    if own and not prev and s == 0:
                        for i in range(2):
                            sp.wait_ge(stored_before[i], before_in_all)
                    if own and not nxt:
                        open_stage4(s)
                    for u in range(NK):
                        if (pair := here(k_step[u] - LOAD)) and not (s < 0 and u < 2):
                            load_k(pair, u)
                        if (pair := here(v_step[u] - LOAD)) and not (s < 0 and u < 2):
                            load_v(pair, u)
                    for u in range(NQ):
                        if (pair := here(q_step[u] - LOAD)) and not (s < 0 and u < 1):
                            load_q(pair, u)
                    for j in range(STRIPS):
                        if pair := here(w_step[j] - LOAD):
                            if not (s < 0 and j < 2):
                                load_w(pair, j)
                    for c in range(NC):
                        if pair := here(fin[c] + 1 - LOAD):
                            load_mix(pair, c)
                    for k in range(GROUPS):
                        if (pair := formed(p, s, prev, own, nxt, k, 2)) and (own or s < 0 or k < GROUPS - 1):
                            store_result(pair, k)
                    for n in ROW_OF:
                        if ITEMS[n][1] % 4 == 0:
                            if (pair := here(n + AV_LAG + 2)) and (own or n < NI - 1):
                                store_y(pair, n)

            sp.sem_inc(w_in, DMA)
            turns(sp, walk)

        @block.tensor
        def _(pe):
            def projections(p, have):
                for j in range(STRIPS):
                    pe.wait_ge(w_lo_done, event((p, 0), STRIPS, j))
                    for c in range(NC):
                        k = j * NC + c
                        if k < have:
                            continue
                        if 2 <= k < 2 * NC + 2:
                            pe.wait_ge(silu_done, event((p, 0), 2 * NC, k - 2))
                        else:
                            wait(pe, act_out, event((p, 0), GROUPS, k - 2))
                        tok = slice(c * CH, (c + 1) * CH)
                        for kt in range(KT):
                            hi, lo = w_hi[:, j % 2, kt, :], w_lo[:, j % 2, kt, :]
                            o = psum[:, k % 2, :]
                            pe.matmul(o, hi, hT_hi[:, kt, tok], start=kt == 0, stop=False)
                            yield
                            pe.matmul(o, hi, hT_lo[:, kt, tok], start=False, stop=False)
                            yield
                            last = pe.matmul(o, lo, hT_hi[:, kt, tok], start=False, stop=kt == KT - 1)
                            if kt == KT - 1:
                                last.then_inc(proj_done, 1)
                            yield

            def score(pair, n):
                e, i, c, w, first, _l = ITEMS[n]
                wait(pe, beta_done, event(pair, NI, n - 2))
                pe.wait_ge(k_lo, event(pair, NK, NC * e + NC - 1 - c))
                u = TT // 2 * (e + 1) - 1 - i // 2
                pe.wait_ge(q_lo, event(pair, NQ, u))
                cols = slice(i % 2 * P, i % 2 * P + P)
                o = bank_s(n)
                keys = slice(c * CH, c * CH + w)
                pe.matmul(o[:, 0:w], qm_hi[:, u % QN, cols], km[:, keys], start=True, stop=False)
                last = pe.matmul(o[:, 0:w], qm_lo[:, u % QN, cols], km[:, keys], start=False, stop=not first)
                if first:
                    last = pe.matmul(o[:, w - P:w], ident_r[:, :], mask_r[:, :], start=False, stop=True)
                last.then_inc(scored, 1)

            def turn(pair, n):
                w = ITEMS[n][3]
                pe.wait_ge(weights, event(pair, NI, n))
                wait(pe, wt_lo_done, event(pair, NI, n - 2))
                for j in range(w // P):
                    a = CH - w + j * P
                    last = pe.transpose(bank_t(n)[:, j * P:(j + 1) * P], beta[:, n % 4, a:a + P], ident[:, :])
                last.then_inc(turned, 1)

            def weigh(pair, n):
                e, i, c, w, first, final = ITEMS[n]
                row = row_at[n]
                pe.wait_ge(wt_lo_done, event(pair, NI, n))
                pe.wait_ge(v_lo, event(pair, NK, NC * e + NC - 1 - c))
                if first:
                    wait(pe, row_done, event(pair, ROWS, row - 2))
                for j in range(w // P):
                    last = pe.matmul(bank_o(row), vm[:, NC * c + j, :],
                                     wt[:, n % 2, j, :, :].rearrange("p a q -> p (a q)"),
                                     start=first and j == 0, stop=final and j == w // P - 1)
                last.then_inc(weighed, 1)

            def walk(p, steps, prev, own, nxt):
                have = 1 if own and not prev else 0
                if own:
                    proj = running[0] = projections(p, have)
                    plan = due_first if have else due if nxt else due_last
                else:
                    proj, plan = running[0], [round((s + 1) / (AV_LAG + 1) * MM) for s in range(AV_LAG + 1)]
                done = have * MM
                if have:
                    pe.sem_inc(proj_done, 1)
                    for done in range(MM + 1, AHEAD + 1):
                        next(proj)
                for s in steps:
                    here = placed(p, s, prev, own, nxt)
                    forming = own or (prev and s <= AV_LAG)
                    half = (plan[s - 1] if s > 0 else 0) + plan[s] if forming else 0
                    for n in range(NI):
                        if pair := here(n):
                            score(pair, n)
                    while forming and 2 * done < half:
                        next(proj)
                        done += 1
                    for n in range(NI):
                        if pair := here(n + T_LAG):
                            turn(pair, n)
                    while forming and done < plan[s]:
                        next(proj)
                        done += 1
                    for n in range(NI):
                        if pair := here(n + AV_LAG):
                            weigh(pair, n)

            running = [None]
            turns(pe, walk)

        @block.scalar
        def _(act):
            def split_k(pair, u):
                _e, c, before = kv_units[u]
                act.wait_ge(k_in[u % 2], event(pair, NK // 2, u // 2) * (2 * DMA))
                wait(act, scored, event(pair, NI, before))
                act.activation(km[:, c * CH:(c + 1) * CH], k_raw[:, u % 2, :], ACT.Copy).then_inc(k_hi, 1)

            def split_v(pair, u):
                _e, c, before = kv_units[u]
                act.wait_ge(v_in[u % 2], event(pair, NK // 2, u // 2) * DMA)
                wait(act, weighed, event(pair, NI, before))
                act.activation(vm[:, 4 * c:4 * c + 4, 0:HD], v_raw[:, u % 2, :, :], ACT.Copy).then_inc(v_hi, 1)

            def split_q(pair, u):
                act.wait_ge(q_in[u % 2], event(pair, NQ // 2, u // 2) * (2 * DMA))
                wait(act, scored, event(pair, NI, q_before[u]))
                act.activation(qm_hi[:, u % QN, :], q_raw[:, u % 2, :], ACT.Copy).then_inc(q_hi, 1)

            def split_w(pair, j):
                act.wait_ge(w_in, event(pair, STRIPS, j) * DMA)
                wait(act, proj_done, event(pair, GROUPS, NC * (j - 2) + NC - 1))
                act.activation(w_hi[:, j % 2, :, :], w_raw[:, :, :], ACT.Copy).then_inc(w_hi_done, 1)

            def sigmoids(pair, n):
                w = ITEMS[n][3]
                act.wait_ge(scored, event(pair, NI, n))
                wait(act, scanned, event(pair, NI, n - 2))
                act.activation(keep[:, n % 2, CH - w:CH], bank_s(n)[:, 0:w], ACT.Sigmoid,
                               scale=-SCALE).then_inc(keep_done, 1)
                wait(act, turned, event(pair, NI, n - 4))
                act.activation(beta[:, n % 4, CH - w:CH], bank_s(n)[:, 0:w], ACT.Sigmoid,
                               scale=SCALE).then_inc(beta_done, 1)

            def high_part(pair, n):
                w = ITEMS[n][3]
                act.wait_ge(turned, event(pair, NI, n))
                wait(act, weighed, event(pair, NI, n - 2))
                act.activation(wt[:, n % 2, 0:w // P, 0, :], bank_t(n)[:, 0:w].rearrange("p (j q) -> p j q", q=P),
                               ACT.Copy).then_inc(wt_hi_done, 1)

            def other_half(pair, n):
                e, row = ITEMS[n][0], ROW_OF[n]
                mine, other = slice(e * HD, e * HD + HD), slice(HD - e * HD, 2 * HD - e * HD)
                act.wait_ge(weighed, event(pair, NI, n))
                wait(act, row_done, event(pair, ROWS, row - 1))
                act.activation(half_sum[mine, :], bank_o(row)[other, :], ACT.Copy).then_inc(half_done, 1)

            def result(pair, k):
                act.wait_ge(proj_done, event(pair, GROUPS, k))
                if k < 2 and isinstance(pair[0], int) and sum(pair) == 0:
                    act.wait_ge(stored_before[k % 2], before_in_all)
                wait(act, res_stored[k % 2], event(pair, GROUPS // 2, k // 2 - 1), DMA)
                if k < 2 * NC:
                    act.activation(res[:, k % 2, :], psum[:, k % 2, :], ACT.Sigmoid).then_inc(act_out, 1)
                else:
                    b = k // NC - 2
                    act.wait_ge(bias_done, event(pair, 1, 0))
                    act.activation(res[:, k % 2, :], psum[:, k % 2, :], ACT.Sigmoid,
                                   bias=bias[:, b:b + 1]).then_inc(act_out, 1)

            def fetch_bias(pair):
                wait(act, act_out, event(pair, GROUPS, -1))
                act.sem_inc(bias_tick, 1)
                act.activation(bias[:, :], bcol[:, bass.ds(pair[0] * 4 + pair[1] * 4, 4)],
                               ACT.Copy).then_inc(bias_done, 1)

            def walk(p, steps, prev, own, nxt):
                for s in steps:
                    here = placed(p, s, prev, own, nxt)
                    for n in range(NI):
                        if pair := here(n):
                            sigmoids(pair, n)
                    for u in range(NK):
                        if pair := operand(here, p, s, prev, own, "k", u, k_step[u]):
                            split_k(pair, u)
                        if pair := operand(here, p, s, prev, own, "v", u, v_step[u]):
                            split_v(pair, u)
                    for u in range(NQ):
                        if pair := operand(here, p, s, prev, own, "q", u, q_step[u]):
                            split_q(pair, u)
                    for j in range(STRIPS):
                        if pair := operand(here, p, s, prev, own, "w", j, w_step[j]):
                            if not (s < 0 and j == 0):
                                split_w(pair, j)
                    if pair := here(BIAS_STEP):
                        fetch_bias(pair)
                    for n in range(NI):
                        if pair := here(n + T_LAG):
                            high_part(pair, n)
                    for n in ROW_OF:
                        if pair := here(n + AV_LAG + 1):
                            other_half(pair, n)
                    for k in range(GROUPS):
                        if pair := formed(p, s, prev, own, nxt, k, 1, fin_first):
                            result(pair, k)

            bias_tick = sem("s3_bias_tick")
            act.sem_inc(w_hi_done, 1)
            turns(act, walk)

        @block.vector
        def _(dve):
            def scan(pair, n):
                w, first = ITEMS[n][3:5]
                span = slice(CH - w, CH + 1)
                if first:
                    carry = 1.0
                else:
                    dve.wait_ge(scanned, event(pair, NI, n - 1))
                    a = CH - ITEMS[n - 1][3]
                    carry = left[:, (n - 1) % 2, a:a + 1]
                dve.wait_ge(keep_done, event(pair, NI, n))
                k = keep[:, n % 2, span][:, ::-1]
                dve.tensor_tensor_scan(left[:, n % 2, span][:, ::-1], k, k, carry,
                                       ALU.mult, ALU.bypass).then_inc(scanned, 1)

            def weight(pair, n):
                w = ITEMS[n][3]
                dve.wait_ge(beta_done, event(pair, NI, n))
                dve.wait_ge(scanned, event(pair, NI, n))
                dve.tensor_tensor(beta[:, n % 4, CH - w:CH], beta[:, n % 4, CH - w:CH],
                                  left[:, n % 2, CH - w + 1:CH + 1], ALU.mult).then_inc(weights, 1)

            def low_part(pair, n):
                w = ITEMS[n][3]
                dve.wait_ge(wt_hi_done, event(pair, NI, n))
                dve.tensor_tensor(wt[:, n % 2, 0:w // P, 1, :],
                                  bank_t(n)[:, 0:w].rearrange("p (j q) -> p j q", q=P),
                                  wt[:, n % 2, 0:w // P, 0, :].bitcast(F32), ALU.subtract).then_inc(wt_lo_done, 1)

            def add_halves(pair, n):
                e, row = ITEMS[n][0], ROW_OF[n]
                mine = slice(e * HD, e * HD + HD)
                dve.wait_ge(half_done, event(pair, ROWS, row))
                wait(dve, y_done, event(pair, ROWS, row - 1))
                dve.tensor_tensor(row_sum[mine, :], bank_o(row)[mine, :], half_sum[mine, :],
                                  ALU.add).then_inc(row_done, 1)

            def silu(pair, k):
                dve.wait_ge(act_out, event(pair, GROUPS, k))
                dve.tensor_tensor(res[:, k % 2, :], psum[:, k % 2, :], res[:, k % 2, :],
                                  ALU.mult).then_inc(silu_done, 1)

            def walk(p, steps, prev, own, nxt):
                for s in steps:
                    here = placed(p, s, prev, own, nxt)
                    for n in range(NI):
                        if pair := here(n + T_LAG + 1):
                            low_part(pair, n)
                    for n in range(NI):
                        if pair := here(n):
                            scan(pair, n)
                    for n in range(NI):
                        if pair := here(n):
                            weight(pair, n)
                    for n in ROW_OF:
                        if pair := here(n + AV_LAG + 1):
                            add_halves(pair, n)
                    for k in range(2 * NC):
                        if pair := formed(p, s, prev, own, nxt, k, 1, fin_first):
                            silu(pair, k)

            dve.wait_ge(ones, 2)
            turns(dve, walk)

        @block.gpsimd
        def _(pool):
            before = []

            def step(out_, a, b, op, s, value):
                if before:
                    pool.wait_ge(*before)
                pool.tensor_tensor(out_, a, b, op).then_inc(s, 1)
                before[:] = [s, value]

            def low_k(pair, u):
                c = kv_units[u][1]
                pool.wait_ge(k_hi, event(pair, NK, u))
                low = km[HD:P, c * CH:(c + 1) * CH]
                step(low, k_raw[HD:P, u % 2, :], low.bitcast(F32), ALU.subtract, k_lo, event(pair, NK, u))

            def low_v(pair, u):
                c = kv_units[u][1]
                pool.wait_ge(v_hi, event(pair, NK, u))
                step(vm[:, 4 * c:4 * c + 4, HD:2 * HD], v_raw[:, u % 2, :, :],
                     vm[:, 4 * c:4 * c + 4, 0:HD].bitcast(F32), ALU.subtract, v_lo, event(pair, NK, u))

            def low_q(pair, u):
                pool.wait_ge(q_hi, event(pair, NQ, u))
                step(qm_lo[:, u % QN, :], q_raw[:, u % 2, :], qm_hi[:, u % QN, :].bitcast(F32),
                     ALU.subtract, q_lo, event(pair, NQ, u))

            def low_w(pair, j):
                pool.wait_ge(w_hi_done, event(pair, STRIPS, j))
                step(w_lo[:, j % 2, :, :], w_raw[:, :, :], w_hi[:, j % 2, :, :].bitcast(F32),
                     ALU.subtract, w_lo_done, event(pair, STRIPS, j))

            def finish_row(pair, n):
                e, i, row = ITEMS[n][0], ITEMS[n][1], ROW_OF[n]
                mine = slice(e * HD, e * HD + HD)
                u = row // 4
                pool.wait_ge(row_done, event(pair, ROWS, row))
                if i % 4 == 3:
                    wait(pool, y_stored[u % 2], event(pair, 4, u // 2 - 1), DMA)
                step(y_out[mine, u % 2, i % 4 * P:i % 4 * P + P], row_sum[mine, 0:P],
                     row_sum[mine, P:2 * P], ALU.add, y_done, event(pair, ROWS, row))

            def times_mix(pair, c):
                pool.wait_ge(silu_done, event(pair, 2 * NC, c))
                pool.wait_ge(mix_in, event(pair, NC, c) * DMA)
                step(res[:, c % 2, :], res[:, c % 2, :], mix_t[:, :], ALU.mult, yp_done, event(pair, NC, c))

            def walk(p, steps, prev, own, nxt):
                before.clear()
                for s in steps:
                    here = placed(p, s, prev, own, nxt)
                    for u in range(NK):
                        if pair := operand(here, p, s, prev, own, "k", u, k_step[u]):
                            low_k(pair, u)
                        if pair := operand(here, p, s, prev, own, "v", u, v_step[u]):
                            low_v(pair, u)
                    for u in range(NQ):
                        if pair := operand(here, p, s, prev, own, "q", u, q_step[u]):
                            low_q(pair, u)
                    for n in ROW_OF:
                        if pair := here(n + AV_LAG + 1):
                            finish_row(pair, n)
                    for c in range(NC):
                        if pair := here(fin[c] + 1):
                            times_mix(pair, c)
                    for j in range(STRIPS):
                        if pair := operand(here, p, s, prev, own, "w", j, w_step[j]):
                            if not (s < 0 and j == 0):
                                low_w(pair, j)
                if before:
                    pool.wait_ge(*before)

            for i in range(2):
                pool.memset(keep[:, i, CH:CH + 1], 1.0).then_inc(ones, 1)
            pool.wait_ge(ones, 2)
            pool.sem_inc(w_lo_done, 1)
            turns(pool, walk)

    return last_stores


def stage4(nc, sem, psum, sb, sb_y, sb_end, x, gate_d, final_g, out, res_stored, y_stored, opening,
           ident_r, last_stores):
    UK = AW // P
    up_hi = [sb(f"up_hi{b}", [P, UK, D], F32R) for b in range(2)]
    up_lo = [sb(f"up_lo{b}", [P, UK, D], F32R) for b in range(2)]
    wo_hi = sb("wo_hi", [P, KT, D], F32R)
    wo_lo = sb("wo_lo", [P, KT, D], F32R)
    y_hi = [at(f"y_hi{b}", [P, UK, CH], F32R) for b, at in enumerate((sb_y, sb_end))]
    y_lo, z_raw, row, raw = opening.y_lo, opening.z_raw, opening.row, opening.raw
    gate = sb_end("gate", [P, 4, CH])
    m_hi = sb_end("m_hi", [P, KT, CH], F32R)
    m_lo = sb_end("m_lo", [P, KT, CH], F32R)
    fg = sb_end("fg", [P, D])
    st = sb_end("st4", [P, 2, 8])

    UP, SLOTS, EARLY = 2 * KT, opening.SLOTS, opening.EARLY
    arrival = opening.arrival
    n_raw = len(arrival)
    up_ready = [arrival.index(2 * m + 1) + 1 for m in range(KT)]
    by = [up_ready[min(m + 2, KT - 1)] for m in range(KT - 2)] + [n_raw - 2, n_raw]
    fg_in = sem("s4_fg_in")
    raw_in, y_in, z_in = opening.raw_in, opening.y_in, opening.z_in
    raw_hi, raw_lo = sem("s4_raw_hi"), sem("s4_raw_lo")
    z_done = sem("s4_z_done")
    y_hi_done = [sem(f"s4_y_hi{b}") for b in range(2)]
    y_lo_done = [sem(f"s4_y_lo{b}") for b in range(2)]
    g_in = [sem(f"s4_g_in{i}") for i in range(2)]
    up_done = [sem(f"s4_up_done{b}") for b in range(2)]
    gated, summed = sem("s4_gated"), sem("s4_summed")
    m_hi_done, m_lo_done = sem("s4_m_hi"), sem("s4_m_lo")
    out_done, added = sem("s4_out_done"), sem("s4_added")
    x_in = [sem(f"s4_x_in{i}") for i in range(2)]
    squared, mean, rooted, newton, scaled = (sem(f"s4_{n}") for n in ("squared", "mean", "rooted", "newton", "scaled"))
    finished = sem("s4_finished")
    stored = [sem(f"s4_stored{i}") for i in range(2)]
    NM, NT = KT, CH // P

    def event(c, per, n):
        assert n >= -per
        return c * per + (per + n + 1)

    def tokens(c, t=0, n=CH):
        return bass.ds(c * -CH + ((NC - 1) * CH + t * P), n)

    def piece(i):
        n, slot = arrival[i], raw[:, i % SLOTS, :]
        if n < UP:
            m, b = divmod(n, 2)
            cols = slice(m * P, (m + 1) * P)
            return up_hi[b][:, :, cols], up_lo[b][:, :, cols], slot.rearrange("p (k n) -> p k n", n=P)
        k, h = divmod(n - UP, 2)
        half = slice(h * CH, (h + 1) * CH)
        return wo_hi[:, k, half], wo_lo[:, k, half], slot

    with nc.Block() as block:
        @block.sync
        def _(sp):
            def load_weights(a, b):
                for i in range(a, b):
                    if i >= SLOTS:
                        sp.wait_ge(raw_lo, i - SLOTS + 1)
                    opening.load_piece(sp, i)

            def load_y(c, b):
                sp.wait_ge(up_done[b], event(c, NM, -1))
                opening.load_y(sp, b, tokens(c))

            def load_z(c, k):
                sp.wait_ge(y_lo_done[1], event(c, UK, k - 2))
                opening.load_z(sp, k, tokens(c))

            def load_gates(c, m):
                sp.wait_ge(m_lo_done, event(c, NM, m - 2))
                for b in range(2):
                    sp.dma_start(gate[:, m % 2 * 2 + b, :], gate_d[b * KT + m, :, tokens(c)]).then_inc(g_in[m % 2], DMA)

            def load_x(c, t):
                sp.wait_ge(stored[t % 2], c * (2 * DMA) + (2 + t // 2) * DMA)
                sp.dma_start(row[:, t % 2, :], x[tokens(c, t, P), :]).then_inc(x_in[t % 2], DMA)

            def store(c, t):
                sp.wait_ge(finished, event(c, NT, t))
                sp.dma_start(out[tokens(c, t, P), :], row[:, t % 2, :]).then_inc(stored[t % 2], DMA)

            def finish(c, following):
                if following:
                    load_y(c + 1, 0)
                    load_y(c + 1, 1)
                    load_z(c + 1, 0)
                    load_z(c + 1, 1)
                load_x(c, 0)
                load_x(c, 1)
                store(c, 0)
                load_x(c, 2)
                if following:
                    load_z(c + 1, 2)
                store(c, 1)
                load_x(c, 3)
                if following:
                    load_z(c + 1, 3)
                    load_gates(c + 1, 0)
                    load_gates(c + 1, 1)
                store(c, 2)
                store(c, 3)

            for s, n in ((y_in[0], 1), (y_in[1], 1), (z_in[0], UK // 2), (z_in[1], UK // 2), (g_in[0], NM), (g_in[1], NM),
                         (x_in[0], 2), (x_in[1], 2), (stored[0], 2), (stored[1], 2)):
                sp.sem_inc(s, n * DMA)
            last_stores(sp)
            load_weights(EARLY, 4)
            load_z(0, 2)
            load_z(0, 3)
            for i in range(2):
                sp.wait_ge(res_stored[i], PAIRS * 6 * NC // 2 * DMA)
                sp.wait_ge(y_stored[i], PAIRS * 4 * DMA)
            load_gates(0, 0)
            load_weights(4, 6)
            load_gates(0, 1)
            load_weights(6, by[0])
            sp.dma_start(fg[:, :], final_g.partition_broadcast(P)).then_inc(fg_in, DMA)
            for m in range(NM):
                if m >= 2:
                    load_gates(0, m)
                load_weights(by[m], by[min(m + 1, NM - 1)])
            sp.wait_ge(raw_lo, n_raw)
            finish(0, True)
            with sp.Fori(1, NC - 1) as c:
                for m in range(2, NM):
                    load_gates(c, m)
                finish(c, True)
            for m in range(2, NM):
                load_gates(NC - 1, m)
            finish(NC - 1, False)
            for s in stored:
                sp.wait_ge(s, (NC + 1) * 2 * DMA)

        @block.tensor
        def _(pe):
            for s, n in ((up_done[0], NM), (up_done[1], NM), (out_done, 2 * NT)):
                pe.sem_inc(s, n)
            keep_warm(pe, psum[:, 7, :], ident_r, 8)

            def up(c, m, b):
                pe.wait_ge(raw_lo, arrival.index(2 * m + b) + 1)
                pe.wait_ge(gated, event(c, 2 * NM, 2 * m + b - 4))
                for k in range(UK):
                    if m == 0:
                        pe.wait_ge(y_lo_done[b], event(c, UK, k))
                    cols = slice(m * P, (m + 1) * P)
                    last = split3(pe, psum[:, m % 2 * 2 + b, :], up_hi[b][:, k, cols], up_lo[b][:, k, cols],
                                  y_hi[b][:, k, :], y_lo[b][:, k, :], k == 0, k == UK - 1)
                last.then_inc(up_done[b], 1)

            def project(c, t, h, ks):
                n = 2 * t + h
                cols, tok = slice(h * CH, (h + 1) * CH), slice(t * P, (t + 1) * P)
                for k in ks:
                    if t == 0:
                        pe.wait_ge(raw_lo, arrival.index(UP + 2 * k + h) + 1)
                        pe.wait_ge(m_lo_done, event(c, NM, k))
                    if k == 0:
                        pe.wait_ge(squared, event(c, NT, t - 2))
                    last = split3(pe, psum[:, 4 + n % 4, :], m_hi[:, k, tok], m_lo[:, k, tok],
                                  wo_hi[:, k, cols], wo_lo[:, k, cols], k == 0, k == KT - 1)
                if KT - 1 in ks:
                    last.then_inc(out_done, 1)

            with pe.Fori(0, NC) as c:
                for m, b in [(0, 0), (1, 0), (0, 1), (1, 1)] + [(m, b) for m in range(2, NM) for b in range(2)]:
                    up(c, m, b)
                for h in range(2):
                    project(c, 0, h, range(KT - 1))
                for h in range(2):
                    project(c, 0, h, range(KT - 1, KT))
                for t in range(1, NT):
                    for h in range(2):
                        project(c, t, h, range(KT))

        @block.scalar
        def _(act):
            for s, n in ((y_hi_done[0], UK), (y_hi_done[1], UK), (m_hi_done, NM), (squared, NT), (rooted, NT)):
                act.sem_inc(s, n)

            def split_weights(a, b):
                for i in range(a, b):
                    act.wait_ge(raw_in[i % SLOTS], DMA * (i // SLOTS + 1))
                    hi, _lo, slot = piece(i)
                    act.activation(hi, slot, ACT.Copy).then_inc(raw_hi, 1)

            def split_y0(c):
                act.wait_ge(y_in[0], event(c, 1, 0) * DMA)
                for k in range(UK):
                    act.activation(y_hi[0][:, k, :], y_lo[0][:, k, :].bitcast(F32), ACT.Copy).then_inc(y_hi_done[0], 1)

            def split_y1(c, *tiles):
                for k in tiles:
                    act.wait_ge(z_done, event(c, UK, k))
                    act.activation(y_hi[1][:, k, :], z_raw[:, k % 2, :], ACT.Copy).then_inc(y_hi_done[1], 1)

            def merge(c, m):
                act.wait_ge(summed, event(c, NM, m))
                act.wait_ge(out_done, event(c, 2 * NT, -1))
                act.activation(m_hi[:, m, :], gate[:, m % 2 * 2, :], ACT.Copy).then_inc(m_hi_done, 1)

            def square(c, t):
                act.wait_ge(added, event(c, 2 * NT, 2 * t + 1))
                act.activation(psum[:, 4 + 2 * t % 4:6 + 2 * t % 4, :],
                               row[:, t % 2, :].rearrange("p (a b) -> p a b", a=2), ACT.Square,
                               accum_out=st[:, t % 2, 0:1]).then_inc(squared, 1)

            def root(c, t):
                act.wait_ge(mean, event(c, 2 * NT, 2 * t + 1))
                act.activation(st[:, t % 2, 3:4], st[:, t % 2, 2:3], ACT.Sqrt).then_inc(rooted, 1)

            def finish(c, following):
                for t in range(NT):
                    if following and t == 0:
                        split_y0(c + 1)
                    if following and 1 <= t <= 2:
                        split_y1(c + 1, 2 * t - 2, 2 * t - 1)
                    square(c, t)
                    root(c, t)

            split_weights(0, 1)
            split_y0(0)
            split_y1(0, 0)
            split_weights(1, 2)
            split_y1(0, 1)
            split_weights(2, 4)
            split_y1(0, 2, 3)
            split_weights(4, by[0])
            for m in range(NM):
                split_weights(by[m], by[min(m + 1, NM - 1)])
                merge(0, m)
            finish(0, True)
            with act.Fori(1, NC - 1) as c:
                for m in range(NM):
                    merge(c, m)
                finish(c, True)
            for m in range(NM):
                merge(NC - 1, m)
            finish(NC - 1, False)

        @block.vector
        def _(dve):
            for s, n in ((y_lo_done[0], UK), (y_lo_done[1], UK), (gated, 2 * NM),
                         (added, 2 * NT), (mean, 2 * NT), (newton, 2 * NT), (scaled, NT), (finished, NT)):
                dve.sem_inc(s, n)

            def weights_lo(a, b):
                for i in range(a, b):
                    dve.wait_ge(raw_hi, i + 1)
                    hi, lo, slot = piece(i)
                    dve.tensor_tensor(lo, slot, hi.bitcast(F32), ALU.subtract).then_inc(raw_lo, 1)

            def y0_low(c):
                for k in range(UK):
                    dve.wait_ge(y_hi_done[0], event(c, UK, k))
                    dve.tensor_tensor(y_lo[0][:, k, :], y_lo[0][:, k, :].bitcast(F32),
                                      y_hi[0][:, k, :].bitcast(F32), ALU.subtract).then_inc(y_lo_done[0], 1)

            def y1_low(c, *tiles):
                for k in tiles:
                    dve.wait_ge(y_hi_done[1], event(c, UK, k))
                    dve.tensor_tensor(y_lo[1][:, k, :], z_raw[:, k % 2, :], y_hi[1][:, k, :].bitcast(F32),
                                      ALU.subtract).then_inc(y_lo_done[1], 1)

            def apply_gates(c, m):
                for b in range(2):
                    g = gate[:, m % 2 * 2 + b, :]
                    dve.wait_ge(g_in[m % 2], c * (NM * DMA) + (NM + m // 2 * 2 + 2) * DMA)
                    dve.wait_ge(up_done[b], event(c, NM, m))
                    dve.tensor_tensor(g, psum[:, m % 2 * 2 + b, :], g, ALU.mult).then_inc(gated, 1)

            def finish_rows(c, t):
                s = st[:, t % 2, :]
                for h in range(2):
                    r = row[:, t % 2, h * CH:(h + 1) * CH]
                    n = 2 * t + h
                    dve.wait_ge(out_done, event(c, 2 * NT, n))
                    if h == 0:
                        dve.wait_ge(x_in[t % 2], c * (2 * DMA) + (2 + t // 2 + 1) * DMA)
                    dve.tensor_tensor(r, psum[:, 4 + n % 4, :], r, ALU.add).then_inc(added, 1)
                dve.wait_ge(squared, event(c, NT, t))
                dve.tensor_scalar(s[:, 1:2], s[:, 0:1], 1.0 / D, EPS, ALU.mult, ALU.add).then_inc(mean, 1)
                dve.wait_ge(mean, event(c, 2 * NT, 2 * t))
                dve.reciprocal(s[:, 2:3], s[:, 1:2]).then_inc(mean, 1)
                dve.wait_ge(rooted, event(c, NT, t))
                dve.tensor_scalar(s[:, 4:5], s[:, 3:4], s[:, 3:4], s[:, 1:2], ALU.mult,
                                  ALU.mult).then_inc(newton, 1)
                dve.wait_ge(newton, event(c, 2 * NT, 2 * t))
                dve.tensor_scalar(s[:, 5:6], s[:, 4:5], -0.5, 1.5, ALU.mult, ALU.add).then_inc(newton, 1)
                dve.wait_ge(newton, event(c, 2 * NT, 2 * t + 1))
                dve.tensor_tensor(s[:, 6:7], s[:, 3:4], s[:, 5:6], ALU.mult).then_inc(scaled, 1)
                dve.wait_ge(scaled, event(c, NT, t))
                r = row[:, t % 2, :]
                dve.scalar_tensor_tensor(r, r, s[:, 6:7], fg[:, :], ALU.mult, ALU.mult).then_inc(finished, 1)

            def finish(c, following):
                for t in range(NT):
                    if following and t == 0:
                        y0_low(c + 1)
                    if following and 1 <= t <= 2:
                        y1_low(c + 1, 2 * t - 2, 2 * t - 1)
                    finish_rows(c, t)

            weights_lo(0, 1)
            y0_low(0)
            y1_low(0, 0)
            weights_lo(1, 2)
            y1_low(0, 1)
            weights_lo(2, 4)
            y1_low(0, 2, 3)
            weights_lo(4, by[0])
            for m in range(NM):
                if m >= 1:
                    weights_lo(by[m - 1], by[m])
                apply_gates(0, m)
            dve.wait_ge(fg_in, DMA)
            finish(0, True)
            with dve.Fori(1, NC - 1) as c:
                for m in range(NM):
                    apply_gates(c, m)
                finish(c, True)
            for m in range(NM):
                apply_gates(NC - 1, m)
            finish(NC - 1, False)

        @block.gpsimd
        def _(pool):
            for s, n in ((z_done, UK), (summed, NM), (m_lo_done, NM)):
                pool.sem_inc(s, n)

            def gate_attention(c, k):
                pool.wait_ge(y_in[1], event(c, 1, 0) * DMA)
                pool.wait_ge(z_in[k % 2], event(c, UK // 2, k // 2) * DMA)
                z = z_raw[:, k % 2, :]
                pool.tensor_tensor(z, y_lo[1][:, k, :].bitcast(F32), z, ALU.mult).then_inc(z_done, 1)

            def merge(c, m):
                g = m % 2 * 2
                pool.wait_ge(gated, event(c, 2 * NM, 2 * m + 1))
                pool.tensor_tensor(gate[:, g, :], gate[:, g, :], gate[:, g + 1, :], ALU.add).then_inc(summed, 1)
                pool.wait_ge(m_hi_done, event(c, NM, m))
                pool.tensor_tensor(m_lo[:, m, :], gate[:, g, :], m_hi[:, m, :].bitcast(F32),
                                   ALU.subtract).then_inc(m_lo_done, 1)

            with pool.Fori(0, NC) as c:
                for k in range(UK):
                    gate_attention(c, k)
                for m in range(NM):
                    merge(c, m)


def kernel(x, norm_g, w_in, b_gate, pool_w, pool_scale, w_pool_up, w_attn_up, w_out, final_g):
    import numpy as np
    import concourse.bacc as bacc
    from concourse.bass_utils import run_bass_kernel_spmd

    def columns(a):
        return np.ascontiguousarray(np.asarray(a).reshape(-1, P).T)

    def by_k(a):
        a = np.asarray(a)
        return np.ascontiguousarray(a.reshape(-1, P, a.shape[-1]).transpose(1, 0, 2))

    w = np.asarray(w_in)[0]
    v_cols = slice(S_ZA * P - AW, S_ZA * P)
    counts = np.minimum(np.arange(PAD)[None, :] + 1, np.array(WINDOWS)[:, None])
    fix = np.broadcast_to((np.array(WINDOWS)[:, None] / counts).astype(np.float32), (P, len(WINDOWS), PAD))
    arrays = {
        "x": np.ascontiguousarray(np.asarray(x)[0]),
        "x_T": np.ascontiguousarray(np.asarray(x)[0].reshape(TT, P, KT, P).transpose(0, 3, 2, 1)),
        "norm_gT": columns(np.asarray(norm_g)[0]),
        "w_strips": np.ascontiguousarray(w.reshape(KT, P, -1, P).transpose(2, 1, 0, 3)),
        "w_v": by_k(w[:, v_cols]),
        "b_gateT": columns(np.asarray(b_gate)[0]),
        "pool_w": np.ascontiguousarray(np.asarray(pool_w)[0]),
        "pool_scaleT": columns(np.asarray(pool_scale)[0]),
        "w_pool_up": by_k(np.asarray(w_pool_up)[0]),
        "w_attn_up": by_k(np.asarray(w_attn_up)[0]),
        "w_out": by_k(np.asarray(w_out)[0]),
        "final_g": np.ascontiguousarray(np.asarray(final_g)),
        "pool_fix": np.ascontiguousarray(fix),
    }
    nc = bacc.Bacc("TRN2", target_bir_lowering=False, num_devices=1, dynamic_dma_scratch_size=1024)
    args = {n: nc.dram_tensor("in_" + n, a.shape, mybir.dt.from_np(a.dtype), kind="ExternalInput").ap()
            for n, a in arrays.items()}
    out = nc.dram_tensor("out_0", (SEQ, D), F32, kind="ExternalOutput").ap()
    build(nc, **args, out=out)
    r = run_bass_kernel_spmd(nc, [{"in_" + n: a for n, a in arrays.items()}], core_ids=[0])
    return r.results[0]["out_0"].reshape(1, SEQ, D)
```
